# Optimizing a Trainium2 kernel written in Bass

```python
import jax, jax.numpy as jnp
from jax import lax
import numpy as np
import math

D_MODEL = 1024
BATCH = 1
SEQ = 256
DEPTH = 1

MIX_WIDTH = D_MODEL
RWKV_WIDTH = MIX_WIDTH // 2
POOL_WIDTH = MIX_WIDTH - RWKV_WIDTH
HEAD_SIZE = 64
N_HEADS = RWKV_WIDTH // HEAD_SIZE
D_DECAY_LORA = max(32, int(round(1.8 * RWKV_WIDTH ** 0.5 / 32)) * 32)
D_AAA_LORA = max(32, int(round(1.8 * RWKV_WIDTH ** 0.5 / 32)) * 32)
D_GATE_LORA = max(32, int(round(0.6 * RWKV_WIDTH ** 0.8 / 32)) * 32)
POOL_WINDOWS = (2, 4, 8, 16)
N_POOL_GROUPS = len(POOL_WINDOWS)
POOL_GROUP = POOL_WIDTH // N_POOL_GROUPS
D_FF = 256 * ((8 * D_MODEL // 3 + 255) // 256)
SPLIT_SIZES = (RWKV_WIDTH, RWKV_WIDTH, RWKV_WIDTH, D_DECAY_LORA, D_AAA_LORA, D_GATE_LORA, POOL_WIDTH)
RWKV_COLS = sum(SPLIT_SIZES[:6])
IN_COLS = sum(SPLIT_SIZES)
RMS_EPS = 1e-6
GN_EPS = 64e-5
L2_EPS = 1e-12


def rms_norm(x, g):
    xf = x.astype(jnp.float32)
    y = xf * lax.rsqrt(jnp.mean(xf * xf, axis=-1, keepdims=True) + RMS_EPS)
    return (y * g).astype(x.dtype)

def swiglu(x, w_gate, w_up, w_down):
    return (jax.nn.silu(x @ w_gate) * (x @ w_up)) @ w_down

def token_shift(p):
    return jnp.pad(p, ((0, 0), (1, 0), (0, 0)))[:, :-1]

def rwkv7_time_mix(p_r, p_k, p_v, p_w, p_a, p_g, w0, w_lora_up, a0, a_lora_up, g_lora_up,
                   k_k, k_a, r_k, ln_w, ln_b):
    B, S, _ = p_r.shape
    f32 = jnp.float32
    log_w = -jax.nn.softplus(-(w0 + jnp.tanh(p_w) @ w_lora_up).astype(f32)) - 0.5
    decay = jnp.exp(-jnp.exp(log_w))
    a = jax.nn.sigmoid((a0 + p_a @ a_lora_up).astype(f32))
    g = jax.nn.sigmoid(p_g) @ g_lora_up

    def heads(t):
        return t.reshape(B, S, N_HEADS, HEAD_SIZE).astype(f32)

    kk = heads(p_k * k_k)
    kk = kk / jnp.maximum(jnp.sqrt(jnp.sum(kk * kk, axis=-1, keepdims=True)), L2_EPS)
    k = heads(p_k * (1.0 + (a - 1.0) * k_a))
    r, v = heads(p_r), heads(p_v)
    w_h, a_h = heads(decay), heads(a)

    def step(state, inp):
        r_t, w_t, k_t, v_t, kk_t, a_t = inp
        sa = jnp.einsum('bhvk,bhk->bhv', state, -kk_t)
        state = (state * w_t[:, :, None, :]
                 + sa[..., None] * (kk_t * a_t)[:, :, None, :]
                 + v_t[..., None] * k_t[:, :, None, :])
        return state, jnp.einsum('bhvk,bhk->bhv', state, r_t)

    seq_major = lambda t: jnp.moveaxis(t, 1, 0)
    state0 = jnp.zeros((B, N_HEADS, HEAD_SIZE, HEAD_SIZE), f32)
    _, y = lax.scan(step, state0, (seq_major(r), seq_major(w_h), seq_major(k),
                                   seq_major(v), seq_major(kk), seq_major(a_h)))
    y = jnp.moveaxis(y, 0, 1)
    mean = jnp.mean(y, axis=-1, keepdims=True)
    var = jnp.mean(jnp.square(y - mean), axis=-1, keepdims=True)
    y = ((y - mean) * lax.rsqrt(var + GN_EPS)).reshape(B, S, RWKV_WIDTH) * ln_w + ln_b
    bonus = jnp.sum(r * k * r_k, axis=-1, keepdims=True) * v
    y = y + bonus.reshape(B, S, RWKV_WIDTH)
    return (y * g).astype(p_r.dtype)

def multiscale_pool_mix(p, w_pool, pool_scale):
    B, S, _ = p.shape
    f32 = jnp.float32
    pg = p.reshape(B, S, N_POOL_GROUPS, POOL_GROUP).astype(f32)
    cs = jnp.pad(jnp.cumsum(pg, axis=1), ((0, 0), (1, 0), (0, 0), (0, 0)))
    t1 = jnp.arange(1, S + 1)
    outs = []
    for gi, win in enumerate(POOL_WINDOWS):
        csg = cs[:, :, gi]
        lo = jnp.maximum(t1 - win, 0)
        window_sum = csg[:, 1:] - jnp.take(csg, lo, axis=1)
        count = jnp.minimum(t1, win).astype(f32)[None, :, None]
        outs.append(window_sum / count - pg[:, :, gi])
    pooled = jnp.stack(outs, axis=2)
    mixed = jnp.einsum('bsgc,gcd->bsgd', pooled, w_pool.astype(f32))
    return (mixed.reshape(B, S, POOL_WIDTH) * pool_scale).astype(p.dtype)

def first_inputs(seed: int = 0) -> dict:
    key = jax.random.key(seed)
    ks = jax.random.split(key, 32)
    L = DEPTH
    f32 = jnp.float32

    def nrm(k, shape, scale):
        return jax.random.normal(k, shape, f32) * scale

    return {
        "x": nrm(ks[0], (BATCH, SEQ, D_MODEL), 1.0),
        "ffn1_norm": 1.0 + nrm(ks[1], (L, D_MODEL), 0.1),
        "ffn1_w_gate": nrm(ks[2], (L, D_MODEL, D_FF), D_MODEL ** -0.5),
        "ffn1_w_up": nrm(ks[3], (L, D_MODEL, D_FF), D_MODEL ** -0.5),
        "ffn1_w_down": nrm(ks[4], (L, D_FF, D_MODEL), D_FF ** -0.5),
        "mix_norm": 1.0 + nrm(ks[5], (L, D_MODEL), 0.1),
        "w_in": nrm(ks[6], (L, D_MODEL, IN_COLS), D_MODEL ** -0.5),
        "mu_shift": jax.random.uniform(ks[7], (L, RWKV_COLS), f32),
        "w0": jax.random.uniform(ks[8], (L, RWKV_WIDTH), f32, -6.0, -1.0),
        "w_lora_up": nrm(ks[9], (L, D_DECAY_LORA, RWKV_WIDTH), 0.5 * D_DECAY_LORA ** -0.5),
        "a0": nrm(ks[10], (L, RWKV_WIDTH), 0.1),
        "a_lora_up": nrm(ks[11], (L, D_AAA_LORA, RWKV_WIDTH), D_AAA_LORA ** -0.5),
        "g_lora_up": nrm(ks[12], (L, D_GATE_LORA, RWKV_WIDTH), D_GATE_LORA ** -0.5),
        "k_k": 0.85 + nrm(ks[13], (L, RWKV_WIDTH), 0.1),
        "k_a": 1.0 + nrm(ks[14], (L, RWKV_WIDTH), 0.1),
        "r_k": nrm(ks[15], (L, N_HEADS, HEAD_SIZE), 0.1),
        "ln_w": 1.0 + nrm(ks[16], (L, RWKV_WIDTH), 0.1),
        "ln_b": nrm(ks[17], (L, RWKV_WIDTH), 0.02),
        "w_pool": nrm(ks[18], (L, N_POOL_GROUPS, POOL_GROUP, POOL_GROUP), POOL_GROUP ** -0.5),
        "pool_scale": 1.0 + nrm(ks[19], (L, POOL_WIDTH), 0.1),
        "w_out": nrm(ks[20], (L, MIX_WIDTH, D_MODEL), MIX_WIDTH ** -0.5),
        "ffn2_norm": 1.0 + nrm(ks[21], (L, D_MODEL), 0.1),
        "ffn2_w_gate": nrm(ks[22], (L, D_MODEL, D_FF), D_MODEL ** -0.5),
        "ffn2_w_up": nrm(ks[23], (L, D_MODEL, D_FF), D_MODEL ** -0.5),
        "ffn2_w_down": nrm(ks[24], (L, D_FF, D_MODEL), D_FF ** -0.5),
        "final_norm": 1.0 + nrm(ks[25], (D_MODEL,), 0.1),
    }

def first_block(x, ffn1_norm, ffn1_w_gate, ffn1_w_up, ffn1_w_down, mix_norm, w_in, mu_shift,
              w0, w_lora_up, a0, a_lora_up, g_lora_up, k_k, k_a, r_k, ln_w, ln_b,
              w_pool, pool_scale, w_out, ffn2_norm, ffn2_w_gate, ffn2_w_up, ffn2_w_down,
              final_norm):
    split_points = np.cumsum(SPLIT_SIZES[:5]).tolist()
    for l in range(DEPTH):
        x = x + 0.5 * swiglu(rms_norm(x, ffn1_norm[l]), ffn1_w_gate[l], ffn1_w_up[l], ffn1_w_down[l])

        h = rms_norm(x, mix_norm[l])
        p = h @ w_in[l]
        p_rw, p_pool = p[..., :RWKV_COLS], p[..., RWKV_COLS:]
        p_rw = p_rw + (token_shift(p_rw) - p_rw) * mu_shift[l]
        p_r, p_k, p_v, p_w, p_a, p_g = jnp.split(p_rw, split_points, axis=-1)
        y_rw = rwkv7_time_mix(p_r, p_k, p_v, p_w, p_a, p_g, w0[l], w_lora_up[l], a0[l],
                              a_lora_up[l], g_lora_up[l], k_k[l], k_a[l], r_k[l],
                              ln_w[l], ln_b[l])
        y_pool = multiscale_pool_mix(p_pool, w_pool[l], pool_scale[l])
        x = x + jnp.concatenate([y_rw, y_pool], axis=-1) @ w_out[l]

        x = x + 0.5 * swiglu(rms_norm(x, ffn2_norm[l]), ffn2_w_gate[l], ffn2_w_up[l], ffn2_w_down[l])
    return rms_norm(x, final_norm)


MIX_WIDTH_2 = D_MODEL
HEAD_DIM = 64
SWA_Q_HEADS = 8
SWA_KV_HEADS = 2
SWA_GROUP = SWA_Q_HEADS // SWA_KV_HEADS
WINDOW = 128
BLOCK = 128
DIFF_HEADS = 4
DIFF_VDIM = 2 * HEAD_DIM
Q_BLOCK = 128
SWA_Q_COLS = SWA_Q_HEADS * HEAD_DIM
SWA_KV_COLS = SWA_KV_HEADS * HEAD_DIM
DIFF_QK_COLS = DIFF_HEADS * 2 * HEAD_DIM
DIFF_V_COLS = DIFF_HEADS * DIFF_VDIM
IN_COLS_2 = SWA_Q_COLS + 2 * SWA_KV_COLS + 2 * DIFF_QK_COLS + DIFF_V_COLS
SWA_OUT = SWA_Q_HEADS * HEAD_DIM
DIFF_OUT = DIFF_HEADS * DIFF_VDIM
MEM_LEN = 256
CROSS_HEADS = 4
CROSS_HEAD_DIM = D_MODEL // CROSS_HEADS
D_FF_2 = 4 * D_MODEL
ROPE_THETA = 10000.0
NORM_EPS = 1e-5


def rms_norm_2(x, g, eps=NORM_EPS):
    xf = x.astype(jnp.float32)
    y = xf * lax.rsqrt(jnp.mean(xf * xf, axis=-1, keepdims=True) + eps)
    return (y * g.astype(jnp.float32)).astype(x.dtype)

def rope_tables(positions, dim):
    inv_freq = ROPE_THETA ** (-jnp.arange(0, dim, 2, dtype=jnp.float32) / dim)
    ang = positions.astype(jnp.float32)[..., None] * inv_freq
    return jnp.cos(ang), jnp.sin(ang)

def apply_rope(x, cos, sin):
    shp = cos.shape[:2] + (1,) * (x.ndim - 3) + cos.shape[-1:]
    c = cos.reshape(shp).astype(x.dtype)
    s = sin.reshape(shp).astype(x.dtype)
    x1, x2 = jnp.split(x, 2, axis=-1)
    return jnp.concatenate([x1 * c - x2 * s, x2 * c + x1 * s], axis=-1)

def sliding_window_sink_attention(q, k, v, sinks):
    Bn, S = q.shape[0], q.shape[1]
    nb = S // BLOCK
    scale = HEAD_DIM ** -0.5
    qb = q.reshape(Bn, nb, BLOCK, SWA_KV_HEADS, SWA_GROUP, HEAD_DIM)
    kb = k.reshape(Bn, nb, BLOCK, SWA_KV_HEADS, HEAD_DIM)
    vb = v.reshape(Bn, nb, BLOCK, SWA_KV_HEADS, HEAD_DIM)
    pad = ((0, 0), (1, 0), (0, 0), (0, 0), (0, 0))
    kw = jnp.concatenate([jnp.pad(kb, pad)[:, :-1], kb], axis=2)
    vw = jnp.concatenate([jnp.pad(vb, pad)[:, :-1], vb], axis=2)
    s = jnp.einsum('bnqhgd,bnkhd->bnhgqk', qb, kw).astype(jnp.float32) * scale
    qi = jnp.arange(BLOCK)[:, None]
    kj = jnp.arange(2 * BLOCK)[None, :]
    rel = qi + BLOCK - kj
    band = (rel >= 0) & (rel < WINDOW)
    exists = (jnp.arange(nb)[:, None, None] * BLOCK + kj[None]) >= BLOCK
    valid = band[None] & exists
    s = jnp.where(valid[None, :, None, None], s, -jnp.inf)
    sink = sinks.astype(jnp.float32).reshape(SWA_KV_HEADS, SWA_GROUP)[None, None, :, :, None, None]
    m = jnp.maximum(jnp.max(s, axis=-1, keepdims=True), sink)
    e = jnp.exp(s - m)
    p = e / (jnp.sum(e, axis=-1, keepdims=True) + jnp.exp(sink - m))
    o = jnp.einsum('bnhgqk,bnkhd->bnqhgd', p.astype(v.dtype), vw)
    return o.reshape(Bn, S, SWA_OUT)

def differential_attention(q, k, v, lam):
    Bn, S = q.shape[0], q.shape[1]
    nb = S // Q_BLOCK
    scale = HEAD_DIM ** -0.5
    qb = q.reshape(Bn, nb, Q_BLOCK, DIFF_HEADS, 2, HEAD_DIM).swapaxes(0, 1)
    starts = jnp.arange(nb) * Q_BLOCK
    kpos = jnp.arange(S)

    def one_block(args):
        qblk, start = args
        s = jnp.einsum('bqhcd,bkhcd->bhcqk', qblk, k).astype(jnp.float32) * scale
        mask = kpos[None, :] <= (start + jnp.arange(Q_BLOCK))[:, None]
        s = jnp.where(mask, s, -jnp.inf)
        p = jax.nn.softmax(s, axis=-1)
        a = p[:, :, 0] - lam * p[:, :, 1]
        return jnp.einsum('bhqk,bkhe->bqhe', a.astype(v.dtype), v)

    o = lax.map(one_block, (qb, starts))
    return o.swapaxes(0, 1).reshape(Bn, S, DIFF_HEADS, DIFF_VDIM)

def cross_attention(h, m, w_q, w_kv, w_o):
    Bn, S = h.shape[0], h.shape[1]
    q = (h @ w_q).reshape(Bn, S, CROSS_HEADS, CROSS_HEAD_DIM)
    kv = (m @ w_kv).reshape(Bn, m.shape[1], 2, CROSS_HEADS, CROSS_HEAD_DIM)
    k, v = kv[:, :, 0], kv[:, :, 1]
    s = jnp.einsum('bshd,bmhd->bhsm', q, k).astype(jnp.float32) * CROSS_HEAD_DIM ** -0.5
    p = jax.nn.softmax(s, axis=-1)
    o = jnp.einsum('bhsm,bmhd->bshd', p.astype(v.dtype), v).reshape(Bn, S, D_MODEL)
    return o @ w_o

def second_inputs(seed: int = 0) -> dict:
    key = jax.random.key(seed)
    ks = jax.random.split(key, 24)
    f32 = jnp.float32
    L = DEPTH

    def w(k, shape, fan_in):
        return jax.random.normal(k, shape, f32) * fan_in ** -0.5

    def gain(k, shape):
        return 1.0 + 0.02 * jax.random.normal(k, shape, f32)

    x = jax.random.normal(ks[0], (BATCH, SEQ, D_MODEL), f32)
    mem = jax.random.normal(ks[1], (BATCH, MEM_LEN, D_MODEL), f32)
    positions = (jnp.arange(SEQ, dtype=jnp.int32)[None, :]
                 + jax.random.randint(ks[2], (BATCH, 1), 0, 1024, dtype=jnp.int32))
    return {
        "x": x,
        "mem": mem,
        "positions": positions,
        "g_mix": gain(ks[3], (L, D_MODEL)),
        "w_in": w(ks[4], (L, D_MODEL, IN_COLS_2), D_MODEL),
        "sinks": 0.5 * jax.random.normal(ks[5], (L, SWA_Q_HEADS), f32),
        "lambda_q1": 0.1 * jax.random.normal(ks[6], (L, HEAD_DIM), f32),
        "lambda_k1": 0.1 * jax.random.normal(ks[7], (L, HEAD_DIM), f32),
        "lambda_q2": 0.1 * jax.random.normal(ks[8], (L, HEAD_DIM), f32),
        "lambda_k2": 0.1 * jax.random.normal(ks[9], (L, HEAD_DIM), f32),
        "g_diff": gain(ks[10], (L, DIFF_VDIM)),
        "w_out": w(ks[11], (L, MIX_WIDTH_2, D_MODEL), MIX_WIDTH_2),
        "g_cross": gain(ks[12], (L, D_MODEL)),
        "g_mem": gain(ks[13], (L, D_MODEL)),
        "w_cq": w(ks[14], (L, D_MODEL, D_MODEL), D_MODEL),
        "w_ckv": w(ks[15], (L, D_MODEL, 2 * D_MODEL), D_MODEL),
        "w_co": w(ks[16], (L, D_MODEL, D_MODEL), D_MODEL),
        "g_mlp": gain(ks[17], (L, D_MODEL)),
        "w_up": w(ks[18], (L, D_MODEL, D_FF_2), D_MODEL),
        "w_down": w(ks[19], (L, D_FF_2, D_MODEL), D_FF_2),
        "g_final": gain(ks[20], (D_MODEL,)),
    }

def second_block(x, mem, positions, g_mix, w_in, sinks, lambda_q1, lambda_k1, lambda_q2, lambda_k2,
              g_diff, w_out, g_cross, g_mem, w_cq, w_ckv, w_co, g_mlp, w_up, w_down, g_final):
    Bn, S = x.shape[0], x.shape[1]
    cos, sin = rope_tables(positions, HEAD_DIM)
    splits = np.cumsum([SWA_Q_COLS, SWA_KV_COLS, SWA_KV_COLS, DIFF_QK_COLS, DIFF_QK_COLS])
    for l in range(DEPTH):
        h = rms_norm_2(x, g_mix[l])
        proj = h @ w_in[l]
        qa, ka, va, qd, kd, vd = jnp.split(proj, splits, axis=-1)
        qa = apply_rope(qa.reshape(Bn, S, SWA_KV_HEADS, SWA_GROUP, HEAD_DIM), cos, sin)
        ka = apply_rope(ka.reshape(Bn, S, SWA_KV_HEADS, HEAD_DIM), cos, sin)
        va = va.reshape(Bn, S, SWA_KV_HEADS, HEAD_DIM)
        out_a = sliding_window_sink_attention(qa, ka, va, sinks[l])

        lam_init = 0.8 - 0.6 * math.exp(-0.3 * l)
        lam = (jnp.exp(jnp.sum(lambda_q1[l].astype(jnp.float32) * lambda_k1[l].astype(jnp.float32)))
               - jnp.exp(jnp.sum(lambda_q2[l].astype(jnp.float32) * lambda_k2[l].astype(jnp.float32)))
               + lam_init)
        qd = apply_rope(qd.reshape(Bn, S, DIFF_HEADS, 2, HEAD_DIM), cos, sin)
        kd = apply_rope(kd.reshape(Bn, S, DIFF_HEADS, 2, HEAD_DIM), cos, sin)
        vd = vd.reshape(Bn, S, DIFF_HEADS, DIFF_VDIM)
        od = differential_attention(qd, kd, vd, lam)
        out_b = (rms_norm_2(od, g_diff[l]) * (1.0 - lam_init)).reshape(Bn, S, DIFF_OUT)

        x = x + jnp.concatenate([out_a, out_b], axis=-1) @ w_out[l]

        x = x + cross_attention(rms_norm_2(x, g_cross[l]), rms_norm_2(mem, g_mem[l]),
                                w_cq[l], w_ckv[l], w_co[l])

        u = rms_norm_2(x, g_mlp[l]) @ w_up[l]
        x = x + jnp.square(jax.nn.relu(u)) @ w_down[l]
    return rms_norm_2(x, g_final)


def setup_inputs(seed=0):
    out = dict(first_inputs(seed))
    for name, value in second_inputs(seed + 1).items():
        if name != "x":
            out[name + "_2"] = value
    return out


def reference(
    x, ffn1_norm, ffn1_w_gate, ffn1_w_up, ffn1_w_down, mix_norm, w_in, mu_shift, w0, w_lora_up,
    a0, a_lora_up, g_lora_up, k_k, k_a, r_k, ln_w, ln_b, w_pool, pool_scale, w_out, ffn2_norm,
    ffn2_w_gate, ffn2_w_up, ffn2_w_down, final_norm, mem_2, positions_2, g_mix_2, w_in_2,
    sinks_2, lambda_q1_2, lambda_k1_2, lambda_q2_2, lambda_k2_2, g_diff_2, w_out_2, g_cross_2,
    g_mem_2, w_cq_2, w_ckv_2, w_co_2, g_mlp_2, w_up_2, w_down_2, g_final_2,
):
    x = first_block(
        x, ffn1_norm, ffn1_w_gate, ffn1_w_up, ffn1_w_down, mix_norm, w_in, mu_shift, w0,
        w_lora_up, a0, a_lora_up, g_lora_up, k_k, k_a, r_k, ln_w, ln_b, w_pool, pool_scale,
        w_out, ffn2_norm, ffn2_w_gate, ffn2_w_up, ffn2_w_down, final_norm,
    )
    return second_block(
        x, mem_2, positions_2, g_mix_2, w_in_2, sinks_2, lambda_q1_2, lambda_k1_2, lambda_q2_2,
        lambda_k2_2, g_diff_2, w_out_2, g_cross_2, g_mem_2, w_cq_2, w_ckv_2, w_co_2, g_mlp_2,
        w_up_2, w_down_2, g_final_2,
    )


_drawn_inputs = setup_inputs


def setup_inputs(seed=0):
    import zlib

    import numpy as np

    out = dict(_drawn_inputs(seed))
    spreads = {}
    factors = {'w_lora_up': 5.965,
     'a0': 3.165,
     'ln_b': 2.758,
     'g_mix_2': 3.094,
     'sinks_2': 8.0,
     'g_diff_2': 5.406,
     'g_cross_2': 8.0,
     'g_mem_2': 8.0,
     'g_mlp_2': 9.703,
     'g_final_2': 7.953}
    for name, (base, spread) in spreads.items():
        noise = np.random.default_rng([zlib.crc32(name.encode()), seed]).standard_normal(out[name].shape)
        drawn = base * np.exp(spread * noise) if base else spread * noise
        out[name] = __import__('jax').numpy.asarray(drawn.astype(out[name].dtype))
    for name, factor in factors.items():
        out[name] = (out[name] * factor).astype(out[name].dtype)
    return out
```

```python
import math
from contextlib import ExitStack

import numpy as np
import concourse.bass as bass
from concourse import mybir

F32 = mybir.dt.float32
F32R = mybir.dt.float32r
I32 = mybir.dt.int32
ALU = mybir.AluOpType
ACT = mybir.ActivationFunctionType
AX_X = mybir.AxisListType.X

P = 128
D = 1024
T = 256
NT = T // P
KC = D // P
RW = 512
NF = RW // P
FF = 2816
FC = FF // P
FF2 = 4096
FC2 = FF2 // P
LORA = 1536
POOL = 1696
WINDOWS = (2, 4, 8, 16)
PAD = max(WINDOWS)
RMS_EPS = 1e-6
NORM_EPS = 1e-5
GN_EPS = 64e-5
L2_EPS = 1e-12
LN_DECAY = -math.exp(-0.5)
LAM_INIT = 0.8 - 0.6
NEG = -1e30

UNIT = 1024
RAW = 3
RING = 6
LEAD = 4
B_FFN1 = 0
B_WIN = B_FFN1 + 3 * FC
N_WIN = 18
B_WOUT = B_WIN + N_WIN
B_FFN2 = B_WOUT + KC
B_CKV = B_FFN2 + 3 * FC
N_CKV = 2 * KC
B_WIN2 = B_CKV + N_CKV
N_WIN2 = 18
B_WOUT2 = B_WIN2 + N_WIN2
B_CQ = B_WOUT2 + KC
B_CO = B_CQ + KC
B_MLP = B_CO + KC
N_UNITS = B_MLP + 2 * FC2

WIN_COLS = [LORA, LORA + P] + [x for f in range(NF) for x in (RW + f * P, f * P)] + \
           [POOL + g * P for g in range(NF)] + [2 * RW + f * P for f in range(NF)]

VEC_ROWS = {}
_at = 0
for _name, _n in (("ffn1_norm", 8), ("mix_norm", 8), ("ffn2_norm", 8), ("g_mix_2", 8), ("g_cross_2", 8),
                  ("g_mem_2", 8), ("g_mlp_2", 8), ("w0", 4), ("a0", 4), ("k_k", 4), ("k_a", 4), ("r_k", 4),
                  ("ln_w", 4), ("ln_b", 4), ("pool_scale", 4), ("mu_shift", 13), ("mu_tail", 1), ("g_diff_2", 1)):
    VEC_ROWS[_name] = _at
    _at += _n
N_VEC = _at

CONST_COLS = {}
_at = 0
for _name, _n in [("ident", P), ("eps", 1), ("eps_block", 1), ("swap32", P), ("swap64", P), ("blk", P), ("lt", P), ("gt", P), ("le", P),
                  ("lev0t", P), ("lev0", P)] + [(f"lev{k}t", P) for k in range(1, 7)] + \
                 [("prev", P), ("diag", P), ("invc", 4 * PAD), ("freq", 1), ("sign", 1)]:
    CONST_COLS[_name] = (_at, _n)
    _at += _n
N_CONST = _at
N_FIRST = CONST_COLS["swap32"][0]


def constants():
    c = np.zeros((P, N_CONST), np.float32)

    def put(name, value):
        a, n = CONST_COLS[name]
        c[:, a:a + n] = value

    i, j = np.arange(P)[:, None], np.arange(P)[None, :]
    put("ident", i == j)
    put("swap32", j == (i ^ 32))
    put("swap64", j == (i ^ 64))
    put("blk", (i // 64) == (j // 64))
    put("lt", i < j)
    put("gt", i > j)
    put("le", i <= j)
    for k in range(7):
        pair = (i >> (k + 1)) == (j >> (k + 1))
        upper = pair & (((i >> k) & 1) == 0) & (((j >> k) & 1) == 1)
        put(f"lev{k}t", upper)
        if k == 0:
            put("lev0", upper.T)
    put("prev", np.where(j > i, 0.0, NEG))
    put("diag", np.where(j <= i, 0.0, NEG))
    t1 = np.arange(1, PAD + 1)
    put("invc", np.concatenate([1.0 / np.minimum(t1, w) for w in WINDOWS])[None])
    put("freq", (np.float32(10000.0) ** (-(2 * (np.arange(P) % 32)).astype(np.float32) / np.float32(64)))[:, None])
    put("sign", np.where(np.arange(P) % 64 < 32, -1.0, 1.0)[:, None])
    put("eps", RMS_EPS)
    put("eps_block", NORM_EPS)
    return c


def build(nc, t, out):
    ctx = ExitStack()
    with ctx:
        def sb(name, shape, dt=F32):
            return ctx.enter_context(nc.sbuf_tensor(name, shape, dt))

        raw = sb("raw", [P, RAW, UNIT])
        whi = sb("whi", [P, RING, UNIT], F32R)
        wlo = sb("wlo", [P, RING, UNIT], F32R)
        X = sb("X", [P, NT, D])
        XT = sb("XT", [P, KC, 2 * T], F32R)
        H = sb("H", [P, 3, 2 * T], F32R)
        CON = sb("CON", [P, N_CONST])
        VEC = sb("VEC", [P, P])
        LWA = sb("LWA", [64, 2, RW])
        LWG = sb("LWG", [P, RW])
        WPL = sb("WPL", [P, NF, P])
        SMALL = sb("SMALL", [P, 512])
        AN = 24 * 1024
        arena = sb("arena", [P, AN])
        PS = [ctx.enter_context(nc.psum_tensor(f"ps{i}", [P, 512], F32)) for i in range(8)]

        def ar(off, *shape):
            n = int(np.prod(shape))
            assert off + n <= AN, (off, shape)
            v = arena[:, off:off + n]
            if len(shape) == 2:
                v = v.rearrange("p (a b) -> p a b", a=shape[0])
            return v

        def con(name, rows=P):
            a, n = CONST_COLS[name]
            return CON[0:rows, a:a + n]

        def vec(name, i=0):
            c = VEC_ROWS[name] + i
            return VEC[:, c:c + 1]

        ident = con("ident")

        DIAG = ar(0, NT, P)
        GL, GS, SG, UL, US, HS = (ar(2048 + 768 * k, 3, T) for k in range(6))
        SQJ = ar(6656, D)
        ROWS = ar(8192, P)
        FIRST = ar(8320, P)[0:KC, :]
        GFIN = ar(8192, D)
        MEMX = ar(11008, NT, D)
        SS, MS, RR = SMALL[:, 328:330], SMALL[:, 332:334], SMALL[:, 334:336]

        PR, PK, PV, SW, AA, GG, KK, K2, CC, EC, IP, BON = (ar(1024 * k, NF, T) for k in range(12))
        VTOK = ar(1024 * 1, NT, RW)
        BTOK = ar(1024 * 3, RW)
        KTOK = ar(1024 * 3 + 512, RW)
        RB = ar(1024 * 8, 4, T)
        SQ = IP
        YO = PV
        GV = EC
        MB = 12 * 1024
        mats = [{n: ar(MB + 512 * (8 * g + k), 4, P) for k, n in ((4, "XM"), (5, "XMT"), (6, "TS"), (7, "LEV"))}
                for g in range(2)]
        for g in range(2):
            for k, n in ((0, "LT"), (2, "MM")):
                mats[g][n] = ar(MB + 512 * (8 * g + k), 8 * P).rearrange("p (h m s) -> p h m s", h=2, m=4)
        PB = [ar(MB, NF, PAD + T), ar(MB + 1088, NF, PAD + T)]
        MX = ar(MB + 512 * 6, NF, T)
        DP = ar(MB + 512 * 14, NF, T)
        EX = MB + 512 * 16
        LBUF = ar(EX, 2, T)
        LW = ar(EX + 512, T)
        LG = ar(EX + 768, T)
        FAC = ar(EX + 1024, NF)
        CM = ar(EX + 1032, 2 * NF)
        ST = ar(EX + 1040, NF, 64)
        PTM = ar(EX + 1296, PAD)
        WLOW = ar(EX + 1312, 2, T)
        WRAW = ar(EX + 1824, 2, T + 1)
        WDF = ar(EX + 2340, 2, T)
        PP = ar(EX + 2852, NF, PAD + T)

        QKV = ar(0, N_WIN2, T)
        KSW = ar(4608, T)
        RC, RSN = ar(4864, T), ar(5120, T)
        RT = ar(5376, 2, T)
        VT2 = ar(5888, NT, 640)
        SC = ar(7168, 12, 512)
        POSI, POSF, ANG = (ar(9216 + 256 * k, T) for k in range(3))
        RA = [ar(9984 + 256 * k, T) for k in range(4)]
        PTS = ar(13312, 9, 512)
        NMX, SUM, REC, ESK = (ar(17920 + 48 * k, 48) for k in range(4))
        ODJ = ar(0, D)
        ODS = ar(18112, 8)
        ODR = ar(18120, 8)
        ODN = ar(18432, NT, RW)
        LAMV = SMALL[:, 0:320].rearrange("p (a b) -> p a b", a=5)
        SNK = SMALL[:, 320:328]
        LDOT = SMALL[:, 340:342]
        LEXP = SMALL[:, 342:344]
        NLAM = SMALL[:, 344:345]
        GD8 = SMALL[:, 345:346]
        CK = ar(19456, KC, T)
        CVT = ar(21504, NT, D)
        CLOW = ar(23552, 2, T)
        CTM = ar(24064, 2, T)
        CQ = ar(0, KC, T)
        CSC = ar(2048, 4, 512)
        CPT = ar(4096, 4, 512)
        CNM, CSUM, CREC = (ar(6144 + 8 * k, 8) for k in range(3))

        def sems(names):
            return [ctx.enter_context(nc.semaphore(n)) for n in names.split()]

        unit_used, half_used, hi_ready, lo_ready = \
            sems("unit_used half_used hi_ready lo_ready")
        const_in, table_in, rows_zero, rows_in, first_in, x_in, mem_in, small_in, gain_in, pos_in = \
            sems("const_in table_in rows_zero rows_in first_in x_in mem_in small_in gain_in pos_in")
        out_done, = sems("out_done")
        vec_tp, vec_ready, ss, rms, xn, tp, xt_hi = \
            sems("vec_tp vec_ready ss rms xn tp xt_hi")
        xt_ready, x_upd = \
            sems("xt_ready x_upd")
        g_low, g_sum, silu, u_low, u_sum, h_val, h_hi, h_ready = \
            sems("g_low g_sum silu u_low u_sum h_val h_hi h_ready")
        r_low, r_sum, r_hi, r_ready = \
            sems("r_low r_sum r_hi r_ready")
        w_zero, w_low, w_sum, w_mix, lora_act, lora_mm, sw_done, sa_done = \
            sems("w_zero w_low w_sum w_mix lora_act lora_mm sw_done sa_done")
        sg_done, sq_ready, ssq_mm, nrm_done, ec_ready, dec_done, kk_ready, bp_ready = \
            sems("sg_done sq_ready ssq_mm nrm_done ec_ready dec_done kk_ready bp_ready")
        bp_mm, bon_done, tok_mm, tok_ev = \
            sems("bp_mm bon_done tok_mm tok_ev")
        m_mm, m_ev, levmask, t_mm, t_ev, inv_mm, inv_ev, s_r_mm = \
            sems("m_mm m_ev levmask t_mm t_ev inv_mm inv_ev s_r_mm")
        s_r_ev, s_u_mm, s_u_ev, s_y_mm, s_y_ev, s_s_mm, s_s_ev = \
            sems("s_r_ev s_u_mm s_u_ev s_y_mm s_y_ev s_s_mm s_s_ev")
        mean_mm, gd_ready, var_mm, gn_var, gn_std, y_val, y_hi, yt_ready = \
            sems("mean_mm gd_ready var_mm gn_var gn_std y_val y_hi yt_ready")
        shift_ready, pooled, pool_mm, pool_hi = \
            sems("shift_ready pooled pool_mm pool_hi")
        rope_arg, rope_tab, lam_arg, lam_exp, q_low, q_sum, rope_mm, rope_done = \
            sems("rope_arg rope_tab lam_arg lam_exp q_low q_sum rope_mm rope_done")
        vt_mm, vt_ev, sc_mm, sc_sum, sc_max, sc_exp, p_ready, pt_mm = \
            sems("vt_mm vt_ev sc_mm sc_sum sc_max sc_exp p_ready pt_mm")
        pt_ev, pv_mm, o_hi, od_ss, od_ms, od_std, od_norm, odt_mm = \
            sems("pt_ev pv_mm o_hi od_ss od_ms od_std od_norm odt_mm")
        c_low, c_sum, ct_mm, ct_ev = \
            sems("c_low c_sum ct_mm ct_ev")
        own_dve, = sems("own_dve")
        raw_full = [ctx.enter_context(nc.semaphore(f"raw_full{i}")) for i in range(RAW)]
        block = ctx.enter_context(nc.Block())


        def bc(ap, n):
            return ap.rearrange("p (a b) -> p a b", a=1).broadcast_to([P, n, ap.shape[-1]])

        class Count:
            def __init__(self):
                self.n = 0

            def next(self):
                self.n += 1
                return 1

        RMS_NORMS = (0, 1, 2, 4)
        NTP = {"ffn1": 0, "mix": 1, "ffn2": 2, "mem": 3, "mix2": 4, "cross": 5, "mlp": 6}
        JOBS = [("swa", 1, [0, 2]), ("swa", 1, [4, 6]), ("swa", 1, [1, 3]), ("swa", 1, [5, 7]),
                ("swa", 0, [0, 2, 4, 6]), ("swa", 0, [1, 3, 5, 7]),
                ("diff", 1, [0, 2]), ("diff", 1, [1, 3]), ("diff", 1, [4, 6]), ("diff", 1, [5, 7]),
                ("diff", 0, [0, 2, 4, 6]), ("diff", 0, [1, 3, 5, 7])]
        BLOCKS = [[(j, m, kb) for m in range(2) for kb in range(2)] for j in range(4)] + \
                 [[(j, m, 0) for m in range(4)] for j in (4, 5)] + \
                 [[(j, m, kb) for m in range(2) for kb in range(2)] for j in (6, 8)] + \
                 [[(10, m, 0) for m in range(4)]]
        W_BANKS, Q_BANKS, C_BANKS = (4, 5, 2, 3), (4, 5, 0, 1), (4, 5, 6, 7)
        BLOCK_AT = {b: (g, i) for g, bs in enumerate(BLOCKS) for i, b in enumerate(bs)}

        @block.sync
        def _(sp):
            def load(n, dn, src):
                if n >= RAW:
                    sp.wait_ge(lo_ready, n - RAW + 1 + dn)
                dst = raw[:, n % RAW, :]
                if len(src.shape) == 3:
                    dst = dst.rearrange("p (c n) -> p c n", c=src.shape[1])
                sp.dma_start(dst, src).then_inc(raw_full[n % RAW], 16)

            def cols(name, lo=None):
                v = t[name][0].rearrange("(c p) n -> p c n", p=P)
                return v[:, :, lo:lo + P] if lo is not None else v

            def rows(name):
                return t[name][0].rearrange("(j p) n -> p j n", p=P)

            for tt in range(NT):
                sp.dma_start(X[:, tt, :], t["x"][0, tt * P:(tt + 1) * P, :]).then_inc(x_in, 16)
            sp.dma_start(CON[:, 0:N_FIRST], t["consts"][:, 0:N_FIRST]).then_inc(const_in, 16)
            sp.dma_start(FIRST, t["ffn1_norm"][0].rearrange("(a b) -> a b", b=P)).then_inc(first_in, 16)
            for n in range(RAW):
                load(n, 0, cols(("ffn1_w_gate", "ffn1_w_up")[n % 2], (n // 2) * P))
            sp.wait_ge(rows_zero, 1)
            for name in ("mix_norm", "ffn2_norm", "g_mix_2", "g_cross_2", "g_mem_2", "g_mlp_2",
                         "w0", "a0", "k_k", "k_a", "ln_w", "ln_b", "pool_scale", "g_diff_2"):
                r = VEC_ROWS[name] - KC
                n = t[name].shape[1] // P
                sp.dma_start(ROWS[r:r + n, :], t[name][0].rearrange("(a b) -> a b", b=P)).then_inc(rows_in, 16)
            r = VEC_ROWS["r_k"] - KC
            sp.dma_start(ROWS[r:r + 4, :], t["r_k"][0].rearrange("(a h) d -> a (h d)", h=2)).then_inc(rows_in,
                16)
            r = VEC_ROWS["mu_shift"] - KC
            sp.dma_start(ROWS[r:r + 13, :], t["mu_shift"][0, 0:13 * P].rearrange("(a b) -> a b",
                b=P)).then_inc(rows_in, 16)
            sp.dma_start(ROWS[r + 13:r + 14, 0:32], t["mu_shift"][:, 13 * P:POOL]).then_inc(rows_in, 16)
            sp.dma_start(CON[:, N_FIRST:], t["consts"][:, N_FIRST:]).then_inc(table_in, 16)
            sp.dma_start(LWA[0:32, 0, :], t["w_lora_up"][0]).then_inc(small_in, 16)
            sp.dma_start(LWA[32:64, 1, :], t["a_lora_up"][0]).then_inc(small_in, 16)
            sp.dma_start(LWG[64:128, :], t["g_lora_up"][0, 0:64, :]).then_inc(small_in, 16)
            sp.dma_start(LWG[0:32, :], t["g_lora_up"][0, 64:96, :]).then_inc(small_in, 16)
            sp.dma_start(WPL[:, :, :], t["w_pool"][0].rearrange("g c d -> c g d")).then_inc(small_in, 16)

            def load_ffn(b, pre, first):
                g, u, d = pre + "_w_gate", pre + "_w_up", pre + "_w_down"
                for n, src in ((0, cols(g, 0)), (1, cols(u, 0)), (2, cols(g, P))):
                    if not first:
                        load(b + n, 0, src)
                with sp.Fori(0, 10) as i:
                    for k in range(2):
                        for m in range(3):
                            q = 3 * k + m
                            if m == 0:
                                src = cols(u)[:, :, bass.ds(i * (2 * P) + (k + 1) * P, P)]
                            elif m == 1:
                                src = rows(d)[:, bass.ds(i * 2 + k, 1), :]
                            else:
                                src = cols(g)[:, :, bass.ds(i * (2 * P) + (k + 2) * P, P)]
                            load(b + 3 + q, i * 6, src)
                load(b + 63, 0, cols(u, 21 * P))
                load(b + 64, 0, rows(d)[:, 20:21, :])
                load(b + 65, 0, rows(d)[:, 21:22, :])

            load_ffn(B_FFN1, "ffn1", True)
            for i, c in enumerate(WIN_COLS):
                load(B_WIN + i, 0, cols("w_in", c))
            for i, c in enumerate((4, 5, 6, 7, 0, 1, 2, 3)):
                load(B_WOUT + i, 0, rows("w_out")[:, c:c + 1, :])
            load_ffn(B_FFN2, "ffn2", False)
            sp.wait_ge(x_upd, 4 * 2)
            sp.dma_start(GFIN, t["final_norm"].rearrange("(a n) -> a n", a=1).broadcast_to([P,
                D])).then_inc(gain_in, 16)
            sp.dma_start(MEMX, t["mem_2"][0].rearrange("(a p) n -> p a n", p=P)).then_inc(mem_in, 16)
            sp.dma_start(POSI.bitcast(I32), t["positions_2"].broadcast_to([P, T])).then_inc(pos_in, 16)
            for k, name in enumerate(("lambda_q1_2", "lambda_k1_2", "lambda_q2_2", "lambda_k2_2")):
                sp.dma_start(LAMV[:, k, :], t[name].broadcast_to([P, 64])).then_inc(pos_in, 16)
            sp.dma_start(SNK, t["sinks_2"].broadcast_to([P, 8])).then_inc(pos_in, 16)
            for i in range(N_CKV):
                load(B_CKV + i, 0, cols("w_ckv_2", i * P))
            for i in range(N_WIN2):
                load(B_WIN2 + i, 0, cols("w_in_2", i * P))
            for c in range(KC):
                load(B_WOUT2 + c, 0, rows("w_out_2")[:, c:c + 1, :])
            for i in range(KC):
                load(B_CQ + i, 0, cols("w_cq_2", i * P))
            for c in range(KC):
                load(B_CO + c, 0, rows("w_co_2")[:, c:c + 1, :])
            load(B_MLP, 0, cols("w_up_2", 0))
            up, down = cols("w_up_2"), rows("w_down_2")
            with sp.Fori(0, 10) as i:
                for k in range(3):
                    load(B_MLP + 1 + 2 * k, i * 6, up[:, :, bass.ds(i * (3 * P) + (k + 1) * P, P)])
                    load(B_MLP + 2 + 2 * k, i * 6, down[:, bass.ds(i * 3 + k, 1), :])
            load(B_MLP + 61, 0, cols("w_up_2", 31 * P))
            load(B_MLP + 62, 0, down[:, 30:31, :])
            load(B_MLP + 63, 0, down[:, 31:32, :])
            sp.wait_ge(x_upd, 4 * 5)
            sp.dma_start(GFIN, t["g_final_2"].rearrange("(a n) -> a n", a=1).broadcast_to([P,
                D])).then_inc(gain_in, 16)
            sp.wait_ge(x_upd, 4 * 8)
            sp.dma_start(out[0].rearrange("(a p) n -> p a n", p=P), X[:, :, :]).then_inc(out_done, 16)
            sp.wait_ge(out_done, 16)

        @block.tensor
        def _(pe):
            def mm(o, st, mv, start=True, stop=True):
                return pe.matmul(o, st, mv, start=start, stop=stop, skip_group_check=True)

            def a_unit(n, dn, bank, after=None):
                pe.wait_ge(lo_ready, n + 1 + dn)
                s = n % RING
                for c in range(KC):
                    if after and c % 2 == 0:
                        pe.wait_ge(xt_ready, 4 * NTP[after] + c // 2 + 1)
                    cs = slice(c * P, (c + 1) * P)
                    mm(bank[:, :], whi[:, s, cs], XT[:, c, :], start=(c == 0), stop=(c == KC - 1))
                    last = mm(bank[:, 0:T], wlo[:, s, cs], XT[:, c, 0:T], start=False, stop=(c == KC - 1))
                last.then_inc(unit_used, 1)

            def b_unit(n, dn, act, start=False, stop=False):
                pe.wait_ge(lo_ready, n + 1 + dn)
                s = n % RING
                for tt in range(NT):
                    hi = act[:, tt * P:(tt + 1) * P]
                    lo = act[:, T + tt * P:T + (tt + 1) * P]
                    for st, wt, a, z in ((hi, whi, start, False), (hi, wlo, False, False), (lo, whi, False, stop)):
                        for h in range(2):
                            last = mm(PS[2 * tt + h][:, :], st, wt[:, s, 512 * h:512 * h + 512], start=a, stop=z)
                    if stop and tt == 0:
                        last.then_inc(half_used, 1)
                last.then_inc(unit_used, 1)

            def norm_t(name):
                q = NTP[name]
                src = MEMX if name == "mem" else X
                for tt in range(NT):
                    pe.wait_ge(xn, 2 * q + tt + 1)
                    for b in range(4):
                        for c in (2 * b, 2 * b + 1):
                            last = mm(PS[4 + b][:, (c % 2) * T + tt * P:(c % 2) * T + (tt + 1) * P],
                                      src[:, tt, c * P:(c + 1) * P], DIAG[:, tt, :])
                        if tt == NT - 1:
                            last.then_inc(tp, 1)

            def ffn(b, f):
                J = FC * f

                def gate_up(j, n, dn=0, dj=0, after=None):
                    if J + j >= 2:
                        pe.wait_ge(h_ready, J + j - 1 + dj)
                    a_unit(b + n, dn, PS[4 + j % 2], after)
                    a_unit(b + n + 1, dn, PS[6 + j % 2])

                def down(j, n, dn=0, dj=0, **k):
                    pe.wait_ge(h_ready, J + j + 1 + dj)
                    b_unit(b + n, dn, H[:, j % 2, :], **k)

                gate_up(0, 0, after=("ffn1", "ffn2")[f])
                gate_up(1, 2)
                down(0, 4, start=True)
                with pe.Fori(0, 10) as i:
                    for k in range(2):
                        gate_up(2 + k, 5 + 3 * k, i * 6, i * 2)
                        down(1 + k, 7 + 3 * k, i * 6, i * 2)
                if f == 0:
                    pe.wait_ge(table_in, 16)
                    pe.wait_ge(rows_in, 16 * 17)
                    pe.wait_ge(h_ready, FC)
                    pe.transpose(PS[7][:, KC:N_VEC], ROWS[0:N_VEC - KC, :],
                                 ident[0:N_VEC - KC, 0:N_VEC - KC]).then_inc(vec_tp, 1)
                down(21, 65, stop=True)

            def mix():
                def lora(f):
                    fs = slice(f * P, (f + 1) * P)
                    pe.wait_ge(lora_act, 4)
                    if f >= 2:
                        pe.wait_ge(sa_done, f - 1)
                        pe.wait_ge(sg_done, f - 1)
                    wa, gate = PS[6 - 6 * (f % 2)], PS[7 - 6 * (f % 2)]
                    mm(wa[:, 0:T], LWA[:, 0, fs], LW[0:64, :])
                    mm(wa[:, T:2 * T], LWA[:, 1, fs], LW[0:64, :]).then_inc(lora_mm, 1)
                    mm(gate[:, 0:T], LWG[:, fs], LG[:, :]).then_inc(lora_mm, 1)

                def head_sums(src, ready, done):
                    pe.wait_ge(ready, 1)
                    for k in range(2):
                        mm(PS[6 + k][:, :], con("blk"), src[:, 2 * k:2 * k + 2, :]).then_inc(done, 1)

                pe.wait_ge(small_in, 16 * 5)
                pe.wait_ge(w_zero, 6)
                for i in range(N_WIN):
                    if i >= 4:
                        pe.wait_ge(w_sum, i - 3)
                    a_unit(B_WIN + i, 0, PS[W_BANKS[i % 4]], None if i else "mix")
                    if 3 <= i < 3 + NF:
                        lora(i - 3)
                    if i == 12:
                        pe.wait_ge(sg_done, NF)
                        head_sums(SQ, sq_ready, ssq_mm)
                    if i == 15:
                        pe.wait_ge(nrm_done, 2)
                        head_sums(DP, bp_ready, bp_mm)
                pe.wait_ge(w_sum, N_WIN)
                pe.wait_ge(w_mix, 14)
                for c in range(NT):
                    for f in range(NF):
                        last = pe.transpose(PS[c][:, f * P:(f + 1) * P], PV[:, f, c * P:(c + 1) * P], ident)
                    last.then_inc(tok_mm, 1)
                pe.wait_ge(kk_ready, 1)
                for k, src in enumerate((AA, K2)):
                    for f in range(NF):
                        last = pe.transpose(PS[2 + k][:, f * P:(f + 1) * P], src[:, f, 0:P], ident)
                    last.then_inc(tok_mm, 1)
                pe.wait_ge(bon_done, 1)
                for g in range(NF):
                    pe.wait_ge(pooled, g + 1)
                    mm(PS[4 + g][:, 0:T], WPL[:, g, :], PB[g % 2][:, g, PAD:]).then_inc(pool_mm, 1)
                pe.wait_ge(tok_ev, 4)
                pe.wait_ge(yt_ready, 4)
                for wv in range(2):
                    if wv:
                        pe.wait_ge(s_y_ev, 1)
                        pe.wait_ge(s_s_ev, 1)
                        pe.wait_ge(s_u_ev, 2)
                    for g in range(2):
                        f = 2 * wv + g
                        for r, pairs in enumerate((((AA, KK), (K2, KK)), ((KK, AA),), ((AA, PR), (K2, PR)))):
                            for h in range(2):
                                q = g * 6 + 2 * r + h
                                if q >= 8:
                                    pe.wait_ge(m_ev, 12 * wv + q - 7)
                                hp = slice(64 * h, 64 * h + 64)
                                for k, (a, b) in enumerate(pairs):
                                    for c in range(NT):
                                        m = 2 * k + c
                                        last = mm(PS[q % 8][:, m * P:(m + 1) * P], a[hp, f, c * P:(c + 1) * P],
                                                  b[hp, f, c * P:(c + 1) * P])
                                last.then_inc(m_mm, 1)
                    pe.wait_ge(m_ev, 12 * wv + 12)
                    for k in range(1, 7):
                        for g in range(2):
                            n = wv * 12 + (k - 1) * 2 + g
                            pe.wait_ge(inv_ev, wv * 14 + (k - 1) * 2 + g + 1)
                            pe.wait_ge(levmask, n + 1)
                            M = mats[g]
                            for m in range(4):
                                last = mm(PS[3 * g][:, m * P:(m + 1) * P], M["LEV"][:, m, :], M["XM"][:, m, :])
                            last.then_inc(t_mm, 1)
                        for g in range(2):
                            n = wv * 12 + (k - 1) * 2 + g
                            pe.wait_ge(t_ev, n + 1)
                            M = mats[g]
                            if k < 6:
                                for m in range(4):
                                    mm(PS[3 * g + 1][:, m * P:(m + 1) * P], M["XMT"][:, m, :], M["TS"][:, m, :])
                            for m in range(4):
                                last = mm(PS[3 * g + 2][:, m * P:(m + 1) * P], M["TS"][:, m, :], M["XMT"][:, m, :])
                            last.then_inc(inv_mm, 1)
                    pe.wait_ge(inv_ev, wv * 14 + 14)
                    heads = [(g, hh) for g in range(2) for hh in range(2)]
                    for c in range(NT):
                        n = 2 * wv + c

                        def at(g, hh):
                            return 2 * wv + g, slice(64 * hh, 64 * hh + 64), slice(64 * (2 * hh + g), 64 * (2 * hh + g) + 64)

                        def vt(g, hh):
                            f = 2 * wv + g
                            return VTOK[:, c, f * P + 64 * hh:f * P + 64 * hh + 64]

                        if c:
                            pe.wait_ge(s_s_ev, wv + 1)
                        for hh in range(2):
                            for g in range(2):
                                f, hp, hc = at(g, hh)
                                o = PS[5 + hh][:, g * 64:g * 64 + 64]
                                if c:
                                    mm(o, KK[hp, f, P:2 * P], ST[hp, f, :], stop=False)
                                last = mm(o, mats[g]["LT"][:, hh, 2 + c, :], vt(g, hh), start=(c == 0))
                        last.then_inc(s_r_mm, 1)
                        pe.wait_ge(s_r_ev, n + 1)
                        for g, hh in heads:
                            f, hp, hc = at(g, hh)
                            last = mm(PS[7][:, hc], mats[g]["XMT"][:, 2 * hh + c, :], RB[:, 2 * c, hc])
                        last.then_inc(s_u_mm, 1)
                        pe.wait_ge(s_u_ev, n + 1)
                        if c == 0:
                            for g, hh in heads:
                                f, hp, hc = at(g, hh)
                                fc = slice(f * P + 64 * hh, f * P + 64 * hh + 64)
                                o = PS[1][hp, g * 64:g * 64 + 64]
                                mm(o, BTOK[:, fc], RB[:, 1, hc], stop=False)
                                last = mm(o, KTOK[:, fc], vt(g, hh), start=False)
                            last.then_inc(s_s_mm, 1)
                        for g, hh in heads:
                            f, hp, hc = at(g, hh)
                            o = PS[0][hp, g * T + c * P:g * T + (c + 1) * P]
                            if c:
                                mm(o, ST[hp, f, :], PR[hp, f, P:2 * P], stop=False)
                            mm(o, RB[:, 2 * c + 1, hc], mats[g]["MM"][:, hh, c, :], start=(c == 0), stop=False)
                            last = mm(o, vt(g, hh), mats[g]["MM"][:, hh, 2 + c, :], start=False)
                        if c:
                            last.then_inc(s_y_mm, 1)
                for k in range(2):
                    pe.wait_ge(s_y_ev, k + 1)
                    mm(PS[2 + k][:, :], con("blk"), YO[:, 2 * k:2 * k + 2, :]).then_inc(mean_mm, 1)
                for k in range(2):
                    pe.wait_ge(gd_ready, k + 1)
                    mm(PS[2 + k][:, :], con("blk"), GV[:, 2 * k:2 * k + 2, :]).then_inc(var_mm, 1)
                pe.wait_ge(gn_var, 2)
                for i, c in enumerate((4, 5, 6, 7, 0, 1, 2, 3)):
                    pe.wait_ge(yt_ready, i + 1)
                    b_unit(B_WOUT + i, 0, XT[:, c, :], start=(i == 0), stop=(i == KC - 1))

            def attention():
                norm_t("mem")

                def turn_value(i):
                    pe.wait_ge(c_sum, i + 1)
                    k = i - KC
                    if k >= 2:
                        pe.wait_ge(ct_ev, k - 1)
                    for tt in range(NT):
                        last = pe.transpose(PS[6 + i % 2][:, tt * P:(tt + 1) * P], CTM[:, i % 2, tt * P:(tt + 1) * P],
                                            ident)
                    last.then_inc(ct_mm, 1)

                for i in range(N_CKV):
                    if i == 2:
                        pe.wait_ge(x_upd, 4 * 3)
                    if i >= 4:
                        pe.wait_ge(c_sum, i - 3)
                    a_unit(B_CKV + i, 0, PS[Q_BANKS[i % 4]], None if i else "mem")
                    if i - 1 >= KC:
                        turn_value(i - 1)
                turn_value(N_CKV - 1)
                pe.wait_ge(ct_ev, KC)
                norm_t("mix2")

                n_rope = n_vt = 0
                for i in range(N_WIN2 + 1):
                    if i < N_WIN2:
                        if i >= 4:
                            pe.wait_ge(q_sum, i - 3)
                        a_unit(B_WIN2 + i, 0, PS[Q_BANKS[i % 4]], None if i else "mix2")
                    k = i - 1
                    if k < 0:
                        continue
                    pe.wait_ge(q_sum, k + 1)
                    if k == 5 or k >= 14:
                        if n_vt >= 2:
                            pe.wait_ge(vt_ev, n_vt - 1)
                        for tt in range(NT):
                            last = pe.transpose(PS[7 - 4 * (n_vt % 2)][:, tt * P:(tt + 1) * P], QKV[:, k, tt * P:(tt + 1) * P], ident)
                        last.then_inc(vt_mm, 1)
                        n_vt += 1
                    else:
                        if n_rope >= 2:
                            pe.wait_ge(rope_done, n_rope - 1)
                        mm(PS[6 - 4 * (n_rope % 2)][:, 0:T], con("swap32"), QKV[:, k, :]).then_inc(rope_mm, 1)
                        n_rope += 1
                pe.wait_ge(rope_done, n_rope)
                mm(PS[6][:, 0:T], con("swap64"), QKV[:, 4, :]).then_inc(rope_mm, 1)
                pe.wait_ge(rope_done, n_rope + 1)
                pe.wait_ge(vt_ev, 5)
                for j, (kind, n, maps) in enumerate(JOBS):
                    if j >= 4:
                        pe.wait_ge(sc_sum, j - 3)
                    nk = (n + 1) * P
                    for m, h in enumerate(maps):
                        hp = slice(64 * (h % 2), 64 * (h % 2) + 64)
                        if kind == "swa":
                            q, kt = QKV[hp, h // 2, n * P:(n + 1) * P], (QKV[hp, 4, 0:nk] if h // 4 == h % 2 else KSW[hp, 0:nk])
                        else:
                            q, kt = QKV[hp, 6 + h // 2, n * P:(n + 1) * P], QKV[hp, 10 + h // 2, 0:nk]
                        last = mm(PS[j % 4][:, m * nk:(m + 1) * nk], q, kt)
                    last.then_inc(sc_mm, 1)
                pe.wait_ge(vt_ev, 5)
                for g, bs in enumerate(BLOCKS):
                    pe.wait_ge(p_ready, g + 1)
                    if g >= 4:
                        pe.wait_ge(pt_ev, g - 3)
                    for i, (j, m, kb) in enumerate(bs):
                        nk = (JOBS[j][1] + 1) * P
                        last = pe.transpose(PS[4 + g % 4][:, i * P:(i + 1) * P],
                                            SC[:, j, m * nk + kb * P:m * nk + (kb + 1) * P], ident)
                    last.then_inc(pt_mm, 1)

                def pt(j, m, kb):
                    g, i = BLOCK_AT[(j, m, kb)]
                    return PTS[:, g, i * P:(i + 1) * P]

                pe.wait_ge(sc_sum, 12)
                pe.wait_ge(pt_ev, 9)
                for h in range(8):
                    hp = slice(64 * (h % 2), 64 * (h % 2) + 64)
                    c, kv = h // 2, slice(64 * (h // 4), 64 * (h // 4) + 64)
                    o = PS[c // 2][hp, (c % 2) * T:(c % 2 + 1) * T]
                    j, m = 2 * (h % 2) + h // 4, (h // 2) % 2
                    mm(o[:, 0:P], VT2[:, 0, kv], pt(4 + h % 2, h // 2, 0))
                    mm(o[:, P:T], VT2[:, 0, kv], pt(j, m, 0), stop=False)
                    last = mm(o[:, P:T], VT2[:, 1, kv], pt(j, m, 1), start=False)
                    if h % 4 == 3:
                        last.then_inc(pv_mm, 1)
                for n in range(NT):
                    for h in range(4):
                        o = PS[2 + n][:, h * P:(h + 1) * P]
                        vs = slice(P + h * P, P + (h + 1) * P)
                        if n == 0:
                            last = mm(o, pt(10, h, 0), VT2[:, 0, vs])
                        else:
                            mm(o, pt(6 + 2 * (h // 2), h % 2, 0), VT2[:, 0, vs], stop=False)
                            last = mm(o, pt(6 + 2 * (h // 2), h % 2, 1), VT2[:, 1, vs], start=False)
                    last.then_inc(pv_mm, 1)
                for n in range(NT):
                    pe.wait_ge(od_norm, n + 1)
                for b in range(2):
                    for h in (2 * b, 2 * b + 1):
                        for n in range(NT):
                            last = pe.transpose(PS[4 + b][:, (h % 2) * T + n * P:(h % 2) * T + (n + 1) * P],
                                                ODN[:, n, h * P:(h + 1) * P], ident)
                    last.then_inc(odt_mm, 1)
                for c in range(KC):
                    pe.wait_ge(yt_ready, KC + max(4, c + 1))
                    b_unit(B_WOUT2 + c, 0, XT[:, c, :], start=(c == 0), stop=(c == KC - 1))

            def cross():
                norm_t("cross")
                for i in range(KC):
                    if i >= 4:
                        pe.wait_ge(c_sum, N_CKV + i - 3)
                    a_unit(B_CQ + i, 0, PS[C_BANKS[i % 4]], None if i else "cross")
                pe.wait_ge(x_upd, 4 * 5)
                for j in range(4):
                    n = j // 2
                    for m in range(2):
                        h = 2 * (j % 2) + m
                        pe.wait_ge(c_sum, N_CKV + 2 * h + 2)
                        for k in range(2):
                            last = mm(PS[j][:, m * T:(m + 1) * T], CQ[:, 2 * h + k, n * P:(n + 1) * P],
                                      CK[:, 2 * h + k, :], start=(k == 0), stop=(k == 1))
                    last.then_inc(sc_mm, 1)
                pe.wait_ge(c_sum, N_CKV + KC)
                for h in range(4):
                    pe.wait_ge(p_ready, 9 + 3 + h // 2)
                    for kb in range(2):
                        for n in range(NT):
                            last = pe.transpose(PS[4 + h][:, kb * T + n * P:kb * T + (n + 1) * P],
                                                CSC[:, 2 * n + h // 2, (h % 2) * T + kb * P:(h % 2) * T + (kb + 1) * P],
                                                ident)
                    last.then_inc(pt_mm, 1)
                pe.wait_ge(sc_sum, 12 + 4)
                for h in range(4):
                    pe.wait_ge(pt_ev, 9 + h + 1)
                    for d in range(2):
                        for kb in range(2):
                            last = mm(PS[h][:, d * T:(d + 1) * T], CVT[:, kb, h * 2 * P + d * P:h * 2 * P + (d + 1) * P],
                                      CPT[:, h, kb * T:(kb + 1) * T], start=(kb == 0), stop=(kb == 1))
                    last.then_inc(pv_mm, 1)
                pe.wait_ge(yt_ready, 2 * KC + KC)
                for c in range(KC):
                    b_unit(B_CO + c, 0, XT[:, c, :], start=(c == 0), stop=(c == KC - 1))

            def mlp():
                def up(j, n, dn=0, dj=0, after=None):
                    if j >= 3:
                        pe.wait_ge(r_ready, j - 2 + dj)
                    a_unit(B_MLP + n, dn, PS[4 + j % 3], after)

                def down(j, n, dn=0, dj=0, **k):
                    pe.wait_ge(r_ready, j + 1 + dj)
                    b_unit(B_MLP + n, dn, H[:, j % 3, :], **k)

                up(0, 0, after="mlp")
                up(1, 1)
                down(0, 2, start=True)
                up(2, 3)
                down(1, 4)
                up(3, 5)
                down(2, 6)
                with pe.Fori(0, 9) as i:
                    for k in range(3):
                        up(4 + k, 7 + 2 * k, i * 6, i * 3)
                        down(3 + k, 8 + 2 * k, i * 6, i * 3)
                up(31, 61)
                down(30, 62)
                down(31, 63, stop=True)

            pe.wait_ge(const_in, 16)
            pe.wait_ge(first_in, 16)
            pe.transpose(PS[7][:, 0:KC], FIRST, ident[0:KC, 0:KC]).then_inc(vec_tp, 1)
            pe.wait_ge(vec_ready, 1)
            norm_t("ffn1")
            ffn(B_FFN1, 0)
            pe.wait_ge(vec_ready, 2)
            norm_t("mix")
            pe.wait_ge(x_upd, 4 * 1)
            mix()
            norm_t("ffn2")
            pe.wait_ge(x_upd, 4 * 2)
            ffn(B_FFN2, 1)
            attention()
            cross()
            norm_t("mlp")
            pe.wait_ge(x_upd, 4 * 6)
            mlp()

        @block.scalar
        def _(act):
            def split_hi(n, i=None):
                c = 16 * (n // RAW + 1)
                act.wait_ge(raw_full[n % RAW], c if i is None else i * (16 * RING // RAW) + c)
                if n >= RING:
                    act.wait_ge(unit_used, n - RING + 1 if i is None else i * RING + (n - RING + 1))
                act.activation(whi[:, n % RING, :], raw[:, n % RAW, :], ACT.Copy).then_inc(hi_ready, 1)

            splits = Count()

            def split_to(n):
                while splits.n < min(n, N_UNITS):
                    split_hi(splits.n)
                    splits.next()

            def norm_sums(q, src, upd):
                if q:
                    act.activation(SMALL[:, 346 + q:347 + q], con("eps"), ACT.Sqrt)
                for tt in range(NT):
                    if upd:
                        act.wait_ge(x_upd, 4 * (upd - 1) + 2 * tt + 2)
                    if q + tt:
                        act.wait_ge(ss, 2 * q + tt)
                    act.activation(SQJ, src[:, tt, :], ACT.Square, accum_out=SS[:, tt:tt + 1]).then_inc(ss, 1)
                    act.wait_ge(ss, 2 * q + tt + 1)
                    act.activation(MS[:, tt:tt + 1], SS[:, tt:tt + 1], ACT.Sqrt, scale=1.0 / D,
                                   bias=con("eps" if q in RMS_NORMS else "eps_block")).then_inc(rms, 1)

            def norm_hi(name, gain):
                q = NTP[name]
                for b in range(4):
                    act.wait_ge(tp, 4 * q + b + 1)
                    for c in (2 * b, 2 * b + 1):
                        ins = act.activation(XT[:, c, 0:T], PS[4 + b][:, (c % 2) * T:(c % 2 + 1) * T], ACT.Copy,
                            scale=vec(gain, c))
                        if c % 2:
                            ins.then_inc(xt_hi, 1)

            def ffn(b, f):
                J = FC * f

                def chunk(j, i=None):
                    dj, dn = (0, 0) if i is None else (i * 2, i * 6)
                    q = j % 2
                    n_gate, n_up = (0, 1) if j == 0 else (3 * j - 1, 3 * j)

                    def next_split(k):
                        n = b + 3 * j + 4 + k
                        if n < N_UNITS:
                            split_hi(n, i)
                            if i is None:
                                splits.n = n + 1

                    next_split(0)
                    act.wait_ge(unit_used, b + n_gate + 1 + dn)
                    if J + j >= 2:
                        act.wait_ge(g_sum, J + j - 1 + dj)
                    act.activation(GL[:, q, :], PS[4 + q][:, T:2 * T], ACT.Copy).then_inc(g_low, 1)
                    next_split(1)
                    act.wait_ge(unit_used, b + n_up + 1 + dn)
                    if J + j >= 2:
                        act.wait_ge(u_sum, J + j - 1 + dj)
                    act.activation(UL[:, q, :], PS[6 + q][:, T:2 * T], ACT.Copy).then_inc(u_low, 1)
                    next_split(2)
                    act.wait_ge(g_sum, J + j + 1 + dj)
                    if J + j >= 2:
                        act.wait_ge(h_val, J + j - 1 + dj)
                    act.activation(SG[:, q, :], GS[:, q, :], ACT.Silu).then_inc(silu, 1)
                    act.wait_ge(h_val, J + j + 1 + dj)
                    if j >= 2:
                        act.wait_ge(unit_used, b + 3 * (j - 2) + 4 + 1 + dn)
                    act.activation(H[:, q, 0:T], HS[:, q, :], ACT.Copy).then_inc(h_hi, 1)

                split_to(b + LEAD)
                chunk(0)
                chunk(1)
                with act.Fori(0, 9) as i:
                    for k in range(2):
                        chunk(2 + k, i)
                chunk(20)
                chunk(21)

            def low(i, n, bank, dst, sem_low, sem_sum, base=0):
                split_to(n + LEAD + 1)
                act.wait_ge(unit_used, n + 1)
                if base + i >= 2:
                    act.wait_ge(sem_sum, base + i - 1)
                act.activation(dst[:, i % 2, :], bank[:, T:2 * T], ACT.Copy).then_inc(sem_low, 1)

            def mix():
                for i in range(N_WIN):
                    low(i, B_WIN + i, PS[W_BANKS[i % 4]], WLOW, w_low, w_sum)
                    if i == 2:
                        act.wait_ge(w_mix, 2)
                        act.wait_ge(w_zero, 6)
                        act.activation(LW[0:32, :], LBUF[0:32, 0, :], ACT.Tanh).then_inc(lora_act, 1)
                        act.activation(LW[32:64, :], LBUF[32:64, 0, :], ACT.Copy).then_inc(lora_act, 1)
                        act.activation(LG[64:128, :], LBUF[64:128, 0, :], ACT.Sigmoid).then_inc(lora_act, 1)
                        act.activation(LG[0:32, :], LBUF[0:32, 1, :], ACT.Sigmoid).then_inc(lora_act, 1)
                    if 4 <= i < 4 + NF:
                        f = i - 4
                        wa, gate = PS[6 - 6 * (f % 2)], PS[7 - 6 * (f % 2)]
                        act.wait_ge(lora_mm, 2 * f + 1)
                        act.activation(SW[:, f, :], wa[:, 0:T], ACT.Sigmoid, bias=vec("w0",
                            f)).then_inc(sw_done, 1)
                        act.activation(AA[:, f, :], wa[:, T:2 * T], ACT.Sigmoid, bias=vec("a0",
                            f)).then_inc(sa_done, 1)
                        act.wait_ge(lora_mm, 2 * f + 2)
                        act.activation(GG[:, f, :], gate[:, 0:T], ACT.Copy).then_inc(sg_done, 1)
                    if i == 13:
                        for k in range(2):
                            act.wait_ge(ssq_mm, k + 1)
                            act.activation(MX[:, 2 * k:2 * k + 2, :], PS[6 + k][:, :],
                                ACT.Sqrt).then_inc(nrm_done, 1)
                        act.wait_ge(ec_ready, 1)
                        act.wait_ge(ssq_mm, 2)
                        act.activation(IP[:, :, :], CC[:, :, :], ACT.Exp, scale=-LN_DECAY).then_inc(dec_done, 1)
                        act.activation(EC[:, :, :], EC[:, :, :], ACT.Exp, scale=LN_DECAY).then_inc(dec_done, 1)
                        act.activation(CC[:, :, :], CC[:, :, :], ACT.Exp, scale=LN_DECAY).then_inc(dec_done, 1)
                        act.activation(FAC, FAC, ACT.Exp, scale=LN_DECAY).then_inc(dec_done, 1)
                act.wait_ge(kk_ready, 1)
                for b, dst in enumerate((VTOK[:, 0, :], VTOK[:, 1, :], BTOK, KTOK)):
                    act.wait_ge(tok_mm, b + 1)
                    act.activation(dst, PS[b][:, :], ACT.Copy).then_inc(tok_ev, 1)
                act.wait_ge(unit_used, B_WIN + N_WIN)
                for g in range(NF):
                    act.wait_ge(pool_mm, g + 1)
                    act.activation(XT[:, 4 + g, 0:T], PS[4 + g][:, 0:T], ACT.Copy, scale=vec("pool_scale",
                        g)).then_inc(pool_hi, 1)
                split_to(B_WOUT + RING)
                for wv in range(2):
                    for k in range(1, 7):
                        for g in range(2):
                            n = wv * 12 + (k - 1) * 2 + g
                            act.wait_ge(t_mm, n + 1)
                            if n >= 2:
                                act.wait_ge(inv_mm, n - 1)
                            act.activation(mats[g]["TS"][:, :, :], PS[3 * g][:, :].rearrange("p (a b) -> p a b",
                                a=4), ACT.Copy).then_inc(t_ev, 1)
                    for c in range(NT):
                        n = 2 * wv + c
                        act.wait_ge(s_r_mm, n + 1)
                        act.activation(RB[:, 2 * c, 0:P], PS[5][:, 0:P], ACT.Copy)
                        act.activation(RB[:, 2 * c, P:2 * P], PS[6][:, 0:P], ACT.Copy).then_inc(s_r_ev, 1)
                        act.wait_ge(s_u_mm, n + 1)
                        act.activation(RB[:, 2 * c + 1, :], PS[7][:, 0:T], ACT.Copy).then_inc(s_u_ev, 1)
                    act.wait_ge(s_y_mm, wv + 1)
                    act.activation(YO[:, 2 * wv:2 * wv + 2, :], PS[0][:, :].rearrange("p (a b) -> p a b", a=2),
                        ACT.Copy).then_inc(s_y_ev, 1)
                for k in range(2):
                    act.wait_ge(gn_var, k + 1)
                    act.activation(GV[:, 2 * k:2 * k + 2, :], GV[:, 2 * k:2 * k + 2, :],
                        ACT.Sqrt).then_inc(gn_std, 1)
                for f in range(NF):
                    act.wait_ge(y_val, f + 1)
                    act.activation(XT[:, f, 0:T], YO[:, f, :], ACT.Copy).then_inc(y_hi, 1)
                for c in range(KC):
                    split_to(B_WOUT + c + LEAD + 1)

            def attention():
                act.wait_ge(mem_in, 16)
                norm_sums(3, MEMX, 0)
                norm_hi("mem", "g_mem_2")
                norm_sums(4, X, 3)
                for i in range(N_CKV):
                    low(i, B_CKV + i, PS[Q_BANKS[i % 4]], CLOW, c_low, c_sum)
                    if i == 2:
                        norm_sums(5, X, 4)
                    if i - 2 >= KC:
                        value(i - 2)
                for i in (N_CKV - 2, N_CKV - 1):
                    value(i)
                norm_hi("mix2", "g_mix_2")
                n_vt = 0
                for i in range(N_WIN2 + 1):
                    if i < N_WIN2:
                        low(i, B_WIN2 + i, PS[Q_BANKS[i % 4]], CLOW, q_low, q_sum)
                    if i == 1:
                        act.wait_ge(rope_arg, 1)
                        act.activation(RC, RA[0], ACT.Sin).then_inc(rope_tab, 1)
                        act.activation(RSN, RA[1], ACT.Sin).then_inc(rope_tab, 1)
                        act.wait_ge(lam_arg, 1)
                        act.activation(LEXP, LDOT, ACT.Exp).then_inc(lam_exp, 1)
                    k = i - 1
                    if k == 5 or k >= 14:
                        act.wait_ge(vt_mm, n_vt + 1)
                        act.activation(VT2[:, :, n_vt * P:(n_vt + 1) * P], PS[7 - 4 * (n_vt % 2)][:,
                            0:T].rearrange("p (a b) -> p a b", a=NT), ACT.Copy).then_inc(vt_ev, 1)
                        n_vt += 1
                split_to(B_WOUT2 + RING)
                for j, (kind, n, maps) in enumerate(JOBS):
                    act.wait_ge(sc_max, j + 1)
                    nk = (n + 1) * P
                    for m in range(len(maps)):
                        e = SC[:, j, m * nk:(m + 1) * nk]
                        q = 4 * j + m
                        done = m == len(maps) - 1 and kind == "diff"
                        ins = act.activation(e, e, ACT.Exp, bias=NMX[:, q:q + 1], accum_out=SUM[:, q:q + 1])
                        if done:
                            ins.then_inc(sc_exp, 1)
                    if kind == "swa":
                        q = slice(4 * j, 4 * j + len(maps))
                        act.activation(ESK[:, q], ESK[:, q], ACT.Exp).then_inc(sc_exp, 1)
                for g in range(9):
                    act.wait_ge(pt_mm, g + 1)
                    act.activation(PTS[:, g, :], PS[4 + g % 4][:, :], ACT.Copy).then_inc(pt_ev, 1)
                for n in range(NT):
                    act.wait_ge(pv_mm, 3 + n)
                    for h in range(4):
                        ins = act.activation(ODJ[:, (4 * n + h) * P:(4 * n + h + 1) * P], PS[2 + n][:,
                            h * P:(h + 1) * P], ACT.Square, accum_out=ODS[:, 4 * n + h:4 * n + h + 1])
                        if h == 3:
                            ins.then_inc(od_ss, 1)
                act.wait_ge(od_ms, 1)
                act.activation(ODS, ODS, ACT.Sqrt).then_inc(od_std, 1)
                for c in range(4):
                    act.wait_ge(pv_mm, c // 2 + 1)
                    ins = act.activation(XT[:, c, 0:T], PS[c // 2][:, (c % 2) * T:(c % 2 + 1) * T], ACT.Copy)
                    if c % 2:
                        ins.then_inc(o_hi, 1)
                for h in range(4):
                    act.wait_ge(odt_mm, h // 2 + 1)
                    ins = act.activation(XT[:, 4 + h, 0:T], PS[4 + h // 2][:, (h % 2) * T:(h % 2 + 1) * T], ACT.Copy,
                        scale=GD8)
                    if h % 2:
                        ins.then_inc(o_hi, 1)
                for c in range(KC):
                    split_to(B_WOUT2 + c + LEAD + 1)

            def value(i):
                k = i - KC
                act.wait_ge(ct_mm, k + 1)
                act.activation(CVT[:, :, k * P:(k + 1) * P], PS[6 + i % 2][:, 0:T].rearrange("p (a b) -> p a b",
                    a=NT), ACT.Copy).then_inc(ct_ev, 1)

            def cross():
                norm_sums(6, X, 5)
                norm_hi("cross", "g_cross_2")
                for i in range(KC):
                    low(i, B_CQ + i, PS[C_BANKS[i % 4]], CLOW, c_low, c_sum, N_CKV)
                split_to(B_CO + RING)
                for j in range(4):
                    act.wait_ge(sc_max, 12 + j + 1)
                    for m in range(2):
                        e, q = CSC[:, j, m * T:(m + 1) * T], 2 * j + m
                        ins = act.activation(e, e, ACT.Exp, bias=CNM[:, q:q + 1], accum_out=CSUM[:, q:q + 1])
                        if m:
                            ins.then_inc(sc_exp, 1)
                for h in range(4):
                    act.wait_ge(pt_mm, 9 + h + 1)
                    act.activation(CPT[:, h, :], PS[4 + h][:, :], ACT.Copy).then_inc(pt_ev, 1)
                for h in range(4):
                    act.wait_ge(pv_mm, 4 + h + 1)
                    for d in range(2):
                        ins = act.activation(XT[:, 2 * h + d, 0:T], PS[h][:, d * T:(d + 1) * T], ACT.Copy)
                        if d:
                            ins.then_inc(o_hi, 1)
                for c in range(KC):
                    split_to(B_CO + c + LEAD + 1)

            def mlp():
                def chunk(j, i=None):
                    dj, dn = (0, 0) if i is None else (i * 3, i * 6)
                    q = j % 3
                    for k in range(2):
                        if k:
                            act.wait_ge(unit_used, B_MLP + max(0, 2 * j - 1) + 1 + dn)
                            if j >= 3:
                                act.wait_ge(r_sum, j - 2 + dj)
                            act.activation(UL[:, q, :], PS[4 + q][:, T:2 * T], ACT.Copy).then_inc(r_low, 1)
                        n = B_MLP + 2 * j + LEAD + k
                        if n < N_UNITS:
                            split_hi(n, i)
                    act.wait_ge(h_val, 2 * FC + j + 1 + dj)
                    if j >= 3:
                        act.wait_ge(unit_used, B_MLP + 2 * (j - 3) + 2 + 1 + dn)
                    act.activation(H[:, q, 0:T], HS[:, q, :], ACT.Copy).then_inc(r_hi, 1)

                split_to(B_MLP + LEAD)
                for j in range(3):
                    chunk(j)
                with act.Fori(0, 9) as i:
                    for k in range(3):
                        chunk(3 + k, i)
                for j in (30, 31):
                    chunk(j)

            act.wait_ge(const_in, 16)
            act.wait_ge(x_in, 32)
            norm_sums(0, X, 0)
            split_to(2)
            act.wait_ge(vec_ready, 1)
            norm_hi("ffn1", "ffn1_norm")
            ffn(B_FFN1, 0)
            norm_sums(1, X, 1)
            act.wait_ge(vec_ready, 2)
            norm_hi("mix", "mix_norm")
            mix()
            norm_sums(2, X, 2)
            norm_hi("ffn2", "ffn2_norm")
            ffn(B_FFN2, 1)
            attention()
            cross()
            norm_sums(7, X, 6)
            norm_hi("mlp", "g_mlp_2")
            mlp()
            norm_sums(8, X, 7)

        @block.vector
        def _(dve):
            own = Count()

            add, sub, mul, mx, mn = ALU.add, ALU.subtract, ALU.mult, ALU.max, ALU.min

            def split_lo(n, i=None):
                dve.wait_ge(hi_ready, n + 1 if i is None else i * RING + (n + 1))
                if n >= RING:
                    dve.wait_ge(unit_used, n - RING + 1 if i is None else i * RING + (n - RING + 1))
                dve.tensor_tensor(wlo[:, n % RING, :], raw[:, n % RAW, :], whi[:, n % RING, :].bitcast(F32),
                    sub).then_inc(lo_ready, 1)

            splits = Count()

            def split_to(n):
                while splits.n < min(n, N_UNITS):
                    split_lo(splits.n)
                    splits.next()

            def norm(q, in_place=False):
                for tt in range(NT):
                    dve.wait_ge(rms, 2 * q + tt + 1)
                    dve.reciprocal(RR[:, tt:tt + 1], MS[:, tt:tt + 1]).then_inc(own_dve, own.next())
                    dve.wait_ge(own_dve, own.n)
                    if in_place:
                        for h in range(2):
                            xs, hs = X[:, tt, 512 * h:512 * h + 512], slice(512 * h, 512 * h + 512)
                            dve.scalar_tensor_tensor(xs, xs, RR[:, tt:tt + 1], GFIN[:, hs], mul, mul).then_inc(x_upd, 1)
                    else:
                        dve.tensor_scalar(DIAG[:, tt, :], ident, RR[:, tt:tt + 1], None, mul).then_inc(xn, 1)

            def rest(c, ps, scale=None):
                hi = XT[:, c, 0:T].bitcast(F32)
                if scale is None:
                    return dve.tensor_tensor(XT[:, c, T:2 * T], ps, hi, sub)
                return dve.scalar_tensor_tensor(XT[:, c, T:2 * T], ps, scale, hi, mul, sub)

            def norm_lo(name, gain):
                q = NTP[name]
                for b in range(4):
                    dve.wait_ge(xt_hi, 4 * q + b + 1)
                    for c in (2 * b, 2 * b + 1):
                        ins = rest(c, PS[4 + b][:, (c % 2) * T:(c % 2 + 1) * T], vec(gain, c))
                    ins.then_inc(xt_ready, 1)

            def update_x(nth, end, factor):
                dve.wait_ge(half_used, nth)
                for k in range(4):
                    if k == 2:
                        dve.wait_ge(unit_used, end)
                    xs = X[:, k // 2, (k % 2) * 512:(k % 2 + 1) * 512]
                    dve.scalar_tensor_tensor(xs, PS[k][:, :], factor, xs, mul, add).then_inc(x_upd, 1)

            def ffn(b, f):
                J = FC * f

                def chunk(j, i=None):
                    dj = 0 if i is None else i * 2
                    q = j % 2

                    def next_split(k):
                        n = b + 3 * j + 4 + k
                        if n < N_UNITS:
                            split_lo(n, i)
                            if i is None:
                                splits.n = n + 1

                    next_split(0)
                    dve.wait_ge(g_low, J + j + 1 + dj)
                    dve.tensor_tensor(GS[:, q, :], PS[4 + q][:, 0:T], GL[:, q, :], add).then_inc(g_sum, 1)
                    next_split(1)
                    dve.wait_ge(u_low, J + j + 1 + dj)
                    dve.tensor_tensor(US[:, q, :], PS[6 + q][:, 0:T], UL[:, q, :], add).then_inc(u_sum, 1)
                    next_split(2)
                    dve.wait_ge(u_sum, J + j + 1 + dj)
                    dve.wait_ge(silu, J + j + 1 + dj)
                    dve.tensor_tensor(HS[:, q, :], SG[:, q, :], US[:, q, :], mul).then_inc(h_val, 1)
                    dve.wait_ge(h_val, J + j + 1 + dj)
                    dve.wait_ge(h_hi, J + j + 1 + dj)
                    dve.tensor_tensor(H[:, q, T:2 * T], HS[:, q, :], H[:, q, 0:T].bitcast(F32),
                        sub).then_inc(h_ready, 1)

                split_to(b + LEAD)
                chunk(0)
                chunk(1)
                with dve.Fori(0, 9) as i:
                    for k in range(2):
                        chunk(2 + k, i)
                chunk(20)
                chunk(21)
                if f == 0:
                    dve.wait_ge(vec_tp, 2)
                    dve.tensor_copy(VEC[:, KC:N_VEC], PS[7][:, KC:N_VEC]).then_inc(vec_ready, 1)
                update_x(2 * f + 1, b + 66, 0.5)

            def mix():
                CC8 = CC.rearrange("p f (c s) -> p (f c) s", c=2)
                for i, col in enumerate(WIN_COLS):
                    n = B_WIN + i
                    split_to(n + LEAD + 1)
                    dve.wait_ge(w_low, i + 1)
                    ps, low = PS[W_BANKS[i % 4]][:, 0:T], WLOW[:, i % 2, :]
                    if 10 <= i < 14:
                        dve.tensor_tensor(PP[:, i - 10, PAD:], ps, low, add).then_inc(w_sum, 1)
                    else:
                        dst = LBUF[:, i, :] if i < 2 else PV[:, i - 14, :] if i >= 14 else \
                            (PK, PR)[i % 2][:, (i - 2) // 2, :]
                        mu = vec("mu_tail") if i == 1 else vec("mu_shift", col // P)
                        now, before = WRAW[:, i % 2, 1:T + 1], WRAW[:, i % 2, 0:T]
                        if i == 0:
                            dve.wait_ge(w_zero, 6)
                        dve.tensor_tensor(now, ps, low, add).then_inc(w_sum, 1)
                        dve.wait_ge(w_sum, i + 1)
                        dve.tensor_tensor(WDF[:, i % 2, :], before, now, sub).then_inc(own_dve, own.next())
                        dve.wait_ge(own_dve, own.n)
                        dve.scalar_tensor_tensor(dst, WDF[:, i % 2, :], mu, now, mul, add).then_inc(w_mix, 1)
                    if i == 8:
                        dve.wait_ge(sw_done, NF)
                        for f in range(NF):
                            for c in range(NT):
                                cs = slice(c * P, (c + 1) * P)
                                dve.tensor_tensor_scan(CC[:, f, cs], SW[:, f, cs], SW[:, f, cs], 0.0, add, mx).then_inc(own_dve, own.next())
                        dve.wait_ge(own_dve, own.n)
                        dve.tensor_copy(CM, CC8[:, :, P // 2 - 1]).then_inc(own_dve, own.next())
                        dve.wait_ge(own_dve, own.n)
                        for k in range(2 * NF):
                            dve.tensor_scalar(CC8[:, k, :], CC8[:, k, :], CM[:, k:k + 1], None,
                                sub).then_inc(own_dve, own.next())
                    if i == 9:
                        dve.wait_ge(sa_done, NF)
                        dve.wait_ge(w_mix, 10)
                        for f in range(NF):
                            dve.tensor_scalar(EC[:, f, :], AA[:, f, :], -1.0, vec("k_a", f), add,
                                mul).then_inc(own_dve, own.next())
                            dve.tensor_scalar(KK[:, f, :], PK[:, f, :], vec("k_k", f), None,
                                mul).then_inc(own_dve, own.next())
                        dve.wait_ge(own_dve, own.n)
                        dve.scalar_tensor_tensor(K2, EC, 1.0, PK, add, mul).then_inc(own_dve, own.next())
                        dve.tensor_tensor(SQ, KK, KK, mul).then_inc(sq_ready, 1)
                        dve.wait_ge(own_dve, own.n)
                        for f in range(NF):
                            ins = dve.scalar_tensor_tensor(DP[:, f, :], PR[:, f, :], vec("r_k", f), K2[:, f, :], mul,
                                mul)
                            if f == NF - 1:
                                ins.then_inc(bp_ready, 1)
                            else:
                                ins.then_inc(own_dve, own.next())
                        dve.tensor_tensor(EC, CC, SW, sub).then_inc(own_dve, own.next())
                        dve.tensor_tensor(FAC, CC[:, :, P - 1], CM.rearrange("p (f c) -> p f c", c=2)[:, :, 1],
                            add).then_inc(ec_ready, 1)
                    if i == 14:
                        dve.wait_ge(nrm_done, 2)
                        dve.tensor_scalar(MX, MX, L2_EPS, None, mx).then_inc(own_dve, own.next())
                        dve.wait_ge(own_dve, own.n)
                        dve.reciprocal(MX, MX).then_inc(own_dve, own.next())
                        dve.wait_ge(own_dve, own.n)
                        dve.tensor_tensor(KK, KK, MX, mul).then_inc(own_dve, own.next())
                        dve.wait_ge(own_dve, own.n)
                        dve.tensor_tensor(AA, AA, KK, mul).then_inc(own_dve, own.next())
                        dve.wait_ge(dec_done, 3)
                        dve.wait_ge(bp_ready, 1)
                        dve.wait_ge(own_dve, own.n)
                        dve.tensor_tensor(K2, K2, IP, mul).then_inc(own_dve, own.next())
                        dve.tensor_tensor(AA, AA, IP, mul).then_inc(own_dve, own.next())
                        dve.tensor_tensor(PR, PR, CC, mul).then_inc(own_dve, own.next())
                        dve.scalar_tensor_tensor(KK, KK, -1.0, EC, mul, mul).then_inc(kk_ready, 1)
                dve.wait_ge(w_mix, 14)
                for k in range(2):
                    dve.wait_ge(bp_mm, k + 1)
                    ins = dve.tensor_tensor(BON[:, 2 * k:2 * k + 2, :], PS[6 + k][:, :].rearrange("p (a b) -> p a b",
                        a=2), PV[:, 2 * k:2 * k + 2, :], mul)
                    if k:
                        ins.then_inc(bon_done, 1)
                    else:
                        ins.then_inc(own_dve, own.next())
                dve.wait_ge(shift_ready, 4)
                for g, win in enumerate(WINDOWS):
                    s, first = PB[g % 2][:, g, PAD:], PB[g % 2][:, g, PAD:PAD + win]
                    a = CONST_COLS["invc"][0] + g * PAD
                    if g:
                        dve.wait_ge(pooled, g)
                    dve.tensor_tensor(PTM[:, 0:win], first, CON[:, a:a + win], mul).then_inc(own_dve, own.next())
                    dve.wait_ge(own_dve, own.n)
                    dve.scalar_tensor_tensor(s, s, 1.0 / win, PP[:, g, PAD:], mul, sub).then_inc(own_dve,
                        own.next())
                    dve.wait_ge(own_dve, own.n)
                    dve.tensor_tensor(first, PTM[:, 0:win], PP[:, g, PAD:PAD + win], sub).then_inc(pooled, 1)
                for g in range(NF):
                    dve.wait_ge(pool_hi, g + 1)
                    rest(4 + g, PS[4 + g][:, 0:T], vec("pool_scale", g)).then_inc(yt_ready, 1)
                split_to(B_WOUT + RING)
                for wv in range(2):
                    for g in range(2):
                        M = mats[g]
                        for h in range(2):
                            dve.wait_ge(m_mm, 12 * wv + 6 * g + h + 1)
                            dve.tensor_tensor(M["LT"][:, h, :, :], PS[(6 * g + h) % 8][:,
                                :].rearrange("p (a b) -> p a b", a=4), bc(con("lt"), 4), mul).then_inc(m_ev, 1)
                        for h in range(2):
                            dve.wait_ge(m_mm, 12 * wv + 6 * g + 2 + h + 1)
                            dve.tensor_tensor(M["XM"][:, 2 * h:2 * h + 2, :], PS[(6 * g + 2 + h) % 8][:,
                                0:T].rearrange("p (a b) -> p a b", a=2), bc(con("lev0"), 2), mul).then_inc(m_ev,
                                    1)
                        for h in range(2):
                            dve.wait_ge(m_mm, 12 * wv + 6 * g + 4 + h + 1)
                            dve.tensor_tensor(M["MM"][:, h, :, :], PS[(6 * g + 4 + h) % 8][:,
                                :].rearrange("p (a b) -> p a b", a=4), bc(con("le"), 4), mul).then_inc(m_ev, 1)
                        dve.wait_ge(m_ev, 12 * wv + 6 * g + 6)
                        for h in range(2):
                            dve.tensor_tensor(M["XMT"][:, 2 * h:2 * h + 2, :], M["LT"][:, h, 0:2, :],
                                bc(con("lev0t"), 2), mul).then_inc(own_dve, own.next())
                        dve.tensor_tensor(M["XM"][:, :, :], M["XM"][:, :, :], bc(ident, 4),
                            add).then_inc(own_dve, own.next())
                        dve.wait_ge(own_dve, own.n)
                        dve.tensor_tensor(M["XMT"][:, :, :], M["XMT"][:, :, :], bc(ident, 4),
                            add).then_inc(inv_ev, 1)
                    for k in range(1, 7):
                        for g in range(2):
                            M = mats[g]
                            dve.wait_ge(inv_mm, wv * 12 + (k - 1) * 2 + g + 1)
                            psx, psxt = (PS[3 * g + n][:, :].rearrange("p (a b) -> p a b", a=4) for n in (1, 2))
                            if k < 6:
                                dve.tensor_tensor(M["XM"], psx, M["XM"], add).then_inc(own_dve, own.next())
                            dve.tensor_tensor(M["XMT"], psxt, M["XMT"], add).then_inc(inv_ev, 1)
                    dve.wait_ge(s_s_mm, wv + 1)
                    dve.wait_ge(dec_done, 4)
                    for g in range(2):
                        f = 2 * wv + g
                        ins = dve.tensor_scalar(ST[:, f, :], PS[1][:, g * 64:g * 64 + 64], FAC[:, f:f + 1], None, mul)
                        if g:
                            ins.then_inc(s_s_ev, 1)
                        else:
                            ins.then_inc(own_dve, own.next())
                for k in range(2):
                    fs = slice(2 * k, 2 * k + 2)
                    dve.wait_ge(mean_mm, k + 1)
                    dve.scalar_tensor_tensor(YO[:, fs, :], PS[2 + k][:, :].rearrange("p (a b) -> p a b", a=2),
                        -1.0 / 64, YO[:, fs, :], mul, add).then_inc(own_dve, own.next())
                    dve.wait_ge(own_dve, own.n)
                    dve.tensor_tensor(GV[:, fs, :], YO[:, fs, :], YO[:, fs, :], mul).then_inc(gd_ready, 1)
                for k in range(2):
                    fs = slice(2 * k, 2 * k + 2)
                    dve.wait_ge(var_mm, k + 1)
                    dve.tensor_scalar(GV[:, fs, :], PS[2 + k][:, :].rearrange("p (a b) -> p a b", a=2), 1.0 / 64,
                        GN_EPS, mul, add).then_inc(gn_var, 1)
                for k in range(2):
                    fs = slice(2 * k, 2 * k + 2)
                    dve.wait_ge(gn_std, k + 1)
                    dve.reciprocal(GV[:, fs, :], GV[:, fs, :]).then_inc(own_dve, own.next())
                    dve.wait_ge(own_dve, own.n)
                    dve.tensor_tensor(YO[:, fs, :], YO[:, fs, :], GV[:, fs, :], mul).then_inc(own_dve,
                        own.next())
                    dve.wait_ge(own_dve, own.n)
                    for f in (2 * k, 2 * k + 1):
                        dve.tensor_scalar(YO[:, f, :], YO[:, f, :], vec("ln_w", f), vec("ln_b", f), mul,
                            add).then_inc(own_dve, own.next())
                    dve.wait_ge(own_dve, own.n)
                    dve.tensor_tensor(YO[:, fs, :], YO[:, fs, :], BON[:, fs, :], add).then_inc(own_dve,
                        own.next())
                    dve.wait_ge(own_dve, own.n)
                    for f in (2 * k, 2 * k + 1):
                        dve.tensor_tensor(YO[:, f, :], YO[:, f, :], GG[:, f, :], mul).then_inc(y_val, 1)
                for f in range(NF):
                    dve.wait_ge(y_hi, f + 1)
                    rest(f, YO[:, f, :]).then_inc(yt_ready, 1)
                for c in range(KC):
                    split_to(B_WOUT + c + LEAD + 1)
                update_x(2, B_WOUT + KC, 1.0)

            def rope_args():
                C1, big = 6.28125, 12582912.0
                C2 = float(np.float32(2 * math.pi - C1))
                dve.wait_ge(pos_in, 16 * 6)
                dve.tensor_copy(POSF, POSI.bitcast(I32)).then_inc(own_dve, own.next())
                dve.wait_ge(own_dve, own.n)
                dve.tensor_scalar(ANG, POSF, con("freq"), None, mul).then_inc(own_dve, own.next())
                dve.wait_ge(own_dve, own.n)
                for k, turn in ((0, 0.25), (1, 0.0)):
                    dve.tensor_scalar(RA[k], ANG, 1.0 / (2 * math.pi), turn, mul, add).then_inc(own_dve,
                        own.next())
                    dve.wait_ge(own_dve, own.n)
                    dve.tensor_scalar(RA[k], RA[k], big, -big, add, add).then_inc(own_dve, own.next())
                    dve.wait_ge(own_dve, own.n)
                    dve.scalar_tensor_tensor(RA[2 + k], RA[k], -C1, ANG, mul, add).then_inc(own_dve, own.next())
                    dve.wait_ge(own_dve, own.n)
                    dve.scalar_tensor_tensor(RA[2 + k], RA[k], -C2, RA[2 + k], mul, add).then_inc(own_dve,
                        own.next())
                    dve.wait_ge(own_dve, own.n)
                    dve.tensor_scalar(RA[k], RA[2 + k], turn * 2 * math.pi, 3.1415925, add,
                        mn).then_inc(own_dve, own.next())
                    dve.wait_ge(own_dve, own.n)
                    dve.tensor_scalar(RA[k], RA[k], -3.1415925, None, mx).then_inc(own_dve, own.next())
                    dve.wait_ge(own_dve, own.n)
                dve.tensor_scalar(RA[1], RA[1], con("sign"), None, mul).then_inc(rope_arg, 1)
                for k in range(2):
                    dve.wait_ge(own_dve, own.n)
                    dve.tensor_tensor(LAMV[:, 4, :], LAMV[:, 2 * k, :], LAMV[:, 2 * k + 1, :],
                        mul).then_inc(own_dve, own.next())
                    dve.wait_ge(own_dve, own.n)
                    ins = dve.tensor_reduce(LDOT[:, k:k + 1], LAMV[:, 4, :], AX_X, add)
                    if k:
                        ins.then_inc(lam_arg, 1)
                    else:
                        ins.then_inc(own_dve, own.next())
                dve.tensor_scalar(GD8, vec("g_diff_2"), 1.0 - LAM_INIT, None, mul).then_inc(own_dve, own.next())

            def attention():
                norm(3)
                norm_lo("mem", "g_mem_2")
                dve.wait_ge(gain_in, 16)
                norm(4, in_place=True)
                for i in range(N_CKV):
                    split_to(B_CKV + i + LEAD + 1)
                    dve.wait_ge(c_low, i + 1)
                    k = i - KC
                    if k >= 2:
                        dve.wait_ge(ct_mm, k - 1)
                    dve.tensor_tensor(CK[:, i, :] if k < 0 else CTM[:, i % 2, :], PS[Q_BANKS[i % 4]][:, 0:T],
                        CLOW[:, i % 2, :], add).then_inc(c_sum, 1)
                    if i == 2:
                        norm(5)
                    if i == 6:
                        rope_args()
                norm_lo("mix2", "g_mix_2")
                dve.wait_ge(lam_arg, 1)
                n_rope = 0
                for i in range(N_WIN2 + 1):
                    if i < N_WIN2:
                        split_to(B_WIN2 + i + LEAD + 1)
                        dve.wait_ge(q_low, i + 1)
                        dve.tensor_tensor(QKV[:, i, :], PS[Q_BANKS[i % 4]][:, 0:T], CLOW[:, i % 2, :],
                            add).then_inc(q_sum, 1)
                    k = i - 1
                    if k >= 0 and k != 5 and k < 14:
                        if n_rope == 0:
                            dve.wait_ge(rope_tab, 2)
                            dve.wait_ge(lam_exp, 1)
                            dve.tensor_tensor(NLAM, LEXP[:, 1:2], LEXP[:, 0:1], sub).then_inc(own_dve,
                                own.next())
                            dve.wait_ge(own_dve, own.n)
                            dve.tensor_scalar(NLAM, NLAM, -LAM_INIT, None, add).then_inc(own_dve, own.next())
                        dve.wait_ge(rope_mm, n_rope + 1)
                        dve.wait_ge(q_sum, k + 1)
                        if n_rope:
                            dve.wait_ge(rope_done, n_rope)
                        dve.tensor_tensor(RT[:, 0, :], QKV[:, k, :], RC, mul).then_inc(own_dve, own.next())
                        dve.tensor_tensor(RT[:, 1, :], PS[6 - 4 * (n_rope % 2)][:, 0:T], RSN, mul).then_inc(own_dve, own.next())
                        dve.wait_ge(own_dve, own.n)
                        dve.tensor_tensor(QKV[:, k, :], RT[:, 0, :], RT[:, 1, :], add).then_inc(rope_done, 1)
                        n_rope += 1
                dve.wait_ge(rope_mm, n_rope + 1)
                dve.tensor_copy(KSW, PS[6][:, 0:T]).then_inc(rope_done, 1)
                split_to(B_WOUT2 + RING)

                def maxima(j):
                    kind, n, maps = JOBS[j]
                    nk, m = (n + 1) * P, len(maps)
                    q = slice(4 * j, 4 * j + m)
                    dve.wait_ge(sc_mm, j + 1)
                    s = SC[:, j, :].rearrange("p (m k) -> p m k", m=m)
                    ps = PS[j % 4][:, :].rearrange("p (m k) -> p m k", m=m)
                    if n and kind == "swa":
                        a = CONST_COLS["prev"][0]
                        dve.scalar_tensor_tensor(s, ps, 0.125, bc(CON[:, a:a + 2 * P], m), mul,
                            add).then_inc(sc_sum, 1)
                    elif n:
                        dve.tensor_scalar(s[:, :, 0:P], ps[:, :, 0:P], 0.125, None, mul).then_inc(own_dve,
                            own.next())
                        dve.scalar_tensor_tensor(s[:, :, P:], ps[:, :, P:], 0.125, bc(con("diag"), m), mul,
                            add).then_inc(sc_sum, 1)
                    else:
                        dve.scalar_tensor_tensor(s, ps, 0.125, bc(con("diag"), m), mul, add).then_inc(sc_sum, 1)
                    dve.wait_ge(sc_sum, j + 1)
                    dve.wait_ge(own_dve, own.n)
                    dve.tensor_reduce(NMX[:, q], s, AX_X, mx).then_inc(own_dve, own.next())
                    dve.wait_ge(own_dve, own.n)
                    if kind == "swa":
                        sink = SNK[:, maps[0]:maps[-1] + 1:2]
                        dve.tensor_tensor(NMX[:, q], NMX[:, q], sink, mx).then_inc(own_dve, own.next())
                        dve.wait_ge(own_dve, own.n)
                        dve.tensor_scalar(NMX[:, q], NMX[:, q], -1.0, None, mul).then_inc(own_dve, own.next())
                        dve.wait_ge(own_dve, own.n)
                        dve.tensor_tensor(ESK[:, q], sink, NMX[:, q], add).then_inc(sc_max, 1)
                    else:
                        dve.tensor_scalar(NMX[:, q], NMX[:, q], -1.0, None, mul).then_inc(sc_max, 1)

                def normalise(j):
                    kind, n, maps = JOBS[j]
                    nk, m = (n + 1) * P, len(maps)
                    q = slice(4 * j, 4 * j + m)
                    dve.wait_ge(sc_exp, j + 1)
                    if kind == "swa":
                        dve.tensor_tensor(SUM[:, q], SUM[:, q], ESK[:, q], add).then_inc(own_dve, own.next())
                        dve.wait_ge(own_dve, own.n)
                    dve.reciprocal(REC[:, q], SUM[:, q]).then_inc(own_dve, own.next())
                    dve.wait_ge(own_dve, own.n)
                    if kind == "diff" and j % 2 == 0:
                        return
                    if kind == "diff":
                        dve.tensor_scalar(REC[:, q], REC[:, q], NLAM, None, mul).then_inc(own_dve, own.next())
                        dve.wait_ge(own_dve, own.n)
                    for k in range(m):
                        e = SC[:, j, k * nk:(k + 1) * nk]
                        ins = dve.tensor_scalar(e, e, REC[:, 4 * j + k:4 * j + k + 1], None, mul)
                        if kind == "swa" and k == m - 1:
                            ins.then_inc(p_ready, 1)
                        else:
                            ins.then_inc(own_dve, own.next())
                    if kind == "diff":
                        dve.wait_ge(own_dve, own.n)
                        for k in range(m):
                            e, e1 = (SC[:, x, k * nk:(k + 1) * nk] for x in (j - 1, j))
                            ins = dve.scalar_tensor_tensor(e, e, REC[:, 4 * (j - 1) + k:4 * (j - 1) + k + 1], e1,
                                mul, add)
                            if k == m - 1:
                                ins.then_inc(p_ready, 1)
                            else:
                                ins.then_inc(own_dve, own.next())

                for j in range(12):
                    maxima(j)
                    if j:
                        normalise(j - 1)
                normalise(11)
                dve.wait_ge(od_ss, 2)
                dve.tensor_scalar(ODS, ODS, 1.0 / P, NORM_EPS, mul, add).then_inc(od_ms, 1)
                dve.wait_ge(od_std, 1)
                dve.reciprocal(ODR, ODS).then_inc(own_dve, own.next())
                dve.wait_ge(own_dve, own.n)
                for n in range(NT):
                    for h in range(4):
                        ins = dve.tensor_scalar(ODN[:, n, h * P:(h + 1) * P], PS[2 + n][:, h * P:(h + 1) * P], ODR[:,
                            4 * n + h:4 * n + h + 1], None, mul)
                        if h == 3:
                            ins.then_inc(od_norm, 1)
                        else:
                            ins.then_inc(own_dve, own.next())
                for c in range(4):
                    dve.wait_ge(o_hi, c // 2 + 1)
                    rest(c, PS[c // 2][:, (c % 2) * T:(c % 2 + 1) * T]).then_inc(yt_ready, 1)
                for h in range(4):
                    dve.wait_ge(o_hi, 2 + h // 2 + 1)
                    rest(4 + h, PS[4 + h // 2][:, (h % 2) * T:(h % 2 + 1) * T], GD8).then_inc(yt_ready, 1)
                for c in range(KC):
                    split_to(B_WOUT2 + c + LEAD + 1)
                update_x(4, B_WOUT2 + KC, 1.0)

            def cross():
                norm(6)
                norm_lo("cross", "g_cross_2")
                for i in range(KC):
                    split_to(B_CQ + i + LEAD + 1)
                    dve.wait_ge(c_low, N_CKV + i + 1)
                    dve.tensor_tensor(CQ[:, i, :], PS[C_BANKS[i % 4]][:, 0:T], CLOW[:, i % 2, :],
                        add).then_inc(c_sum, 1)
                split_to(B_CO + RING)

                def maxima(j):
                    dve.wait_ge(sc_mm, 12 + j + 1)
                    q = slice(2 * j, 2 * j + 2)
                    dve.tensor_scalar(CSC[:, j, :], PS[j][:, :], 1.0 / 16, None, mul).then_inc(sc_sum, 1)
                    dve.wait_ge(sc_sum, 12 + j + 1)
                    dve.tensor_reduce(CNM[:, q], CSC[:, j, :].rearrange("p (m k) -> p m k", m=2), AX_X, mx).then_inc(own_dve, own.next())
                    dve.wait_ge(own_dve, own.n)
                    dve.tensor_scalar(CNM[:, q], CNM[:, q], -1.0, None, mul).then_inc(sc_max, 1)

                def normalise(j):
                    q = slice(2 * j, 2 * j + 2)
                    dve.wait_ge(sc_exp, 12 + j + 1)
                    dve.reciprocal(CREC[:, q], CSUM[:, q]).then_inc(own_dve, own.next())
                    dve.wait_ge(own_dve, own.n)
                    for m in range(2):
                        e = CSC[:, j, m * T:(m + 1) * T]
                        ins = dve.tensor_scalar(e, e, CREC[:, 2 * j + m:2 * j + m + 1], None, mul)
                        if m:
                            ins.then_inc(p_ready, 1)
                        else:
                            ins.then_inc(own_dve, own.next())

                for j in range(4):
                    maxima(j)
                    if j:
                        normalise(j - 1)
                normalise(3)
                for h in range(4):
                    dve.wait_ge(o_hi, 4 + h + 1)
                    for d in range(2):
                        rest(2 * h + d, PS[h][:, d * T:(d + 1) * T]).then_inc(yt_ready, 1)
                for c in range(KC):
                    split_to(B_CO + c + LEAD + 1)
                update_x(5, B_CO + KC, 1.0)

            def mlp():
                def chunk(j, i=None):
                    dj = 0 if i is None else i * 3
                    q = j % 3
                    for k in range(2):
                        if k:
                            dve.wait_ge(r_low, j + 1 + dj)
                            dve.tensor_tensor(US[:, q, :], PS[4 + q][:, 0:T], UL[:, q, :], add).then_inc(r_sum, 1)
                        n = B_MLP + 2 * j + LEAD + k
                        if n < N_UNITS:
                            split_lo(n, i)
                    dve.wait_ge(r_sum, j + 1 + dj)
                    dve.scalar_tensor_tensor(HS[:, q, :], US[:, q, :], 0.0, US[:, q, :], mx, mul).then_inc(h_val, 1)
                    dve.wait_ge(h_val, 2 * FC + j + 1 + dj)
                    dve.wait_ge(r_hi, j + 1 + dj)
                    dve.tensor_tensor(H[:, q, T:2 * T], HS[:, q, :], H[:, q, 0:T].bitcast(F32), sub)\
                       .then_inc(r_ready, 1)

                split_to(B_MLP + LEAD)
                for j in range(3):
                    chunk(j)
                with dve.Fori(0, 9) as i:
                    for k in range(3):
                        chunk(3 + k, i)
                for j in (30, 31):
                    chunk(j)
                update_x(6, N_UNITS, 1.0)

            dve.wait_ge(vec_tp, 1)
            dve.tensor_copy(VEC[:, 0:KC], PS[7][:, 0:KC]).then_inc(vec_ready, 1)
            norm(0)
            dve.wait_ge(vec_ready, 1)
            split_to(2)
            norm_lo("ffn1", "ffn1_norm")
            ffn(B_FFN1, 0)
            norm(1)
            dve.wait_ge(vec_ready, 2)
            norm_lo("mix", "mix_norm")
            mix()
            norm(2)
            norm_lo("ffn2", "ffn2_norm")
            ffn(B_FFN2, 1)
            attention()
            cross()
            norm(7)
            norm_lo("mlp", "g_mlp_2")
            mlp()
            dve.wait_ge(gain_in, 32)
            norm(8, in_place=True)

        @block.gpsimd
        def _(pool):
            pool.memset(ROWS, 0.0).then_inc(rows_zero, 1)
            pool.wait_ge(rows_zero, 1)
            for n, a in enumerate((LWA[32:64, 0, :], LWA[0:32, 1, :], LWG[32:64, :], LG[32:64, :], WRAW[:, :, 0:1], PP[:, :, 0:PAD])):
                pool.memset(a, 0.0).then_inc(w_zero, 1)
                pool.wait_ge(w_zero, n + 1)
            pool.wait_ge(w_sum, 14)
            A, B = PB
            for k, (dst, src, g) in enumerate(((A, PP, 0), (B, A, 1), (A, B, 2), (B, A, 3))):
                n = 1 << k
                if k:
                    pool.wait_ge(shift_ready, k)
                pool.tensor_tensor(dst[:, g:, 2 * n - 1:], src[:, g:, 2 * n - 1:], src[:, g:, n - 1:PAD + T - n],
                                   ALU.add).then_inc(shift_ready, 1)
            pool.wait_ge(shift_ready, 4)
            for wv in range(2):
                for k in range(1, 7):
                    for g in range(2):
                        n = wv * 12 + (k - 1) * 2 + g
                        M = mats[g]
                        if k == 1:
                            pool.wait_ge(m_ev, 12 * wv + 6 * g + 2)
                        if n >= 2:
                            pool.wait_ge(t_mm, n - 1)
                        mask = con(f"lev{k}t").rearrange("p (a b c) -> p a b c", a=1, b=1)
                        pool.tensor_tensor(M["LEV"].rearrange("p (h c) s -> p h c s", h=2), M["LT"][:, :, 0:2, :],
                                           mask.broadcast_to([P, 2, 2, P]), ALU.mult).then_inc(levmask, 1)
                        pool.wait_ge(levmask, n + 1)


NAMES_IN = ("x ffn1_norm ffn1_w_gate ffn1_w_up ffn1_w_down mix_norm w_in mu_shift w0 w_lora_up a0 a_lora_up "
            "g_lora_up k_k k_a r_k ln_w ln_b w_pool pool_scale w_out ffn2_norm ffn2_w_gate ffn2_w_up ffn2_w_down "
            "final_norm mem_2 positions_2 g_mix_2 w_in_2 sinks_2 lambda_q1_2 lambda_k1_2 lambda_q2_2 lambda_k2_2 "
            "g_diff_2 w_out_2 g_cross_2 g_mem_2 w_cq_2 w_ckv_2 w_co_2 g_mlp_2 w_up_2 w_down_2 g_final_2").split()


def kernel(**inputs):
    import numpy as _np
    import concourse.bacc as _bacc
    from concourse import mybir as _mybir
    from concourse.bass_utils import run_bass_kernel_spmd as _run

    nc = _bacc.Bacc("TRN2", target_bir_lowering=False, num_devices=1)
    arrays, handles = {}, {}
    for name in NAMES_IN:
        a = _np.ascontiguousarray(inputs[name])
        arrays[f"in_{name}"] = a
        handles[name] = nc.dram_tensor(f"in_{name}", a.shape, _mybir.dt.from_np(a.dtype), kind="ExternalInput").ap()
    c = constants()
    arrays["in_consts"] = c
    handles["consts"] = nc.dram_tensor("in_consts", c.shape, _mybir.dt.float32, kind="ExternalInput").ap()
    out = nc.dram_tensor("out", (1, T, D), _mybir.dt.float32, kind="ExternalOutput").ap()
    build(nc, handles, out)
    r = _run(nc, [arrays], core_ids=[0])
    return r.results[0]["out"]
```

```python
import math
from contextlib import ExitStack

import numpy as np
import concourse.bass as bass
from concourse import mybir

F32 = mybir.dt.float32
F32R = mybir.dt.float32r
I32 = mybir.dt.int32
ALU = mybir.AluOpType
ACT = mybir.ActivationFunctionType
AX_X = mybir.AxisListType.X

P = 128
D = 1024
T = 256
NT = T // P
KC = D // P
RW = 512
NF = RW // P
FF = 2816
FC = FF // P
FF2 = 4096
FC2 = FF2 // P
LORA = 1536
POOL = 1696
WINDOWS = (2, 4, 8, 16)
PAD = max(WINDOWS)
RMS_EPS = 1e-6
NORM_EPS = 1e-5
GN_EPS = 64e-5
L2_EPS = 1e-12
LN_DECAY = -math.exp(-0.5)
LAM_INIT = 0.8 - 0.6
NEG = -1e30

UNIT = 1024
RAW = 3
RING = 6
LEAD = 4
B_FFN1 = 0
B_WIN = B_FFN1 + 3 * FC
N_WIN = 18
B_WOUT = B_WIN + N_WIN
B_FFN2 = B_WOUT + KC
B_CKV = B_FFN2 + 3 * FC
N_CKV = 2 * KC
B_WIN2 = B_CKV + N_CKV
N_WIN2 = 18
B_WOUT2 = B_WIN2 + N_WIN2
B_CQ = B_WOUT2 + KC
B_CO = B_CQ + KC
B_MLP = B_CO + KC
N_UNITS = B_MLP + 2 * FC2

WIN_COLS = [LORA, LORA + P] + [x for f in range(NF) for x in (RW + f * P, f * P)] + \
           [2 * RW + f * P for f in range(NF)] + [POOL + g * P for g in range(NF)]

VEC_ROWS = {}
_at = 0
for _name, _n in (("ffn1_norm", 8), ("mix_norm", 8), ("ffn2_norm", 8), ("g_mix_2", 8), ("g_cross_2", 8),
                  ("g_mem_2", 8), ("g_mlp_2", 8), ("w0", 4), ("a0", 4), ("k_k", 4), ("k_a", 4), ("r_k", 4),
                  ("ln_w", 4), ("ln_b", 4), ("pool_scale", 4), ("mu_shift", 13), ("mu_tail", 1), ("g_diff_2", 1)):
    VEC_ROWS[_name] = _at
    _at += _n
N_VEC = _at

CONST_COLS = {}
_at = 0
for _name, _n in [("ident", P), ("eps", 1), ("eps_block", 1), ("eps_group", 1), ("swap32", P), ("swap64", P), ("blk", P), ("lt", P), ("gt", P), ("le", P),
                  ("lev0t", P), ("lev0", P)] + [(f"lev{k}t", P) for k in range(1, 7)] + \
                 [("prev", P), ("diag", P), ("invc", 4 * PAD), ("freq", 1), ("sign", 1),
                     ("heads", NF * 8), ("spread", NF * P)]:
    CONST_COLS[_name] = (_at, _n)
    _at += _n
N_CONST = _at
N_FIRST = CONST_COLS["swap32"][0]


def constants():
    c = np.zeros((P, N_CONST), np.float32)

    def put(name, value):
        a, n = CONST_COLS[name]
        c[:, a:a + n] = value

    i, j = np.arange(P)[:, None], np.arange(P)[None, :]
    put("ident", i == j)
    put("swap32", j == (i ^ 32))
    put("swap64", j == (i ^ 64))
    put("blk", (i // 64) == (j // 64))
    put("lt", i < j)
    put("gt", i > j)
    put("le", i <= j)
    for k in range(7):
        pair = (i >> (k + 1)) == (j >> (k + 1))
        upper = pair & (((i >> k) & 1) == 0) & (((j >> k) & 1) == 1)
        put(f"lev{k}t", upper)
        if k == 0:
            put("lev0", upper.T)
    put("prev", np.where(j > i, 0.0, NEG))
    put("diag", np.where(j <= i, 0.0, NEG))
    t1 = np.arange(1, PAD + 1)
    put("invc", np.concatenate([1.0 / np.minimum(t1, w) for w in WINDOWS])[None])
    put("freq", (np.float32(10000.0) ** (-(2 * (np.arange(P) % 32)).astype(np.float32) / np.float32(64)))[:, None])
    put("sign", np.where(np.arange(P) % 64 < 32, -1.0, 1.0)[:, None])
    q = np.arange(2 * NF)
    put("heads", np.concatenate([q[None] == 2 * f + i // 64 for f in range(NF)], 1))
    put("spread", np.concatenate([i == 2 * f + j // 64 for f in range(NF)], 1))
    put("eps", RMS_EPS)
    put("eps_group", GN_EPS)
    put("eps_block", NORM_EPS)
    return c


def build(nc, t, out):
    ctx = ExitStack()
    with ctx:
        def sb(name, shape, dt=F32):
            return ctx.enter_context(nc.sbuf_tensor(name, shape, dt))

        raw = sb("raw", [P, RAW, UNIT])
        whi = sb("whi", [P, RING, UNIT], F32R)
        wlo = sb("wlo", [P, RING, UNIT], F32R)
        X = sb("X", [P, NT, D])
        XT = sb("XT", [P, KC, 2 * T], F32R)
        H = sb("H", [P, 3, 2 * T], F32R)
        CON = sb("CON", [P, N_CONST])
        VEC = sb("VEC", [P, P])
        LWA = sb("LWA", [64, 2, RW])
        LWG = sb("LWG", [P, RW])
        WPL = sb("WPL", [P, NF, P])
        SMALL = sb("SMALL", [P, 512])
        AN = 24 * 1024
        arena = sb("arena", [P, AN])
        PS = [ctx.enter_context(nc.psum_tensor(f"ps{i}", [P, 512], F32)) for i in range(8)]

        def ar(off, *shape):
            n = int(np.prod(shape))
            assert off + n <= AN, (off, shape)
            v = arena[:, off:off + n]
            if len(shape) == 2:
                v = v.rearrange("p (a b) -> p a b", a=shape[0])
            return v

        def con(name, rows=P):
            a, n = CONST_COLS[name]
            return CON[0:rows, a:a + n]

        def vec(name, i=0):
            c = VEC_ROWS[name] + i
            return VEC[:, c:c + 1]

        ident = con("ident")

        DIAG = ar(0, NT, P)
        GL, GS, SG, UL, US, HS = (ar(2048 + 768 * k, 3, T) for k in range(6))
        SQJ = ar(6656, D)
        ROWS = ar(8192, P)
        FIRST = ar(8320, P)[0:KC, :]
        GFIN = ar(8192, D)
        MEMX = ar(11008, NT, D)
        SS, MS, RR = SMALL[:, 328:330], SMALL[:, 332:334], SMALL[:, 334:336]

        PR, PK, PV, SW, AA, GG, KK, K2, CC, EC, IP, BON = (ar(1024 * k, NF, T) for k in range(12))
        VTOK = ar(1024 * 1, NT, RW)
        BTOK = ar(1024 * 3, RW)
        KTOK = ar(1024 * 3 + 512, RW)
        RB = ar(1024 * 8, 4, T)
        SQ = IP
        YO = PV
        GV = EC
        MB = 12 * 1024
        mats = [{n: ar(MB + 512 * (8 * g + k), 4, P) for k, n in ((4, "XM"), (5, "XMT"), (6, "TS"), (7, "LEV"))}
                for g in range(2)]
        for g in range(2):
            for k, n in ((0, "LT"), (2, "MM")):
                mats[g][n] = ar(MB + 512 * (8 * g + k), 8 * P).rearrange("p (h m s) -> p h m s", h=2, m=4)
        MX = ar(MB + 512 * 6, NF, T)
        DP = ar(MB + 512 * 14, NF, T)
        EX = MB + 512 * 16
        LBUF = ar(EX, 2, T)
        LW = ar(EX + 512, T)
        LG = ar(EX + 768, T)
        FAC = ar(EX + 1024, NF)
        CM = ar(EX + 1032, 2 * NF)
        ST = ar(EX + 1040, NF, 64)
        PTM = ar(EX + 1296, PAD)
        WLOW = ar(EX + 1312, 2, T)
        WRAW = ar(EX + 1824, 2, T + 1)
        WDF = ar(EX + 2340, 2, T)
        PP = ar(EX + 2852, NF, PAD + T)
        PB = [ar(EX + 1312, NF, PAD + T), ar(1024 * 10, NF - 1, PAD + T)]
        OMK = SMALL[:, 360:360 + NF]

        MXR = MX[0:8, 0, :]
        GVR = GV[0:8, 0, :]

        def heads(f):
            a = CONST_COLS["heads"][0] + 8 * f
            return CON[:, a:a + 8]

        def spread(f):
            a = CONST_COLS["spread"][0] + P * f
            return CON[0:8, a:a + P]

        def window(g, first=0, last=PAD + T):
            return PB[g % 2][:, g - g % 2:g - g % 2 + 1, first:last]


        QKV = ar(0, N_WIN2, T)
        KSW = ar(4608, T)
        RC, RSN = ar(4864, T), ar(5120, T)
        RT = ar(5376, 2, T)
        VT2 = ar(5888, NT, 640)
        SC = ar(7168, 12, 512)
        POSI, POSF, ANG = (ar(9216 + 256 * k, T) for k in range(3))
        RA = [ar(9984 + 256 * k, T) for k in range(4)]
        PTS = ar(13312, 9, 512)
        NMX, SUM, REC, ESK = (ar(17920 + 48 * k, 48) for k in range(4))
        ODJ = ar(0, D)
        ODS = ar(18112, 8)
        ODR = ar(18120, 8)
        ODN = ar(18432, NT, RW)
        LAMV = SMALL[:, 0:320].rearrange("p (a b) -> p a b", a=5)
        SNK = SMALL[:, 320:328]
        LDOT = SMALL[:, 340:342]
        LEXP = SMALL[:, 342:344]
        NLAM = SMALL[:, 344:345]
        GD8 = SMALL[:, 345:346]
        CK = ar(19456, KC, T)
        CVT = ar(21504, NT, D)
        CLOW = ar(23552, 2, T)
        CTM = ar(24064, 2, T)
        CQ = ar(0, KC, T)
        CSC = ar(2048, 4, 512)
        CPT = ar(4096, 4, 512)
        CNM, CSUM, CREC = (ar(6144 + 8 * k, 8) for k in range(3))

        def sems(names):
            return [ctx.enter_context(nc.semaphore(n)) for n in names.split()]

        unit_used, half_used, hi_ready, lo_ready = \
            sems("unit_used half_used hi_ready lo_ready")
        const_in, table_in, rows_zero, rows_in, first_in, x_in, mem_in, small_in, gain_in, pos_in = \
            sems("const_in table_in rows_zero rows_in first_in x_in mem_in small_in gain_in pos_in")
        out_done, = sems("out_done")
        vec_tp, vec_ready, ss, rms, xn, tp, xt_hi = \
            sems("vec_tp vec_ready ss rms xn tp xt_hi")
        xt_ready, x_upd = \
            sems("xt_ready x_upd")
        g_low, g_sum, silu, u_low, u_sum, h_val, h_hi, h_ready = \
            sems("g_low g_sum silu u_low u_sum h_val h_hi h_ready")
        r_low, r_sum, r_hi, r_ready = \
            sems("r_low r_sum r_hi r_ready")
        w_zero, w_low, w_sum, w_mix, lora_act, lora_mm, sw_done, sa_done = \
            sems("w_zero w_low w_sum w_mix lora_act lora_mm sw_done sa_done")
        sg_done, sq_ready, ssq_mm, nrm_done, ec_ready, dec_done, kk_ready, bp_ready = \
            sems("sg_done sq_ready ssq_mm nrm_done ec_ready dec_done kk_ready bp_ready")
        bp_mm, bon_done, tok_mm, tok_ev, nrm_inv, nrm_mm, omk_ready, ec_base, k2_ready, scaled = \
            sems("bp_mm bon_done tok_mm tok_ev nrm_inv nrm_mm omk_ready ec_base k2_ready scaled")
        m_mm, m_ev, levmask, t_mm, t_ev, inv_mm, inv_ev, s_r_mm = \
            sems("m_mm m_ev levmask t_mm t_ev inv_mm inv_ev s_r_mm")
        s_r_ev, s_u_mm, s_u_ev, s_y_mm, s_y_ev, s_s_mm, s_s_ev = \
            sems("s_r_ev s_u_mm s_u_ev s_y_mm s_y_ev s_s_mm s_s_ev")
        mean_mm, gd_ready, var_mm, gn_inv, gn_mm, gn_scaled, gn_std, y_val, y_hi, yt_ready = \
            sems("mean_mm gd_ready var_mm gn_inv gn_mm gn_scaled gn_std y_val y_hi yt_ready")
        pooled, pool_mm, pool_hi, mid_upd = \
            sems("pooled pool_mm pool_hi mid_upd")
        rope_arg, rope_tab, lam_arg, lam_exp, q_low, q_sum, rope_mm, rope_done = \
            sems("rope_arg rope_tab lam_arg lam_exp q_low q_sum rope_mm rope_done")
        vt_mm, vt_ev, sc_mm, sc_sum, sc_max, sc_exp, p_ready, pt_mm = \
            sems("vt_mm vt_ev sc_mm sc_sum sc_max sc_exp p_ready pt_mm")
        pt_ev, pv_mm, o_hi, od_ss, od_ms, od_std, od_norm, odt_mm = \
            sems("pt_ev pv_mm o_hi od_ss od_ms od_std od_norm odt_mm")
        c_low, c_sum, ct_mm, ct_ev = \
            sems("c_low c_sum ct_mm ct_ev")
        own_dve, = sems("own_dve")
        raw_full = [ctx.enter_context(nc.semaphore(f"raw_full{i}")) for i in range(RAW)]
        block = ctx.enter_context(nc.Block())


        def bc(ap, n):
            return ap.rearrange("p (a b) -> p a b", a=1).broadcast_to([P, n, ap.shape[-1]])

        class Count:
            def __init__(self):
                self.n = 0

            def next(self):
                self.n += 1
                return 1

        RMS_NORMS = (0, 1, 2, 4)
        NTP = {"ffn1": 0, "mix": 1, "ffn2": 2, "mem": 3, "mix2": 4, "cross": 5, "mlp": 6}
        JOBS = [("swa", 1, [0, 2]), ("swa", 1, [4, 6]), ("swa", 1, [1, 3]), ("swa", 1, [5, 7]),
                ("swa", 0, [0, 2, 4, 6]), ("swa", 0, [1, 3, 5, 7]),
                ("diff", 1, [0, 2]), ("diff", 1, [1, 3]), ("diff", 1, [4, 6]), ("diff", 1, [5, 7]),
                ("diff", 0, [0, 2, 4, 6]), ("diff", 0, [1, 3, 5, 7])]
        BLOCKS = [[(j, m, kb) for m in range(2) for kb in range(2)] for j in range(4)] + \
                 [[(j, m, 0) for m in range(4)] for j in (4, 5)] + \
                 [[(j, m, kb) for m in range(2) for kb in range(2)] for j in (6, 8)] + \
                 [[(10, m, 0) for m in range(4)]]
        W_BANKS, Q_BANKS, C_BANKS = (4, 5, 2, 3), (4, 5, 0, 1), (4, 5, 6, 7)
        BLOCK_AT = {b: (g, i) for g, bs in enumerate(BLOCKS) for i, b in enumerate(bs)}

        @block.sync
        def _(sp):
            def load(n, dn, src):
                if n >= RAW:
                    sp.wait_ge(lo_ready, n - RAW + 1 + dn)
                dst = raw[:, n % RAW, :]
                if len(src.shape) == 3:
                    dst = dst.rearrange("p (c n) -> p c n", c=src.shape[1])
                sp.dma_start(dst, src).then_inc(raw_full[n % RAW], 16)

            def cols(name, lo=None):
                v = t[name][0].rearrange("(c p) n -> p c n", p=P)
                return v[:, :, lo:lo + P] if lo is not None else v

            def rows(name):
                return t[name][0].rearrange("(j p) n -> p j n", p=P)

            for tt in range(NT):
                sp.dma_start(X[:, tt, :], t["x"][0, tt * P:(tt + 1) * P, :]).then_inc(x_in, 16)
            sp.dma_start(CON[:, 0:N_FIRST], t["consts"][:, 0:N_FIRST]).then_inc(const_in, 16)
            sp.dma_start(FIRST, t["ffn1_norm"][0].rearrange("(a b) -> a b", b=P)).then_inc(first_in, 16)
            for n in range(RAW):
                load(n, 0, cols(("ffn1_w_gate", "ffn1_w_up")[n % 2], (n // 2) * P))
            sp.wait_ge(rows_zero, 1)
            for name in ("mix_norm", "ffn2_norm", "g_mix_2", "g_cross_2", "g_mem_2", "g_mlp_2",
                         "w0", "a0", "k_k", "k_a", "ln_w", "ln_b", "pool_scale", "g_diff_2"):
                r = VEC_ROWS[name] - KC
                n = t[name].shape[1] // P
                sp.dma_start(ROWS[r:r + n, :], t[name][0].rearrange("(a b) -> a b", b=P)).then_inc(rows_in, 16)
            r = VEC_ROWS["r_k"] - KC
            sp.dma_start(ROWS[r:r + 4, :], t["r_k"][0].rearrange("(a h) d -> a (h d)", h=2)).then_inc(rows_in,
                16)
            r = VEC_ROWS["mu_shift"] - KC
            sp.dma_start(ROWS[r:r + 13, :], t["mu_shift"][0, 0:13 * P].rearrange("(a b) -> a b",
                b=P)).then_inc(rows_in, 16)
            sp.dma_start(ROWS[r + 13:r + 14, 0:32], t["mu_shift"][:, 13 * P:POOL]).then_inc(rows_in, 16)
            sp.dma_start(CON[:, N_FIRST:], t["consts"][:, N_FIRST:]).then_inc(table_in, 16)
            sp.dma_start(LWA[0:32, 0, :], t["w_lora_up"][0]).then_inc(small_in, 16)
            sp.dma_start(LWA[32:64, 1, :], t["a_lora_up"][0]).then_inc(small_in, 16)
            sp.dma_start(LWG[64:128, :], t["g_lora_up"][0, 0:64, :]).then_inc(small_in, 16)
            sp.dma_start(LWG[0:32, :], t["g_lora_up"][0, 64:96, :]).then_inc(small_in, 16)
            sp.dma_start(WPL[:, :, :], t["w_pool"][0].rearrange("g c d -> c g d")).then_inc(small_in, 16)

            def load_ffn(b, pre, first):
                g, u, d = pre + "_w_gate", pre + "_w_up", pre + "_w_down"
                for n, src in ((0, cols(g, 0)), (1, cols(u, 0)), (2, cols(g, P))):
                    if not first:
                        load(b + n, 0, src)
                with sp.Fori(0, 10) as i:
                    for k in range(2):
                        for m in range(3):
                            q = 3 * k + m
                            if m == 0:
                                src = cols(u)[:, :, bass.ds(i * (2 * P) + (k + 1) * P, P)]
                            elif m == 1:
                                src = rows(d)[:, bass.ds(i * 2 + k, 1), :]
                            else:
                                src = cols(g)[:, :, bass.ds(i * (2 * P) + (k + 2) * P, P)]
                            load(b + 3 + q, i * 6, src)
                load(b + 63, 0, cols(u, 21 * P))
                load(b + 64, 0, rows(d)[:, 20:21, :])
                load(b + 65, 0, rows(d)[:, 21:22, :])

            load_ffn(B_FFN1, "ffn1", True)
            for i, c in enumerate(WIN_COLS):
                load(B_WIN + i, 0, cols("w_in", c))
            for i, c in enumerate((4, 5, 6, 7, 0, 1, 2, 3)):
                load(B_WOUT + i, 0, rows("w_out")[:, c:c + 1, :])
            load_ffn(B_FFN2, "ffn2", False)
            sp.wait_ge(x_upd, 4 * 2)
            sp.dma_start(GFIN, t["final_norm"].rearrange("(a n) -> a n", a=1).broadcast_to([P,
                D])).then_inc(gain_in, 16)
            sp.dma_start(MEMX, t["mem_2"][0].rearrange("(a p) n -> p a n", p=P)).then_inc(mem_in, 16)
            sp.dma_start(POSI.bitcast(I32), t["positions_2"].broadcast_to([P, T])).then_inc(pos_in, 16)
            for k, name in enumerate(("lambda_q1_2", "lambda_k1_2", "lambda_q2_2", "lambda_k2_2")):
                sp.dma_start(LAMV[:, k, :], t[name].broadcast_to([P, 64])).then_inc(pos_in, 16)
            sp.dma_start(SNK, t["sinks_2"].broadcast_to([P, 8])).then_inc(pos_in, 16)
            for i in range(N_CKV):
                load(B_CKV + i, 0, cols("w_ckv_2", i * P))
            for i in range(N_WIN2):
                load(B_WIN2 + i, 0, cols("w_in_2", i * P))
            for c in range(KC):
                load(B_WOUT2 + c, 0, rows("w_out_2")[:, c:c + 1, :])
            for i in range(KC):
                load(B_CQ + i, 0, cols("w_cq_2", i * P))
            for c in range(KC):
                load(B_CO + c, 0, rows("w_co_2")[:, c:c + 1, :])
            load(B_MLP, 0, cols("w_up_2", 0))
            up, down = cols("w_up_2"), rows("w_down_2")
            with sp.Fori(0, 10) as i:
                for k in range(3):
                    load(B_MLP + 1 + 2 * k, i * 6, up[:, :, bass.ds(i * (3 * P) + (k + 1) * P, P)])
                    load(B_MLP + 2 + 2 * k, i * 6, down[:, bass.ds(i * 3 + k, 1), :])
            load(B_MLP + 61, 0, cols("w_up_2", 31 * P))
            load(B_MLP + 62, 0, down[:, 30:31, :])
            load(B_MLP + 63, 0, down[:, 31:32, :])
            sp.wait_ge(x_upd, 4 * 5)
            sp.dma_start(GFIN, t["g_final_2"].rearrange("(a n) -> a n", a=1).broadcast_to([P,
                D])).then_inc(gain_in, 16)
            sp.wait_ge(x_upd, 4 * 8)
            sp.dma_start(out[0].rearrange("(a p) n -> p a n", p=P), X[:, :, :]).then_inc(out_done, 16)
            sp.wait_ge(out_done, 16)

        @block.tensor
        def _(pe):
            def mm(o, st, mv, start=True, stop=True):
                return pe.matmul(o, st, mv, start=start, stop=stop, skip_group_check=True)

            def a_unit(n, dn, bank, after=None):
                pe.wait_ge(lo_ready, n + 1 + dn)
                s = n % RING
                for c in range(KC):
                    if after and c % 2 == 0:
                        pe.wait_ge(xt_ready, 4 * NTP[after] + c // 2 + 1)
                    cs = slice(c * P, (c + 1) * P)
                    mm(bank[:, :], whi[:, s, cs], XT[:, c, :], start=(c == 0), stop=(c == KC - 1))
                    last = mm(bank[:, 0:T], wlo[:, s, cs], XT[:, c, 0:T], start=False, stop=(c == KC - 1))
                last.then_inc(unit_used, 1)

            def b_half(n, dn, act, tt, start=False, stop=False):
                pe.wait_ge(lo_ready, n + 1 + dn)
                s = n % RING
                hi = act[:, tt * P:(tt + 1) * P]
                lo = act[:, T + tt * P:T + (tt + 1) * P]
                for st, wt, a, z in ((hi, whi, start, False), (hi, wlo, False, False), (lo, whi, False, stop)):
                    for h in range(2):
                        last = mm(PS[2 * tt + h][:, :], st, wt[:, s, 512 * h:512 * h + 512], start=a, stop=z)
                if tt == NT - 1:
                    last.then_inc(unit_used, 1)
                return last

            def b_unit(n, dn, act, start=False, stop=False):
                for tt in range(NT):
                    last = b_half(n, dn, act, tt, start, stop)
                    if stop and tt == 0:
                        last.then_inc(half_used, 1)

            def norm_t(name):
                q = NTP[name]
                src = MEMX if name == "mem" else X
                for tt in range(NT):
                    pe.wait_ge(xn, 2 * q + tt + 1)
                    for b in range(4):
                        for c in (2 * b, 2 * b + 1):
                            last = mm(PS[4 + b][:, (c % 2) * T + tt * P:(c % 2) * T + (tt + 1) * P],
                                      src[:, tt, c * P:(c + 1) * P], DIAG[:, tt, :])
                        if tt == NT - 1:
                            last.then_inc(tp, 1)

            def ffn(b, f):
                J = FC * f

                def gate_up(j, n, dn=0, dj=0, after=None):
                    if J + j >= 2:
                        pe.wait_ge(h_ready, J + j - 1 + dj)
                    a_unit(b + n, dn, PS[4 + j % 2], after)
                    a_unit(b + n + 1, dn, PS[6 + j % 2])

                def down(j, n, dn=0, dj=0, **k):
                    pe.wait_ge(h_ready, J + j + 1 + dj)
                    b_unit(b + n, dn, H[:, j % 2, :], **k)

                gate_up(0, 0, after=("ffn1", "ffn2")[f])
                gate_up(1, 2)
                down(0, 4, start=True)
                with pe.Fori(0, 10) as i:
                    for k in range(2):
                        gate_up(2 + k, 5 + 3 * k, i * 6, i * 2)
                        down(1 + k, 7 + 3 * k, i * 6, i * 2)
                if f == 0:
                    pe.wait_ge(table_in, 16)
                    pe.wait_ge(rows_in, 16 * 17)
                    pe.wait_ge(h_ready, FC)
                    pe.transpose(PS[7][:, KC:N_VEC], ROWS[0:N_VEC - KC, :],
                                 ident[0:N_VEC - KC, 0:N_VEC - KC]).then_inc(vec_tp, 1)
                down(21, 65, stop=True)

            def mix():
                def lora(f):
                    fs = slice(f * P, (f + 1) * P)
                    pe.wait_ge(lora_act, 4)
                    if f >= 2:
                        pe.wait_ge(sa_done, f - 1)
                        pe.wait_ge(sg_done, f - 1)
                    wa, gate = PS[6 - 6 * (f % 2)], PS[7 - 6 * (f % 2)]
                    mm(wa[:, 0:T], LWA[:, 0, fs], LW[0:64, :])
                    mm(wa[:, T:2 * T], LWA[:, 1, fs], LW[0:64, :]).then_inc(lora_mm, 1)
                    mm(gate[:, 0:T], LWG[:, fs], LG[:, :]).then_inc(lora_mm, 1)

                def row_sums(bank, src, tiles, ready, n):
                    pe.wait_ge(ready, n)
                    for k, f in enumerate(tiles):
                        last = mm(bank[0:8, 0:T], heads(f), src[:, f, :], start=(k == 0), stop=(k == len(tiles) - 1))
                    return last

                def head_sums(src, ready, done):
                    pe.wait_ge(ready, NF)
                    for k in range(2):
                        mm(PS[6 + k][:, :], con("blk"), src[:, 2 * k:2 * k + 2, :]).then_inc(done, 1)

                pe.wait_ge(small_in, 16 * 5)
                pe.wait_ge(w_zero, 6)
                for i in range(N_WIN):
                    if i >= 4:
                        pe.wait_ge(w_sum, i - 3)
                    a_unit(B_WIN + i, 0, PS[W_BANKS[i % 4]], None if i else "mix")
                    if 3 <= i < 3 + NF:
                        lora(i - 3)
                    if i == 11:
                        pe.wait_ge(sa_done, NF - 1)
                        row_sums(PS[6], SQ, range(NF), sq_ready, NF).then_inc(ssq_mm, 1)
                    if i == 14:
                        pe.wait_ge(sg_done, NF)
                        pe.wait_ge(nrm_inv, 1)
                        for f in range(NF):
                            mm(PS[f // 2][:, (f % 2) * T:(f % 2 + 1) * T], spread(f), MXR).then_inc(nrm_mm, 1)
                        head_sums(DP, bp_ready, bp_mm)
                pe.wait_ge(w_sum, N_WIN)
                pe.wait_ge(w_mix, 14)
                for c in range(NT):
                    for f in range(NF):
                        last = pe.transpose(PS[2 + c][:, f * P:(f + 1) * P], PV[:, f, c * P:(c + 1) * P], ident)
                    last.then_inc(tok_mm, 1)
                pe.wait_ge(kk_ready, 1)
                pe.wait_ge(scaled, 2)
                for k, src in enumerate((AA, K2)):
                    for f in range(NF):
                        last = pe.transpose(PS[k][:, f * P:(f + 1) * P], src[:, f, 0:P], ident)
                    last.then_inc(tok_mm, 1)
                pe.wait_ge(bon_done, 1)
                fill = 0

                def fill_in():
                    nonlocal fill
                    n, tt = fill // 2, fill % 2
                    pe.wait_ge(yt_ready, n + 1)
                    b_half(B_WOUT + n, 0, XT[:, 4 + n, :], tt, start=(n % 2 == 0), stop=(n == 1))
                    fill += 1

                for wv in range(2):
                    if wv:
                        pe.wait_ge(s_y_ev, 1)
                        pe.wait_ge(s_s_ev, 1)
                        pe.wait_ge(s_u_ev, 2)
                    for g in range(2):
                        f = 2 * wv + g
                        for r, terms in enumerate((((AA, KK), (K2, KK)), ((KK, AA),), ((AA, PR), (K2, PR)))):
                            for h in range(2):
                                q = g * 6 + 2 * r + h
                                if q >= 8:
                                    pe.wait_ge(m_ev, 12 * wv + q - 7)
                                elif q == 4 and wv:
                                    pe.wait_ge(mid_upd, 4)
                                elif q == 4:
                                    pe.wait_ge(tok_ev, 4)
                                hp = slice(64 * h, 64 * h + 64)
                                for k, (a, b) in enumerate(terms):
                                    for c in range(NT):
                                        m = 2 * k + c
                                        last = mm(PS[(q + 4) % 8][:, m * P:(m + 1) * P], a[hp, f, c * P:(c + 1) * P],
                                                  b[hp, f, c * P:(c + 1) * P])
                                last.then_inc(m_mm, 1)
                    pe.wait_ge(m_ev, 12 * wv + 12)
                    for k in range(1, 7):
                        for g in range(2):
                            n = wv * 12 + (k - 1) * 2 + g
                            pe.wait_ge(inv_ev, wv * 14 + (k - 1) * 2 + g + 1)
                            pe.wait_ge(levmask, n + 1)
                            M = mats[g]
                            for m in range(4):
                                last = mm(PS[3 * g][:, m * P:(m + 1) * P], M["LEV"][:, m, :], M["XM"][:, m, :])
                            last.then_inc(t_mm, 1)
                        for g in range(2):
                            n = wv * 12 + (k - 1) * 2 + g
                            pe.wait_ge(t_ev, n + 1)
                            M = mats[g]
                            if k < 6:
                                for m in range(4):
                                    mm(PS[3 * g + 1][:, m * P:(m + 1) * P], M["XMT"][:, m, :], M["TS"][:, m, :])
                            for m in range(4):
                                last = mm(PS[3 * g + 2][:, m * P:(m + 1) * P], M["TS"][:, m, :], M["XMT"][:, m, :])
                            last.then_inc(inv_mm, 1)
                        if wv == 0 and k >= 5:
                            for g in (2 * k - 10, 2 * k - 9):
                                pe.wait_ge(pooled, g + 1)
                                last = mm(PS[k + 1][:, (g % 2) * T:(g % 2 + 1) * T], WPL[:, g, :], window(g, PAD))
                            last.then_inc(pool_mm, 1)
                        if wv and k == 1:
                            mm(PS[6][:, :], con("blk"), YO[:, 0:2, :]).then_inc(mean_mm, 1)
                        if wv and k == 3:
                            row_sums(PS[6], GV, (0, 1), gd_ready, 1).then_inc(var_mm, 1)
                        if wv and k == 5:
                            pe.wait_ge(gn_inv, 1)
                            for f in (0, 1):
                                last = mm(PS[7][:, f * T:(f + 1) * T], spread(f), GVR)
                            last.then_inc(gn_mm, 1)
                    pe.wait_ge(inv_ev, wv * 14 + 14)
                    if wv:
                        pe.wait_ge(gn_std, 1)
                        pe.wait_ge(gn_scaled, 1)
                    else:
                        pe.wait_ge(yt_ready, 4)
                    pairs = [(g, hh) for g in range(2) for hh in range(2)]
                    for c in range(NT):
                        n = 2 * wv + c

                        def at(g, hh):
                            return 2 * wv + g, slice(64 * hh, 64 * hh + 64), slice(64 * (2 * hh + g), 64 * (2 * hh + g) + 64)

                        def vt(g, hh):
                            f = 2 * wv + g
                            return VTOK[:, c, f * P + 64 * hh:f * P + 64 * hh + 64]

                        if c:
                            pe.wait_ge(s_s_ev, wv + 1)
                        for hh in range(2):
                            for g in range(2):
                                f, hp, hc = at(g, hh)
                                o = PS[5 + hh][:, g * 64:g * 64 + 64]
                                if c:
                                    mm(o, KK[hp, f, P:2 * P], ST[hp, f, :], stop=False)
                                last = mm(o, mats[g]["LT"][:, hh, 2 + c, :], vt(g, hh), start=(c == 0))
                        last.then_inc(s_r_mm, 1)
                        fill_in()
                        pe.wait_ge(s_r_ev, n + 1)
                        for g, hh in pairs:
                            f, hp, hc = at(g, hh)
                            last = mm(PS[7][:, hc], mats[g]["XMT"][:, 2 * hh + c, :], RB[:, 2 * c, hc])
                        last.then_inc(s_u_mm, 1)
                        fill_in()
                        pe.wait_ge(s_u_ev, n + 1)
                        if c == 0:
                            for g, hh in pairs:
                                f, hp, hc = at(g, hh)
                                fc = slice(f * P + 64 * hh, f * P + 64 * hh + 64)
                                o = PS[7][hp, T + g * 64:T + g * 64 + 64]
                                mm(o, BTOK[:, fc], RB[:, 1, hc], stop=False)
                                last = mm(o, KTOK[:, fc], vt(g, hh), start=False)
                            last.then_inc(s_s_mm, 1)
                        for g, hh in pairs:
                            f, hp, hc = at(g, hh)
                            o = PS[4][hp, g * T + c * P:g * T + (c + 1) * P]
                            if c:
                                mm(o, ST[hp, f, :], PR[hp, f, P:2 * P], stop=False)
                            mm(o, RB[:, 2 * c + 1, hc], mats[g]["MM"][:, hh, c, :], start=(c == 0), stop=False)
                            last = mm(o, vt(g, hh), mats[g]["MM"][:, hh, 2 + c, :], start=False)
                        if c:
                            last.then_inc(s_y_mm, 1)
                pe.wait_ge(s_y_ev, 2)
                mm(PS[6][:, :], con("blk"), YO[:, 2:4, :]).then_inc(mean_mm, 1)
                for c in range(NF):
                    pe.wait_ge(yt_ready, 4 + c + 1)
                    b_unit(B_WOUT + 4 + c, 0, XT[:, c, :], stop=(c == NF - 1))
                    if c == 0:
                        row_sums(PS[6], GV, (2, 3), gd_ready, 2).then_inc(var_mm, 1)
                    if c == 1:
                        pe.wait_ge(gn_inv, 2)
                        for f in (2, 3):
                            last = mm(PS[7][:, (f - 2) * T:(f - 1) * T], spread(f), GVR)
                        last.then_inc(gn_mm, 1)

            def attention():
                norm_t("mem")

                def turn_value(i):
                    pe.wait_ge(c_sum, i + 1)
                    k = i - KC
                    if k >= 2:
                        pe.wait_ge(ct_ev, k - 1)
                    for tt in range(NT):
                        last = pe.transpose(PS[6 + i % 2][:, tt * P:(tt + 1) * P], CTM[:, i % 2, tt * P:(tt + 1) * P],
                                            ident)
                    last.then_inc(ct_mm, 1)

                for i in range(N_CKV):
                    if i == 2:
                        pe.wait_ge(x_upd, 4 * 3)
                    if i >= 4:
                        pe.wait_ge(c_sum, i - 3)
                    a_unit(B_CKV + i, 0, PS[Q_BANKS[i % 4]], None if i else "mem")
                    if i - 1 >= KC:
                        turn_value(i - 1)
                turn_value(N_CKV - 1)
                pe.wait_ge(ct_ev, KC)
                norm_t("mix2")

                n_rope = n_vt = 0
                for i in range(N_WIN2 + 1):
                    if i < N_WIN2:
                        if i >= 4:
                            pe.wait_ge(q_sum, i - 3)
                        a_unit(B_WIN2 + i, 0, PS[Q_BANKS[i % 4]], None if i else "mix2")
                    k = i - 1
                    if k < 0:
                        continue
                    pe.wait_ge(q_sum, k + 1)
                    if k == 5 or k >= 14:
                        if n_vt >= 2:
                            pe.wait_ge(vt_ev, n_vt - 1)
                        for tt in range(NT):
                            last = pe.transpose(PS[7 - 4 * (n_vt % 2)][:, tt * P:(tt + 1) * P], QKV[:, k, tt * P:(tt + 1) * P], ident)
                        last.then_inc(vt_mm, 1)
                        n_vt += 1
                    else:
                        if n_rope >= 2:
                            pe.wait_ge(rope_done, n_rope - 1)
                        mm(PS[6 - 4 * (n_rope % 2)][:, 0:T], con("swap32"), QKV[:, k, :]).then_inc(rope_mm, 1)
                        n_rope += 1
                pe.wait_ge(rope_done, n_rope)
                mm(PS[6][:, 0:T], con("swap64"), QKV[:, 4, :]).then_inc(rope_mm, 1)
                pe.wait_ge(rope_done, n_rope + 1)
                pe.wait_ge(vt_ev, 5)
                for j, (kind, n, maps) in enumerate(JOBS):
                    if j >= 4:
                        pe.wait_ge(sc_sum, j - 3)
                    nk = (n + 1) * P
                    for m, h in enumerate(maps):
                        hp = slice(64 * (h % 2), 64 * (h % 2) + 64)
                        if kind == "swa":
                            q, kt = QKV[hp, h // 2, n * P:(n + 1) * P], (QKV[hp, 4, 0:nk] if h // 4 == h % 2 else KSW[hp, 0:nk])
                        else:
                            q, kt = QKV[hp, 6 + h // 2, n * P:(n + 1) * P], QKV[hp, 10 + h // 2, 0:nk]
                        last = mm(PS[j % 4][:, m * nk:(m + 1) * nk], q, kt)
                    last.then_inc(sc_mm, 1)
                pe.wait_ge(vt_ev, 5)
                for g, bs in enumerate(BLOCKS):
                    pe.wait_ge(p_ready, g + 1)
                    if g >= 4:
                        pe.wait_ge(pt_ev, g - 3)
                    for i, (j, m, kb) in enumerate(bs):
                        nk = (JOBS[j][1] + 1) * P
                        last = pe.transpose(PS[4 + g % 4][:, i * P:(i + 1) * P],
                                            SC[:, j, m * nk + kb * P:m * nk + (kb + 1) * P], ident)
                    last.then_inc(pt_mm, 1)

                def pt(j, m, kb):
                    g, i = BLOCK_AT[(j, m, kb)]
                    return PTS[:, g, i * P:(i + 1) * P]

                pe.wait_ge(sc_sum, 12)
                pe.wait_ge(pt_ev, 9)
                for h in range(8):
                    hp = slice(64 * (h % 2), 64 * (h % 2) + 64)
                    c, kv = h // 2, slice(64 * (h // 4), 64 * (h // 4) + 64)
                    o = PS[c // 2][hp, (c % 2) * T:(c % 2 + 1) * T]
                    j, m = 2 * (h % 2) + h // 4, (h // 2) % 2
                    mm(o[:, 0:P], VT2[:, 0, kv], pt(4 + h % 2, h // 2, 0))
                    mm(o[:, P:T], VT2[:, 0, kv], pt(j, m, 0), stop=False)
                    last = mm(o[:, P:T], VT2[:, 1, kv], pt(j, m, 1), start=False)
                    if h % 4 == 3:
                        last.then_inc(pv_mm, 1)
                for n in range(NT):
                    for h in range(4):
                        o = PS[2 + n][:, h * P:(h + 1) * P]
                        vs = slice(P + h * P, P + (h + 1) * P)
                        if n == 0:
                            last = mm(o, pt(10, h, 0), VT2[:, 0, vs])
                        else:
                            mm(o, pt(6 + 2 * (h // 2), h % 2, 0), VT2[:, 0, vs], stop=False)
                            last = mm(o, pt(6 + 2 * (h // 2), h % 2, 1), VT2[:, 1, vs], start=False)
                    last.then_inc(pv_mm, 1)
                for n in range(NT):
                    pe.wait_ge(od_norm, n + 1)
                for b in range(2):
                    for h in (2 * b, 2 * b + 1):
                        for n in range(NT):
                            last = pe.transpose(PS[4 + b][:, (h % 2) * T + n * P:(h % 2) * T + (n + 1) * P],
                                                ODN[:, n, h * P:(h + 1) * P], ident)
                    last.then_inc(odt_mm, 1)
                for c in range(KC):
                    pe.wait_ge(yt_ready, KC + max(4, c + 1))
                    b_unit(B_WOUT2 + c, 0, XT[:, c, :], start=(c == 0), stop=(c == KC - 1))

            def cross():
                norm_t("cross")
                for i in range(KC):
                    if i >= 4:
                        pe.wait_ge(c_sum, N_CKV + i - 3)
                    a_unit(B_CQ + i, 0, PS[C_BANKS[i % 4]], None if i else "cross")
                pe.wait_ge(x_upd, 4 * 5)
                for j in range(4):
                    n = j // 2
                    for m in range(2):
                        h = 2 * (j % 2) + m
                        pe.wait_ge(c_sum, N_CKV + 2 * h + 2)
                        for k in range(2):
                            last = mm(PS[j][:, m * T:(m + 1) * T], CQ[:, 2 * h + k, n * P:(n + 1) * P],
                                      CK[:, 2 * h + k, :], start=(k == 0), stop=(k == 1))
                    last.then_inc(sc_mm, 1)
                pe.wait_ge(c_sum, N_CKV + KC)
                for h in range(4):
                    pe.wait_ge(p_ready, 9 + 3 + h // 2)
                    for kb in range(2):
                        for n in range(NT):
                            last = pe.transpose(PS[4 + h][:, kb * T + n * P:kb * T + (n + 1) * P],
                                                CSC[:, 2 * n + h // 2, (h % 2) * T + kb * P:(h % 2) * T + (kb + 1) * P],
                                                ident)
                    last.then_inc(pt_mm, 1)
                pe.wait_ge(sc_sum, 12 + 4)
                for h in range(4):
                    pe.wait_ge(pt_ev, 9 + h + 1)
                    for d in range(2):
                        for kb in range(2):
                            last = mm(PS[h][:, d * T:(d + 1) * T], CVT[:, kb, h * 2 * P + d * P:h * 2 * P + (d + 1) * P],
                                      CPT[:, h, kb * T:(kb + 1) * T], start=(kb == 0), stop=(kb == 1))
                    last.then_inc(pv_mm, 1)
                pe.wait_ge(yt_ready, 2 * KC + KC)
                for c in range(KC):
                    b_unit(B_CO + c, 0, XT[:, c, :], start=(c == 0), stop=(c == KC - 1))

            def mlp():
                def up(j, n, dn=0, dj=0, after=None):
                    if j >= 3:
                        pe.wait_ge(r_ready, j - 2 + dj)
                    a_unit(B_MLP + n, dn, PS[4 + j % 3], after)

                def down(j, n, dn=0, dj=0, **k):
                    pe.wait_ge(r_ready, j + 1 + dj)
                    b_unit(B_MLP + n, dn, H[:, j % 3, :], **k)

                up(0, 0, after="mlp")
                up(1, 1)
                down(0, 2, start=True)
                up(2, 3)
                down(1, 4)
                up(3, 5)
                down(2, 6)
                with pe.Fori(0, 9) as i:
                    for k in range(3):
                        up(4 + k, 7 + 2 * k, i * 6, i * 3)
                        down(3 + k, 8 + 2 * k, i * 6, i * 3)
                up(31, 61)
                down(30, 62)
                down(31, 63, stop=True)

            pe.wait_ge(const_in, 16)
            pe.wait_ge(first_in, 16)
            pe.transpose(PS[7][:, 0:KC], FIRST, ident[0:KC, 0:KC]).then_inc(vec_tp, 1)
            pe.wait_ge(vec_ready, 1)
            norm_t("ffn1")
            ffn(B_FFN1, 0)
            pe.wait_ge(vec_ready, 2)
            norm_t("mix")
            pe.wait_ge(x_upd, 4 * 1)
            mix()
            norm_t("ffn2")
            pe.wait_ge(x_upd, 4 * 2)
            ffn(B_FFN2, 1)
            attention()
            cross()
            norm_t("mlp")
            pe.wait_ge(x_upd, 4 * 6)
            mlp()

        @block.scalar
        def _(act):
            def split_hi(n, i=None):
                c = 16 * (n // RAW + 1)
                act.wait_ge(raw_full[n % RAW], c if i is None else i * (16 * RING // RAW) + c)
                if n >= RING:
                    act.wait_ge(unit_used, n - RING + 1 if i is None else i * RING + (n - RING + 1))
                act.activation(whi[:, n % RING, :], raw[:, n % RAW, :], ACT.Copy).then_inc(hi_ready, 1)

            splits = Count()

            def split_to(n):
                while splits.n < min(n, N_UNITS):
                    split_hi(splits.n)
                    splits.next()

            def norm_sums(q, src, upd):
                if q:
                    act.activation(SMALL[:, 346 + q:347 + q], con("eps"), ACT.Sqrt)
                for tt in range(NT):
                    if upd:
                        act.wait_ge(x_upd, 4 * (upd - 1) + 2 * tt + 2)
                    if q + tt:
                        act.wait_ge(ss, 2 * q + tt)
                    act.activation(SQJ, src[:, tt, :], ACT.Square, accum_out=SS[:, tt:tt + 1]).then_inc(ss, 1)
                    act.wait_ge(ss, 2 * q + tt + 1)
                    act.activation(MS[:, tt:tt + 1], SS[:, tt:tt + 1], ACT.Sqrt, scale=1.0 / D,
                                   bias=con("eps" if q in RMS_NORMS else "eps_block")).then_inc(rms, 1)

            def norm_hi(name, gain):
                q = NTP[name]
                for b in range(4):
                    act.wait_ge(tp, 4 * q + b + 1)
                    for c in (2 * b, 2 * b + 1):
                        ins = act.activation(XT[:, c, 0:T], PS[4 + b][:, (c % 2) * T:(c % 2 + 1) * T], ACT.Copy,
                            scale=vec(gain, c))
                        if c % 2:
                            ins.then_inc(xt_hi, 1)

            def ffn(b, f):
                J = FC * f

                def chunk(j, i=None):
                    dj, dn = (0, 0) if i is None else (i * 2, i * 6)
                    q = j % 2
                    n_gate, n_up = (0, 1) if j == 0 else (3 * j - 1, 3 * j)

                    def next_split(k):
                        n = b + 3 * j + 4 + k
                        if n < N_UNITS:
                            split_hi(n, i)
                            if i is None:
                                splits.n = n + 1

                    next_split(0)
                    act.wait_ge(unit_used, b + n_gate + 1 + dn)
                    if J + j >= 2:
                        act.wait_ge(g_sum, J + j - 1 + dj)
                    act.activation(GL[:, q, :], PS[4 + q][:, T:2 * T], ACT.Copy).then_inc(g_low, 1)
                    next_split(1)
                    act.wait_ge(unit_used, b + n_up + 1 + dn)
                    if J + j >= 2:
                        act.wait_ge(u_sum, J + j - 1 + dj)
                    act.activation(UL[:, q, :], PS[6 + q][:, T:2 * T], ACT.Copy).then_inc(u_low, 1)
                    next_split(2)
                    act.wait_ge(g_sum, J + j + 1 + dj)
                    if J + j >= 2:
                        act.wait_ge(h_val, J + j - 1 + dj)
                    act.activation(SG[:, q, :], GS[:, q, :], ACT.Silu).then_inc(silu, 1)
                    act.wait_ge(h_val, J + j + 1 + dj)
                    if j >= 2:
                        act.wait_ge(unit_used, b + 3 * (j - 2) + 4 + 1 + dn)
                    act.activation(H[:, q, 0:T], HS[:, q, :], ACT.Copy).then_inc(h_hi, 1)

                split_to(b + LEAD)
                chunk(0)
                chunk(1)
                with act.Fori(0, 9) as i:
                    for k in range(2):
                        chunk(2 + k, i)
                chunk(20)
                chunk(21)

            def low(i, n, bank, dst, sem_low, sem_sum, base=0):
                split_to(n + LEAD + 1)
                act.wait_ge(unit_used, n + 1)
                if base + i >= 2:
                    act.wait_ge(sem_sum, base + i - 1)
                act.activation(dst[:, i % 2, :], bank[:, T:2 * T], ACT.Copy).then_inc(sem_low, 1)

            def deviation(wv):
                act.wait_ge(var_mm, wv + 1)
                act.activation(GVR, PS[6][0:8, 0:T], ACT.Sqrt, scale=1.0 / 64,
                               bias=con("eps_group", 8)).then_inc(gn_std, 1)

            def y_upper(wv):
                for f in (2 * wv, 2 * wv + 1):
                    act.wait_ge(y_val, f + 1)
                    act.activation(XT[:, f, 0:T], YO[:, f, :], ACT.Copy).then_inc(y_hi, 1)

            def mix():
                for i in range(N_WIN):
                    low(i, B_WIN + i, PS[W_BANKS[i % 4]], WLOW, w_low, w_sum)
                    if i == 2:
                        act.wait_ge(w_mix, 2)
                        act.wait_ge(w_zero, 6)
                        act.activation(LW[0:32, :], LBUF[0:32, 0, :], ACT.Tanh).then_inc(lora_act, 1)
                        act.activation(LW[32:64, :], LBUF[32:64, 0, :], ACT.Copy).then_inc(lora_act, 1)
                        act.activation(LG[64:128, :], LBUF[64:128, 0, :], ACT.Sigmoid).then_inc(lora_act, 1)
                        act.activation(LG[0:32, :], LBUF[0:32, 1, :], ACT.Sigmoid).then_inc(lora_act, 1)
                    if 4 <= i < 4 + NF:
                        f = i - 4
                        wa, gate = PS[6 - 6 * (f % 2)], PS[7 - 6 * (f % 2)]
                        act.wait_ge(lora_mm, 2 * f + 1)
                        act.activation(SW[:, f, :], wa[:, 0:T], ACT.Sigmoid, bias=vec("w0",
                            f)).then_inc(sw_done, 1)
                        act.activation(AA[:, f, :], wa[:, T:2 * T], ACT.Sigmoid, bias=vec("a0",
                            f)).then_inc(sa_done, 1)
                        act.wait_ge(lora_mm, 2 * f + 2)
                        act.activation(GG[:, f, :], gate[:, 0:T], ACT.Copy).then_inc(sg_done, 1)
                    if i == 10:
                        act.wait_ge(w_mix, 10)
                        act.wait_ge(sa_done, NF)
                        act.wait_ge(omk_ready, 1)
                        for f in range(NF):
                            act.activation(SQ[:, f, :], PK[:, f, :], ACT.Square, scale=vec("k_k", f)).then_inc(sq_ready, 1)
                        for f in range(NF):
                            act.activation(EC[:, f, :], AA[:, f, :], ACT.Identity, scale=vec("k_a", f),
                                           bias=OMK[:, f:f + 1]).then_inc(ec_base, 1)
                        for f in range(NF):
                            act.activation(KK[:, f, :], PK[:, f, :], ACT.Copy, scale=vec("k_k", f)).then_inc(ec_base, 1)
                    if i == 12:
                        act.wait_ge(ssq_mm, 1)
                        act.activation(MXR, PS[6][0:8, 0:T], ACT.Sqrt).then_inc(nrm_done, 1)
                    if i == 13:
                        act.wait_ge(ec_ready, 2)
                        act.wait_ge(ssq_mm, 1)
                        act.activation(IP[:, :, :], CC[:, :, :], ACT.Exp, scale=-LN_DECAY).then_inc(dec_done, 1)
                        act.activation(EC[:, :, :], EC[:, :, :], ACT.Exp, scale=LN_DECAY).then_inc(dec_done, 1)
                        act.activation(CC[:, :, :], CC[:, :, :], ACT.Exp, scale=LN_DECAY).then_inc(dec_done, 1)
                        act.activation(FAC, FAC, ACT.Exp, scale=LN_DECAY).then_inc(dec_done, 1)
                act.wait_ge(kk_ready, 1)
                for b, dst in enumerate((VTOK[:, 0, :], VTOK[:, 1, :], BTOK, KTOK)):
                    act.wait_ge(tok_mm, b + 1)
                    act.activation(dst, PS[(b + 2) % 4][:, :], ACT.Copy).then_inc(tok_ev, 1)
                for wv in range(2):
                    for k in range(1, 7):
                        for g in range(2):
                            n = wv * 12 + (k - 1) * 2 + g
                            act.wait_ge(t_mm, n + 1)
                            if n >= 2:
                                act.wait_ge(inv_mm, n - 1)
                            act.activation(mats[g]["TS"][:, :, :], PS[3 * g][:, :].rearrange("p (a b) -> p a b",
                                a=4), ACT.Copy).then_inc(t_ev, 1)
                        if k == 1:
                            split_to(B_WOUT + 2 * wv + RING)
                        if wv and k == 4:
                            deviation(0)
                    if wv == 0:
                        for g in range(NF):
                            act.wait_ge(pool_mm, g // 2 + 1)
                            act.activation(XT[:, 4 + g, 0:T], PS[6 + g // 2][:, (g % 2) * T:(g % 2 + 1) * T], ACT.Copy,
                                           scale=vec("pool_scale", g)).then_inc(pool_hi, 1)
                    for c in range(NT):
                        n = 2 * wv + c
                        act.wait_ge(s_r_mm, n + 1)
                        act.activation(RB[:, 2 * c, 0:P], PS[5][:, 0:P], ACT.Copy)
                        act.activation(RB[:, 2 * c, P:2 * P], PS[6][:, 0:P], ACT.Copy).then_inc(s_r_ev, 1)
                        act.wait_ge(s_u_mm, n + 1)
                        act.activation(RB[:, 2 * c + 1, :], PS[7][:, 0:T], ACT.Copy).then_inc(s_u_ev, 1)
                        if wv and c == 0:
                            y_upper(0)
                    act.wait_ge(s_y_mm, wv + 1)
                    act.activation(YO[:, 2 * wv:2 * wv + 2, :], PS[4][:, :].rearrange("p (a b) -> p a b", a=2),
                        ACT.Copy).then_inc(s_y_ev, 1)
                deviation(1)
                y_upper(1)
                for c in range(KC):
                    split_to(B_WOUT + c + LEAD + 1)

            def attention():
                act.wait_ge(mem_in, 16)
                norm_sums(3, MEMX, 0)
                norm_hi("mem", "g_mem_2")
                norm_sums(4, X, 3)
                for i in range(N_CKV):
                    low(i, B_CKV + i, PS[Q_BANKS[i % 4]], CLOW, c_low, c_sum)
                    if i == 2:
                        norm_sums(5, X, 4)
                    if i - 2 >= KC:
                        value(i - 2)
                for i in (N_CKV - 2, N_CKV - 1):
                    value(i)
                norm_hi("mix2", "g_mix_2")
                n_vt = 0
                for i in range(N_WIN2 + 1):
                    if i < N_WIN2:
                        low(i, B_WIN2 + i, PS[Q_BANKS[i % 4]], CLOW, q_low, q_sum)
                    if i == 1:
                        act.wait_ge(rope_arg, 1)
                        act.activation(RC, RA[0], ACT.Sin).then_inc(rope_tab, 1)
                        act.activation(RSN, RA[1], ACT.Sin).then_inc(rope_tab, 1)
                        act.wait_ge(lam_arg, 1)
                        act.activation(LEXP, LDOT, ACT.Exp).then_inc(lam_exp, 1)
                    k = i - 1
                    if k == 5 or k >= 14:
                        act.wait_ge(vt_mm, n_vt + 1)
                        act.activation(VT2[:, :, n_vt * P:(n_vt + 1) * P], PS[7 - 4 * (n_vt % 2)][:,
                            0:T].rearrange("p (a b) -> p a b", a=NT), ACT.Copy).then_inc(vt_ev, 1)
                        n_vt += 1
                split_to(B_WOUT2 + RING)
                for j, (kind, n, maps) in enumerate(JOBS):
                    act.wait_ge(sc_max, j + 1)
                    nk = (n + 1) * P
                    for m in range(len(maps)):
                        e = SC[:, j, m * nk:(m + 1) * nk]
                        q = 4 * j + m
                        done = m == len(maps) - 1 and kind == "diff"
                        ins = act.activation(e, e, ACT.Exp, bias=NMX[:, q:q + 1], accum_out=SUM[:, q:q + 1])
                        if done:
                            ins.then_inc(sc_exp, 1)
                    if kind == "swa":
                        q = slice(4 * j, 4 * j + len(maps))
                        act.activation(ESK[:, q], ESK[:, q], ACT.Exp).then_inc(sc_exp, 1)
                for g in range(9):
                    act.wait_ge(pt_mm, g + 1)
                    act.activation(PTS[:, g, :], PS[4 + g % 4][:, :], ACT.Copy).then_inc(pt_ev, 1)
                for n in range(NT):
                    act.wait_ge(pv_mm, 3 + n)
                    for h in range(4):
                        ins = act.activation(ODJ[:, (4 * n + h) * P:(4 * n + h + 1) * P], PS[2 + n][:,
                            h * P:(h + 1) * P], ACT.Square, accum_out=ODS[:, 4 * n + h:4 * n + h + 1])
                        if h == 3:
                            ins.then_inc(od_ss, 1)
                act.wait_ge(od_ms, 1)
                act.activation(ODS, ODS, ACT.Sqrt).then_inc(od_std, 1)
                for c in range(4):
                    act.wait_ge(pv_mm, c // 2 + 1)
                    ins = act.activation(XT[:, c, 0:T], PS[c // 2][:, (c % 2) * T:(c % 2 + 1) * T], ACT.Copy)
                    if c % 2:
                        ins.then_inc(o_hi, 1)
                for h in range(4):
                    act.wait_ge(odt_mm, h // 2 + 1)
                    ins = act.activation(XT[:, 4 + h, 0:T], PS[4 + h // 2][:, (h % 2) * T:(h % 2 + 1) * T], ACT.Copy,
                        scale=GD8)
                    if h % 2:
                        ins.then_inc(o_hi, 1)
                for c in range(KC):
                    split_to(B_WOUT2 + c + LEAD + 1)

            def value(i):
                k = i - KC
                act.wait_ge(ct_mm, k + 1)
                act.activation(CVT[:, :, k * P:(k + 1) * P], PS[6 + i % 2][:, 0:T].rearrange("p (a b) -> p a b",
                    a=NT), ACT.Copy).then_inc(ct_ev, 1)

            def cross():
                norm_sums(6, X, 5)
                norm_hi("cross", "g_cross_2")
                for i in range(KC):
                    low(i, B_CQ + i, PS[C_BANKS[i % 4]], CLOW, c_low, c_sum, N_CKV)
                split_to(B_CO + RING)
                for j in range(4):
                    act.wait_ge(sc_max, 12 + j + 1)
                    for m in range(2):
                        e, q = CSC[:, j, m * T:(m + 1) * T], 2 * j + m
                        ins = act.activation(e, e, ACT.Exp, bias=CNM[:, q:q + 1], accum_out=CSUM[:, q:q + 1])
                        if m:
                            ins.then_inc(sc_exp, 1)
                for h in range(4):
                    act.wait_ge(pt_mm, 9 + h + 1)
                    act.activation(CPT[:, h, :], PS[4 + h][:, :], ACT.Copy).then_inc(pt_ev, 1)
                for h in range(4):
                    act.wait_ge(pv_mm, 4 + h + 1)
                    for d in range(2):
                        ins = act.activation(XT[:, 2 * h + d, 0:T], PS[h][:, d * T:(d + 1) * T], ACT.Copy)
                        if d:
                            ins.then_inc(o_hi, 1)
                for c in range(KC):
                    split_to(B_CO + c + LEAD + 1)

            def mlp():
                def chunk(j, i=None):
                    dj, dn = (0, 0) if i is None else (i * 3, i * 6)
                    q = j % 3
                    for k in range(2):
                        if k:
                            act.wait_ge(unit_used, B_MLP + max(0, 2 * j - 1) + 1 + dn)
                            if j >= 3:
                                act.wait_ge(r_sum, j - 2 + dj)
                            act.activation(UL[:, q, :], PS[4 + q][:, T:2 * T], ACT.Copy).then_inc(r_low, 1)
                        n = B_MLP + 2 * j + LEAD + k
                        if n < N_UNITS:
                            split_hi(n, i)
                    act.wait_ge(h_val, 2 * FC + j + 1 + dj)
                    if j >= 3:
                        act.wait_ge(unit_used, B_MLP + 2 * (j - 3) + 2 + 1 + dn)
                    act.activation(H[:, q, 0:T], HS[:, q, :], ACT.Copy).then_inc(r_hi, 1)

                split_to(B_MLP + LEAD)
                for j in range(3):
                    chunk(j)
                with act.Fori(0, 9) as i:
                    for k in range(3):
                        chunk(3 + k, i)
                for j in (30, 31):
                    chunk(j)

            act.wait_ge(const_in, 16)
            act.wait_ge(x_in, 32)
            norm_sums(0, X, 0)
            split_to(2)
            act.wait_ge(vec_ready, 1)
            norm_hi("ffn1", "ffn1_norm")
            ffn(B_FFN1, 0)
            norm_sums(1, X, 1)
            act.wait_ge(vec_ready, 2)
            norm_hi("mix", "mix_norm")
            mix()
            norm_sums(2, X, 2)
            norm_hi("ffn2", "ffn2_norm")
            ffn(B_FFN2, 1)
            attention()
            cross()
            norm_sums(7, X, 6)
            norm_hi("mlp", "g_mlp_2")
            mlp()
            norm_sums(8, X, 7)

        @block.vector
        def _(dve):
            own = Count()

            add, sub, mul, mx, mn = ALU.add, ALU.subtract, ALU.mult, ALU.max, ALU.min

            def split_lo(n, i=None):
                dve.wait_ge(hi_ready, n + 1 if i is None else i * RING + (n + 1))
                if n >= RING:
                    dve.wait_ge(unit_used, n - RING + 1 if i is None else i * RING + (n - RING + 1))
                dve.tensor_tensor(wlo[:, n % RING, :], raw[:, n % RAW, :], whi[:, n % RING, :].bitcast(F32),
                    sub).then_inc(lo_ready, 1)

            splits = Count()

            def split_to(n):
                while splits.n < min(n, N_UNITS):
                    split_lo(splits.n)
                    splits.next()

            def norm(q, in_place=False):
                for tt in range(NT):
                    dve.wait_ge(rms, 2 * q + tt + 1)
                    dve.reciprocal(RR[:, tt:tt + 1], MS[:, tt:tt + 1]).then_inc(own_dve, own.next())
                    dve.wait_ge(own_dve, own.n)
                    if in_place:
                        for h in range(2):
                            xs, hs = X[:, tt, 512 * h:512 * h + 512], slice(512 * h, 512 * h + 512)
                            dve.scalar_tensor_tensor(xs, xs, RR[:, tt:tt + 1], GFIN[:, hs], mul, mul).then_inc(x_upd, 1)
                    else:
                        dve.tensor_scalar(DIAG[:, tt, :], ident, RR[:, tt:tt + 1], None, mul).then_inc(xn, 1)

            def rest(c, ps, scale=None):
                hi = XT[:, c, 0:T].bitcast(F32)
                if scale is None:
                    return dve.tensor_tensor(XT[:, c, T:2 * T], ps, hi, sub)
                return dve.scalar_tensor_tensor(XT[:, c, T:2 * T], ps, scale, hi, mul, sub)

            def norm_lo(name, gain):
                q = NTP[name]
                for b in range(4):
                    dve.wait_ge(xt_hi, 4 * q + b + 1)
                    for c in (2 * b, 2 * b + 1):
                        ins = rest(c, PS[4 + b][:, (c % 2) * T:(c % 2 + 1) * T], vec(gain, c))
                    ins.then_inc(xt_ready, 1)

            def update_x(nth, end, factor):
                dve.wait_ge(half_used, nth)
                if nth == 2:
                    dve.wait_ge(mid_upd, 4)
                for k in range(4):
                    if k == 2:
                        dve.wait_ge(unit_used, end)
                    xs = X[:, k // 2, (k % 2) * 512:(k % 2 + 1) * 512]
                    dve.scalar_tensor_tensor(xs, PS[k][:, :], factor, xs, mul, add).then_inc(x_upd, 1)

            def ffn(b, f):
                J = FC * f

                def chunk(j, i=None):
                    dj = 0 if i is None else i * 2
                    q = j % 2

                    def next_split(k):
                        n = b + 3 * j + 4 + k
                        if n < N_UNITS:
                            split_lo(n, i)
                            if i is None:
                                splits.n = n + 1

                    next_split(0)
                    dve.wait_ge(g_low, J + j + 1 + dj)
                    dve.tensor_tensor(GS[:, q, :], PS[4 + q][:, 0:T], GL[:, q, :], add).then_inc(g_sum, 1)
                    next_split(1)
                    dve.wait_ge(u_low, J + j + 1 + dj)
                    dve.tensor_tensor(US[:, q, :], PS[6 + q][:, 0:T], UL[:, q, :], add).then_inc(u_sum, 1)
                    next_split(2)
                    dve.wait_ge(u_sum, J + j + 1 + dj)
                    dve.wait_ge(silu, J + j + 1 + dj)
                    dve.tensor_tensor(HS[:, q, :], SG[:, q, :], US[:, q, :], mul).then_inc(h_val, 1)
                    dve.wait_ge(h_val, J + j + 1 + dj)
                    dve.wait_ge(h_hi, J + j + 1 + dj)
                    dve.tensor_tensor(H[:, q, T:2 * T], HS[:, q, :], H[:, q, 0:T].bitcast(F32),
                        sub).then_inc(h_ready, 1)

                split_to(b + LEAD)
                chunk(0)
                chunk(1)
                with dve.Fori(0, 9) as i:
                    for k in range(2):
                        chunk(2 + k, i)
                chunk(20)
                chunk(21)
                if f == 0:
                    dve.wait_ge(vec_tp, 2)
                    dve.tensor_copy(VEC[:, KC:N_VEC], PS[7][:, KC:N_VEC]).then_inc(vec_ready, 1)
                update_x(2 * f + 1, b + 66, 0.5)

            def mix():
                CC8 = CC.rearrange("p f (c s) -> p (f c) s", c=2)
                ka = VEC_ROWS["k_a"]
                dve.tensor_scalar(OMK, VEC[:, ka:ka + NF], -1.0, 1.0, mul, add).then_inc(omk_ready, 1)
                for i, col in enumerate(WIN_COLS):
                    n = B_WIN + i
                    split_to(n + LEAD + 1)
                    dve.wait_ge(w_low, i + 1)
                    ps, low = PS[W_BANKS[i % 4]][:, 0:T], WLOW[:, i % 2, :]
                    if i >= 14:
                        dve.tensor_tensor(PP[:, i - 14, PAD:], ps, low, add).then_inc(w_sum, 1)
                    else:
                        dst = LBUF[:, i, :] if i < 2 else PV[:, i - 10, :] if i >= 10 else \
                            (PK, PR)[i % 2][:, (i - 2) // 2, :]
                        mu = vec("mu_tail") if i == 1 else vec("mu_shift", col // P)
                        now, before = WRAW[:, i % 2, 1:T + 1], WRAW[:, i % 2, 0:T]
                        if i == 0:
                            dve.wait_ge(w_zero, 6)
                        dve.tensor_tensor(now, ps, low, add).then_inc(w_sum, 1)
                        dve.wait_ge(w_sum, i + 1)
                        dve.tensor_tensor(WDF[:, i % 2, :], before, now, sub).then_inc(own_dve, own.next())
                        dve.wait_ge(own_dve, own.n)
                        dve.scalar_tensor_tensor(dst, WDF[:, i % 2, :], mu, now, mul, add).then_inc(w_mix, 1)
                    if i == 8:
                        dve.wait_ge(sw_done, NF)
                        for f in range(NF):
                            for c in range(NT):
                                cs = slice(c * P, (c + 1) * P)
                                dve.tensor_tensor_scan(CC[:, f, cs], SW[:, f, cs], SW[:, f, cs], 0.0, add, mx).then_inc(own_dve, own.next())
                        dve.wait_ge(own_dve, own.n)
                        dve.tensor_copy(CM, CC8[:, :, P // 2 - 1]).then_inc(own_dve, own.next())
                        dve.wait_ge(own_dve, own.n)
                        for k in range(2 * NF):
                            dve.tensor_scalar(CC8[:, k, :], CC8[:, k, :], CM[:, k:k + 1], None,
                                sub).then_inc(own_dve, own.next())
                    if i == 11:
                        dve.wait_ge(ec_base, 2 * NF)
                        dve.wait_ge(own_dve, own.n)
                        dve.tensor_tensor(K2, EC, PK, mul).then_inc(k2_ready, 1)
                        dve.wait_ge(k2_ready, 1)
                        for f in range(NF):
                            dve.scalar_tensor_tensor(DP[:, f, :], PR[:, f, :], vec("r_k", f), K2[:, f, :], mul,
                                mul).then_inc(bp_ready, 1)
                    if i == 12:
                        dve.wait_ge(nrm_done, 1)
                        dve.tensor_scalar(MXR, MXR, L2_EPS, None, mx).then_inc(own_dve, own.next())
                        dve.wait_ge(own_dve, own.n)
                        dve.reciprocal(MXR, MXR).then_inc(nrm_inv, 1)
                    if i == 14:
                        for k in range(2):
                            dve.wait_ge(nrm_mm, 2 * k + 2)
                            dve.tensor_tensor(KK[:, 2 * k:2 * k + 2, :], PS[k][:, :].rearrange("p (a b) -> p a b",
                                a=2), KK[:, 2 * k:2 * k + 2, :], mul).then_inc(own_dve, own.next())
                        dve.wait_ge(own_dve, own.n)
                        dve.tensor_tensor(AA, AA, KK, mul).then_inc(own_dve, own.next())
                        dve.wait_ge(dec_done, 3)
                        dve.wait_ge(own_dve, own.n)
                        dve.tensor_tensor(AA, AA, IP, mul).then_inc(own_dve, own.next())
                        dve.scalar_tensor_tensor(KK, KK, -1.0, EC, mul, mul).then_inc(kk_ready, 1)
                dve.wait_ge(w_mix, 14)
                for k in range(2):
                    dve.wait_ge(bp_mm, k + 1)
                    ins = dve.tensor_tensor(BON[:, 2 * k:2 * k + 2, :], PS[6 + k][:, :].rearrange("p (a b) -> p a b",
                        a=2), PV[:, 2 * k:2 * k + 2, :], mul)
                    if k:
                        ins.then_inc(bon_done, 1)
                    else:
                        ins.then_inc(own_dve, own.next())

                def window_sum(k):
                    n, first = 1 << k, k - k % 2
                    dst = PB[k % 2][:, first:, 2 * n - 1:]
                    if k == 0:
                        src = PP
                    else:
                        src = PB[1 - k % 2][:, k - (1 - k % 2):, :]
                    dve.wait_ge(own_dve, own.n)
                    dve.tensor_tensor(dst, src[:, :, 2 * n - 1:], src[:, :, n - 1:PAD + T - n],
                                      add).then_inc(own_dve, own.next())

                def window_mean(g):
                    win = WINDOWS[g]
                    s, first = window(g, PAD), window(g, PAD, PAD + win)
                    pp = PP[:, g:g + 1, PAD:]
                    a = CONST_COLS["invc"][0] + g * PAD
                    dve.wait_ge(own_dve, own.n)
                    if g:
                        dve.wait_ge(pooled, g)
                    tm = PTM[:, 0:win].rearrange("p (a b) -> p a b", a=1)
                    dve.tensor_tensor(tm, first, CON[:, a:a + win].rearrange("p (a b) -> p a b", a=1),
                                      mul).then_inc(own_dve, own.next())
                    dve.wait_ge(own_dve, own.n)
                    dve.scalar_tensor_tensor(s, s, 1.0 / win, pp, mul, sub).then_inc(own_dve, own.next())
                    dve.wait_ge(own_dve, own.n)
                    dve.tensor_tensor(first, tm, pp[:, :, 0:win], sub).then_inc(pooled, 1)

                def centre(k):
                    fs = slice(2 * k, 2 * k + 2)
                    dve.wait_ge(mean_mm, k + 1)
                    dve.scalar_tensor_tensor(YO[:, fs, :], PS[6][:, :].rearrange("p (a b) -> p a b", a=2),
                        -1.0 / 64, YO[:, fs, :], mul, add).then_inc(own_dve, own.next())
                    dve.wait_ge(own_dve, own.n)
                    dve.tensor_tensor(GV[:, fs, :], YO[:, fs, :], YO[:, fs, :], mul).then_inc(gd_ready, 1)

                def invert(k):
                    dve.wait_ge(gn_std, k + 1)
                    dve.reciprocal(GVR, GVR).then_inc(gn_inv, 1)

                def outputs(k):
                    dve.wait_ge(gn_mm, k + 1)
                    for f in (2 * k, 2 * k + 1):
                        ins = dve.scalar_tensor_tensor(YO[:, f, :], PS[7][:, (f % 2) * T:(f % 2 + 1) * T],
                            vec("ln_w", f), YO[:, f, :], mul, mul)
                        if f % 2:
                            ins.then_inc(gn_scaled, 1)
                        else:
                            ins.then_inc(own_dve, own.next())
                    dve.wait_ge(gn_scaled, k + 1)
                    dve.wait_ge(own_dve, own.n)
                    for f in (2 * k, 2 * k + 1):
                        dve.scalar_tensor_tensor(YO[:, f, :], YO[:, f, :], vec("ln_b", f), BON[:, f, :], add,
                            add).then_inc(own_dve, own.next())
                    dve.wait_ge(own_dve, own.n)
                    for f in (2 * k, 2 * k + 1):
                        dve.tensor_tensor(YO[:, f, :], YO[:, f, :], GG[:, f, :], mul).then_inc(y_val, 1)

                def lower(k):
                    for f in (2 * k, 2 * k + 1):
                        dve.wait_ge(y_hi, f + 1)
                        rest(f, YO[:, f, :]).then_inc(yt_ready, 1)

                for wv in range(2):
                    for g in range(2):
                        M = mats[g]
                        for h in range(2):
                            dve.wait_ge(m_mm, 12 * wv + 6 * g + h + 1)
                            dve.tensor_tensor(M["LT"][:, h, :, :], PS[(6 * g + h + 4) % 8][:,
                                :].rearrange("p (a b) -> p a b", a=4), bc(con("lt"), 4), mul).then_inc(m_ev, 1)
                        for h in range(2):
                            dve.wait_ge(m_mm, 12 * wv + 6 * g + 2 + h + 1)
                            dve.tensor_tensor(M["XM"][:, 2 * h:2 * h + 2, :], PS[(6 * g + 2 + h + 4) % 8][:,
                                0:T].rearrange("p (a b) -> p a b", a=2), bc(con("lev0"), 2), mul).then_inc(m_ev,
                                    1)
                        for h in range(2):
                            dve.wait_ge(m_mm, 12 * wv + 6 * g + 4 + h + 1)
                            dve.tensor_tensor(M["MM"][:, h, :, :], PS[(6 * g + 4 + h + 4) % 8][:,
                                :].rearrange("p (a b) -> p a b", a=4), bc(con("le"), 4), mul).then_inc(m_ev, 1)
                        dve.wait_ge(m_ev, 12 * wv + 6 * g + 6)
                        for h in range(2):
                            dve.tensor_tensor(M["XMT"][:, 2 * h:2 * h + 2, :], M["LT"][:, h, 0:2, :],
                                bc(con("lev0t"), 2), mul).then_inc(own_dve, own.next())
                        dve.tensor_tensor(M["XM"][:, :, :], M["XM"][:, :, :], bc(ident, 4),
                            add).then_inc(own_dve, own.next())
                        dve.wait_ge(own_dve, own.n)
                        dve.tensor_tensor(M["XMT"][:, :, :], M["XMT"][:, :, :], bc(ident, 4),
                            add).then_inc(inv_ev, 1)
                    for k in range(1, 7):
                        for g in range(2):
                            M = mats[g]
                            dve.wait_ge(inv_mm, wv * 12 + (k - 1) * 2 + g + 1)
                            psx, psxt = (PS[3 * g + n][:, :].rearrange("p (a b) -> p a b", a=4) for n in (1, 2))
                            if k < 6:
                                dve.tensor_tensor(M["XM"], psx, M["XM"], add).then_inc(own_dve, own.next())
                            dve.tensor_tensor(M["XMT"], psxt, M["XMT"], add).then_inc(inv_ev, 1)
                        if k == 1:
                            split_to(B_WOUT + 2 * wv + RING)
                        if wv == 0:
                            if k == 1:
                                dve.wait_ge(scaled, 2)
                            if k <= 4:
                                window_sum(k - 1)
                            if 2 <= k <= 5:
                                window_mean(k - 2)
                        elif k == 2:
                            centre(0)
                        elif k == 4:
                            invert(0)
                        elif k == 5:
                            outputs(0)
                    if wv == 0:
                        for g in range(NF):
                            dve.wait_ge(pool_hi, 2 * (g // 2) + 2)
                            rest(4 + g, PS[6 + g // 2][:, (g % 2) * T:(g % 2 + 1) * T],
                                 vec("pool_scale", g)).then_inc(yt_ready, 1)
                    dve.wait_ge(s_s_mm, wv + 1)
                    dve.wait_ge(dec_done, 4)
                    for g in range(2):
                        f = 2 * wv + g
                        ins = dve.tensor_scalar(ST[:, f, :], PS[7][:, T + g * 64:T + g * 64 + 64], FAC[:, f:f + 1], None, mul)
                        if g:
                            ins.then_inc(s_s_ev, 1)
                        else:
                            ins.then_inc(own_dve, own.next())
                    if wv:
                        lower(0)
                    else:
                        dve.wait_ge(unit_used, B_WOUT + 2)
                        for k in range(4):
                            xs = X[:, k // 2, (k % 2) * 512:(k % 2 + 1) * 512]
                            dve.tensor_tensor(xs, PS[k][:, :], xs, add).then_inc(mid_upd, 1)
                centre(1)
                invert(1)
                outputs(1)
                lower(1)
                for c in range(KC):
                    split_to(B_WOUT + c + LEAD + 1)
                update_x(2, B_WOUT + KC, 1.0)

            def rope_args():
                C1, big = 6.28125, 12582912.0
                C2 = float(np.float32(2 * math.pi - C1))
                dve.wait_ge(pos_in, 16 * 6)
                dve.tensor_copy(POSF, POSI.bitcast(I32)).then_inc(own_dve, own.next())
                dve.wait_ge(own_dve, own.n)
                dve.tensor_scalar(ANG, POSF, con("freq"), None, mul).then_inc(own_dve, own.next())
                dve.wait_ge(own_dve, own.n)
                for k, turn in ((0, 0.25), (1, 0.0)):
                    dve.tensor_scalar(RA[k], ANG, 1.0 / (2 * math.pi), turn, mul, add).then_inc(own_dve,
                        own.next())
                    dve.wait_ge(own_dve, own.n)
                    dve.tensor_scalar(RA[k], RA[k], big, -big, add, add).then_inc(own_dve, own.next())
                    dve.wait_ge(own_dve, own.n)
                    dve.scalar_tensor_tensor(RA[2 + k], RA[k], -C1, ANG, mul, add).then_inc(own_dve, own.next())
                    dve.wait_ge(own_dve, own.n)
                    dve.scalar_tensor_tensor(RA[2 + k], RA[k], -C2, RA[2 + k], mul, add).then_inc(own_dve,
                        own.next())
                    dve.wait_ge(own_dve, own.n)
                    dve.tensor_scalar(RA[k], RA[2 + k], turn * 2 * math.pi, 3.1415925, add,
                        mn).then_inc(own_dve, own.next())
                    dve.wait_ge(own_dve, own.n)
                    dve.tensor_scalar(RA[k], RA[k], -3.1415925, None, mx).then_inc(own_dve, own.next())
                    dve.wait_ge(own_dve, own.n)
                dve.tensor_scalar(RA[1], RA[1], con("sign"), None, mul).then_inc(rope_arg, 1)
                for k in range(2):
                    dve.wait_ge(own_dve, own.n)
                    dve.tensor_tensor(LAMV[:, 4, :], LAMV[:, 2 * k, :], LAMV[:, 2 * k + 1, :],
                        mul).then_inc(own_dve, own.next())
                    dve.wait_ge(own_dve, own.n)
                    ins = dve.tensor_reduce(LDOT[:, k:k + 1], LAMV[:, 4, :], AX_X, add)
                    if k:
                        ins.then_inc(lam_arg, 1)
                    else:
                        ins.then_inc(own_dve, own.next())
                dve.tensor_scalar(GD8, vec("g_diff_2"), 1.0 - LAM_INIT, None, mul).then_inc(own_dve, own.next())

            def attention():
                norm(3)
                norm_lo("mem", "g_mem_2")
                dve.wait_ge(gain_in, 16)
                norm(4, in_place=True)
                for i in range(N_CKV):
                    split_to(B_CKV + i + LEAD + 1)
                    dve.wait_ge(c_low, i + 1)
                    k = i - KC
                    if k >= 2:
                        dve.wait_ge(ct_mm, k - 1)
                    dve.tensor_tensor(CK[:, i, :] if k < 0 else CTM[:, i % 2, :], PS[Q_BANKS[i % 4]][:, 0:T],
                        CLOW[:, i % 2, :], add).then_inc(c_sum, 1)
                    if i == 2:
                        norm(5)
                    if i == 6:
                        rope_args()
                norm_lo("mix2", "g_mix_2")
                dve.wait_ge(lam_arg, 1)
                n_rope = 0
                for i in range(N_WIN2 + 1):
                    if i < N_WIN2:
                        split_to(B_WIN2 + i + LEAD + 1)
                        dve.wait_ge(q_low, i + 1)
                        dve.tensor_tensor(QKV[:, i, :], PS[Q_BANKS[i % 4]][:, 0:T], CLOW[:, i % 2, :],
                            add).then_inc(q_sum, 1)
                    k = i - 1
                    if k >= 0 and k != 5 and k < 14:
                        if n_rope == 0:
                            dve.wait_ge(rope_tab, 2)
                            dve.wait_ge(lam_exp, 1)
                            dve.tensor_tensor(NLAM, LEXP[:, 1:2], LEXP[:, 0:1], sub).then_inc(own_dve,
                                own.next())
                            dve.wait_ge(own_dve, own.n)
                            dve.tensor_scalar(NLAM, NLAM, -LAM_INIT, None, add).then_inc(own_dve, own.next())
                        dve.wait_ge(rope_mm, n_rope + 1)
                        dve.wait_ge(q_sum, k + 1)
                        if n_rope:
                            dve.wait_ge(rope_done, n_rope)
                        dve.tensor_tensor(RT[:, 0, :], QKV[:, k, :], RC, mul).then_inc(own_dve, own.next())
                        dve.tensor_tensor(RT[:, 1, :], PS[6 - 4 * (n_rope % 2)][:, 0:T], RSN, mul).then_inc(own_dve, own.next())
                        dve.wait_ge(own_dve, own.n)
                        dve.tensor_tensor(QKV[:, k, :], RT[:, 0, :], RT[:, 1, :], add).then_inc(rope_done, 1)
                        n_rope += 1
                dve.wait_ge(rope_mm, n_rope + 1)
                dve.tensor_copy(KSW, PS[6][:, 0:T]).then_inc(rope_done, 1)
                split_to(B_WOUT2 + RING)

                def maxima(j):
                    kind, n, maps = JOBS[j]
                    nk, m = (n + 1) * P, len(maps)
                    q = slice(4 * j, 4 * j + m)
                    dve.wait_ge(sc_mm, j + 1)
                    s = SC[:, j, :].rearrange("p (m k) -> p m k", m=m)
                    ps = PS[j % 4][:, :].rearrange("p (m k) -> p m k", m=m)
                    if n and kind == "swa":
                        a = CONST_COLS["prev"][0]
                        dve.scalar_tensor_tensor(s, ps, 0.125, bc(CON[:, a:a + 2 * P], m), mul,
                            add).then_inc(sc_sum, 1)
                    elif n:
                        dve.tensor_scalar(s[:, :, 0:P], ps[:, :, 0:P], 0.125, None, mul).then_inc(own_dve,
                            own.next())
                        dve.scalar_tensor_tensor(s[:, :, P:], ps[:, :, P:], 0.125, bc(con("diag"), m), mul,
                            add).then_inc(sc_sum, 1)
                    else:
                        dve.scalar_tensor_tensor(s, ps, 0.125, bc(con("diag"), m), mul, add).then_inc(sc_sum, 1)
                    dve.wait_ge(sc_sum, j + 1)
                    dve.wait_ge(own_dve, own.n)
                    dve.tensor_reduce(NMX[:, q], s, AX_X, mx).then_inc(own_dve, own.next())
                    dve.wait_ge(own_dve, own.n)
                    if kind == "swa":
                        sink = SNK[:, maps[0]:maps[-1] + 1:2]
                        dve.tensor_tensor(NMX[:, q], NMX[:, q], sink, mx).then_inc(own_dve, own.next())
                        dve.wait_ge(own_dve, own.n)
                        dve.tensor_scalar(NMX[:, q], NMX[:, q], -1.0, None, mul).then_inc(own_dve, own.next())
                        dve.wait_ge(own_dve, own.n)
                        dve.tensor_tensor(ESK[:, q], sink, NMX[:, q], add).then_inc(sc_max, 1)
                    else:
                        dve.tensor_scalar(NMX[:, q], NMX[:, q], -1.0, None, mul).then_inc(sc_max, 1)

                def normalise(j):
                    kind, n, maps = JOBS[j]
                    nk, m = (n + 1) * P, len(maps)
                    q = slice(4 * j, 4 * j + m)
                    dve.wait_ge(sc_exp, j + 1)
                    if kind == "swa":
                        dve.tensor_tensor(SUM[:, q], SUM[:, q], ESK[:, q], add).then_inc(own_dve, own.next())
                        dve.wait_ge(own_dve, own.n)
                    dve.reciprocal(REC[:, q], SUM[:, q]).then_inc(own_dve, own.next())
                    dve.wait_ge(own_dve, own.n)
                    if kind == "diff" and j % 2 == 0:
                        return
                    if kind == "diff":
                        dve.tensor_scalar(REC[:, q], REC[:, q], NLAM, None, mul).then_inc(own_dve, own.next())
                        dve.wait_ge(own_dve, own.n)
                    for k in range(m):
                        e = SC[:, j, k * nk:(k + 1) * nk]
                        ins = dve.tensor_scalar(e, e, REC[:, 4 * j + k:4 * j + k + 1], None, mul)
                        if kind == "swa" and k == m - 1:
                            ins.then_inc(p_ready, 1)
                        else:
                            ins.then_inc(own_dve, own.next())
                    if kind == "diff":
                        dve.wait_ge(own_dve, own.n)
                        for k in range(m):
                            e, e1 = (SC[:, x, k * nk:(k + 1) * nk] for x in (j - 1, j))
                            ins = dve.scalar_tensor_tensor(e, e, REC[:, 4 * (j - 1) + k:4 * (j - 1) + k + 1], e1,
                                mul, add)
                            if k == m - 1:
                                ins.then_inc(p_ready, 1)
                            else:
                                ins.then_inc(own_dve, own.next())

                for j in range(12):
                    maxima(j)
                    if j:
                        normalise(j - 1)
                normalise(11)
                dve.wait_ge(od_ss, 2)
                dve.tensor_scalar(ODS, ODS, 1.0 / P, NORM_EPS, mul, add).then_inc(od_ms, 1)
                dve.wait_ge(od_std, 1)
                dve.reciprocal(ODR, ODS).then_inc(own_dve, own.next())
                dve.wait_ge(own_dve, own.n)
                for n in range(NT):
                    for h in range(4):
                        ins = dve.tensor_scalar(ODN[:, n, h * P:(h + 1) * P], PS[2 + n][:, h * P:(h + 1) * P], ODR[:,
                            4 * n + h:4 * n + h + 1], None, mul)
                        if h == 3:
                            ins.then_inc(od_norm, 1)
                        else:
                            ins.then_inc(own_dve, own.next())
                for c in range(4):
                    dve.wait_ge(o_hi, c // 2 + 1)
                    rest(c, PS[c // 2][:, (c % 2) * T:(c % 2 + 1) * T]).then_inc(yt_ready, 1)
                for h in range(4):
                    dve.wait_ge(o_hi, 2 + h // 2 + 1)
                    rest(4 + h, PS[4 + h // 2][:, (h % 2) * T:(h % 2 + 1) * T], GD8).then_inc(yt_ready, 1)
                for c in range(KC):
                    split_to(B_WOUT2 + c + LEAD + 1)
                update_x(4, B_WOUT2 + KC, 1.0)

            def cross():
                norm(6)
                norm_lo("cross", "g_cross_2")
                for i in range(KC):
                    split_to(B_CQ + i + LEAD + 1)
                    dve.wait_ge(c_low, N_CKV + i + 1)
                    dve.tensor_tensor(CQ[:, i, :], PS[C_BANKS[i % 4]][:, 0:T], CLOW[:, i % 2, :],
                        add).then_inc(c_sum, 1)
                split_to(B_CO + RING)

                def maxima(j):
                    dve.wait_ge(sc_mm, 12 + j + 1)
                    q = slice(2 * j, 2 * j + 2)
                    dve.tensor_scalar(CSC[:, j, :], PS[j][:, :], 1.0 / 16, None, mul).then_inc(sc_sum, 1)
                    dve.wait_ge(sc_sum, 12 + j + 1)
                    dve.tensor_reduce(CNM[:, q], CSC[:, j, :].rearrange("p (m k) -> p m k", m=2), AX_X, mx).then_inc(own_dve, own.next())
                    dve.wait_ge(own_dve, own.n)
                    dve.tensor_scalar(CNM[:, q], CNM[:, q], -1.0, None, mul).then_inc(sc_max, 1)

                def normalise(j):
                    q = slice(2 * j, 2 * j + 2)
                    dve.wait_ge(sc_exp, 12 + j + 1)
                    dve.reciprocal(CREC[:, q], CSUM[:, q]).then_inc(own_dve, own.next())
                    dve.wait_ge(own_dve, own.n)
                    for m in range(2):
                        e = CSC[:, j, m * T:(m + 1) * T]
                        ins = dve.tensor_scalar(e, e, CREC[:, 2 * j + m:2 * j + m + 1], None, mul)
                        if m:
                            ins.then_inc(p_ready, 1)
                        else:
                            ins.then_inc(own_dve, own.next())

                for j in range(4):
                    maxima(j)
                    if j:
                        normalise(j - 1)
                normalise(3)
                for h in range(4):
                    dve.wait_ge(o_hi, 4 + h + 1)
                    for d in range(2):
                        rest(2 * h + d, PS[h][:, d * T:(d + 1) * T]).then_inc(yt_ready, 1)
                for c in range(KC):
                    split_to(B_CO + c + LEAD + 1)
                update_x(5, B_CO + KC, 1.0)

            def mlp():
                def chunk(j, i=None):
                    dj = 0 if i is None else i * 3
                    q = j % 3
                    for k in range(2):
                        if k:
                            dve.wait_ge(r_low, j + 1 + dj)
                            dve.tensor_tensor(US[:, q, :], PS[4 + q][:, 0:T], UL[:, q, :], add).then_inc(r_sum, 1)
                        n = B_MLP + 2 * j + LEAD + k
                        if n < N_UNITS:
                            split_lo(n, i)
                    dve.wait_ge(r_sum, j + 1 + dj)
                    dve.scalar_tensor_tensor(HS[:, q, :], US[:, q, :], 0.0, US[:, q, :], mx, mul).then_inc(h_val, 1)
                    dve.wait_ge(h_val, 2 * FC + j + 1 + dj)
                    dve.wait_ge(r_hi, j + 1 + dj)
                    dve.tensor_tensor(H[:, q, T:2 * T], HS[:, q, :], H[:, q, 0:T].bitcast(F32), sub)\
                       .then_inc(r_ready, 1)

                split_to(B_MLP + LEAD)
                for j in range(3):
                    chunk(j)
                with dve.Fori(0, 9) as i:
                    for k in range(3):
                        chunk(3 + k, i)
                for j in (30, 31):
                    chunk(j)
                update_x(6, N_UNITS, 1.0)

            dve.wait_ge(vec_tp, 1)
            dve.tensor_copy(VEC[:, 0:KC], PS[7][:, 0:KC]).then_inc(vec_ready, 1)
            norm(0)
            dve.wait_ge(vec_ready, 1)
            split_to(2)
            norm_lo("ffn1", "ffn1_norm")
            ffn(B_FFN1, 0)
            norm(1)
            dve.wait_ge(vec_ready, 2)
            norm_lo("mix", "mix_norm")
            mix()
            norm(2)
            norm_lo("ffn2", "ffn2_norm")
            ffn(B_FFN2, 1)
            attention()
            cross()
            norm(7)
            norm_lo("mlp", "g_mlp_2")
            mlp()
            dve.wait_ge(gain_in, 32)
            norm(8, in_place=True)

        @block.gpsimd
        def _(pool):
            pool.memset(ROWS, 0.0).then_inc(rows_zero, 1)
            pool.wait_ge(rows_zero, 1)
            for n, a in enumerate((LWA[32:64, 0, :], LWA[0:32, 1, :], LWG[32:64, :], LG[32:64, :], WRAW[:, :, 0:1], PP[:, :, 0:PAD])):
                pool.memset(a, 0.0).then_inc(w_zero, 1)
                pool.wait_ge(w_zero, n + 1)
            pool.wait_ge(k2_ready, 1)
            pool.tensor_tensor(EC, CC, SW, ALU.subtract).then_inc(ec_ready, 1)
            pool.wait_ge(ec_ready, 1)
            pool.tensor_tensor(FAC, CC[:, :, P - 1], CM.rearrange("p (f c) -> p f c", c=2)[:, :, 1],
                               ALU.add).then_inc(ec_ready, 1)
            pool.wait_ge(dec_done, 3)
            pool.wait_ge(bp_ready, NF)
            pool.wait_ge(ec_ready, 2)
            pool.tensor_tensor(K2, K2, IP, ALU.mult).then_inc(scaled, 1)
            pool.wait_ge(scaled, 1)
            pool.tensor_tensor(PR, PR, CC, ALU.mult).then_inc(scaled, 1)
            pool.wait_ge(scaled, 2)
            for wv in range(2):
                for k in range(1, 7):
                    for g in range(2):
                        n = wv * 12 + (k - 1) * 2 + g
                        M = mats[g]
                        if k == 1:
                            pool.wait_ge(m_ev, 12 * wv + 6 * g + 2)
                        if n >= 2:
                            pool.wait_ge(t_mm, n - 1)
                        mask = con(f"lev{k}t").rearrange("p (a b c) -> p a b c", a=1, b=1)
                        pool.tensor_tensor(M["LEV"].rearrange("p (h c) s -> p h c s", h=2), M["LT"][:, :, 0:2, :],
                                           mask.broadcast_to([P, 2, 2, P]), ALU.mult).then_inc(levmask, 1)
                        pool.wait_ge(levmask, n + 1)


NAMES_IN = ("x ffn1_norm ffn1_w_gate ffn1_w_up ffn1_w_down mix_norm w_in mu_shift w0 w_lora_up a0 a_lora_up "
            "g_lora_up k_k k_a r_k ln_w ln_b w_pool pool_scale w_out ffn2_norm ffn2_w_gate ffn2_w_up ffn2_w_down "
            "final_norm mem_2 positions_2 g_mix_2 w_in_2 sinks_2 lambda_q1_2 lambda_k1_2 lambda_q2_2 lambda_k2_2 "
            "g_diff_2 w_out_2 g_cross_2 g_mem_2 w_cq_2 w_ckv_2 w_co_2 g_mlp_2 w_up_2 w_down_2 g_final_2").split()


def kernel(**inputs):
    import numpy as _np
    import concourse.bacc as _bacc
    from concourse import mybir as _mybir
    from concourse.bass_utils import run_bass_kernel_spmd as _run

    nc = _bacc.Bacc("TRN2", target_bir_lowering=False, num_devices=1)
    arrays, handles = {}, {}
    for name in NAMES_IN:
        a = _np.ascontiguousarray(inputs[name])
        arrays[f"in_{name}"] = a
        handles[name] = nc.dram_tensor(f"in_{name}", a.shape, _mybir.dt.from_np(a.dtype), kind="ExternalInput").ap()
    c = constants()
    arrays["in_consts"] = c
    handles["consts"] = nc.dram_tensor("in_consts", c.shape, _mybir.dt.float32, kind="ExternalInput").ap()
    out = nc.dram_tensor("out", (1, T, D), _mybir.dt.float32, kind="ExternalOutput").ap()
    build(nc, handles, out)
    r = _run(nc, [arrays], core_ids=[0])
    return r.results[0]["out"]
```

```python
import math
from contextlib import ExitStack

import numpy as np
import concourse.bass as bass
from concourse import mybir

F32 = mybir.dt.float32
F32R = mybir.dt.float32r
I32 = mybir.dt.int32
ALU = mybir.AluOpType
ACT = mybir.ActivationFunctionType
AX_X = mybir.AxisListType.X

P = 128
D = 1024
T = 256
NT = T // P
KC = D // P
RW = 512
NF = RW // P
FF = 2816
FC = FF // P
FF2 = 4096
FC2 = FF2 // P
LORA = 1536
POOL = 1696
WINDOWS = (2, 4, 8, 16)
PAD = max(WINDOWS)
RMS_EPS = 1e-6
NORM_EPS = 1e-5
GN_EPS = 64e-5
L2_EPS = 1e-12
LN_DECAY = -math.exp(-0.5)
LAM_INIT = 0.8 - 0.6
NEG = -1e30

UNIT = 1024
RAW = 3
RING = 6
LEAD = 4
B_FFN1 = 0
B_WIN = B_FFN1 + 3 * FC
N_WIN = 18
B_WOUT = B_WIN + N_WIN
B_FFN2 = B_WOUT + KC
B_CKV = B_FFN2 + 3 * FC
N_CKV = 2 * KC
B_WIN2 = B_CKV + N_CKV
N_WIN2 = 18
B_WOUT2 = B_WIN2 + N_WIN2
B_CQ = B_WOUT2 + KC
B_CO = B_CQ + KC
B_MLP = B_CO + KC
N_UNITS = B_MLP + 2 * FC2

WIN_COLS = [LORA, LORA + P] + [x for f in range(NF) for x in (RW + f * P, f * P)] + \
           [2 * RW + f * P for f in range(NF)] + [POOL + g * P for g in range(NF)]

VEC_ROWS = {}
_at = 0
for _name, _n in (("ffn1_norm", 8), ("mix_norm", 8), ("ffn2_norm", 8), ("g_mix_2", 8), ("g_cross_2", 8),
                  ("g_mem_2", 8), ("g_mlp_2", 8), ("w0", 4), ("a0", 4), ("k_k", 4), ("k_a", 4), ("r_k", 4),
                  ("ln_w", 4), ("ln_b", 4), ("pool_scale", 4), ("mu_shift", 13), ("mu_tail", 1), ("g_diff_2", 1)):
    VEC_ROWS[_name] = _at
    _at += _n
N_VEC = _at

CONST_COLS = {}
_at = 0
for _name, _n in [("ident", P), ("eps", 1), ("eps_block", 1), ("eps_group", 1),
                  ("swap32", P), ("swap64", P), ("blk", P), ("lt", P), ("gt", P), ("le", P),
                  ("lev0t", P), ("lev0", P)] + [(f"lev{k}t", P) for k in range(1, 7)] + \
                 [("prev", P), ("diag", P), ("invc", 4 * PAD), ("freq", 1), ("sign", 1),
                     ("heads", NF * 8), ("spread", NF * P)]:
    CONST_COLS[_name] = (_at, _n)
    _at += _n
N_CONST = _at
N_FIRST = CONST_COLS["swap32"][0]


def constants():
    c = np.zeros((P, N_CONST), np.float32)

    def put(name, value):
        a, n = CONST_COLS[name]
        c[:, a:a + n] = value

    i, j = np.arange(P)[:, None], np.arange(P)[None, :]
    put("ident", i == j)
    put("swap32", j == (i ^ 32))
    put("swap64", j == (i ^ 64))
    put("blk", (i // 64) == (j // 64))
    put("lt", i < j)
    put("gt", i > j)
    put("le", i <= j)
    for k in range(7):
        pair = (i >> (k + 1)) == (j >> (k + 1))
        upper = pair & (((i >> k) & 1) == 0) & (((j >> k) & 1) == 1)
        put(f"lev{k}t", upper)
        if k == 0:
            put("lev0", upper.T)
    put("prev", np.where(j > i, 0.0, NEG))
    put("diag", np.where(j <= i, 0.0, NEG))
    t1 = np.arange(1, PAD + 1)
    put("invc", np.concatenate([1.0 / np.minimum(t1, w) for w in WINDOWS])[None])
    put("freq", (np.float32(10000.0) ** (-(2 * (np.arange(P) % 32)).astype(np.float32) / np.float32(64)))[:, None])
    put("sign", np.where(np.arange(P) % 64 < 32, -1.0, 1.0)[:, None])
    q = np.arange(2 * NF)
    put("heads", np.concatenate([q[None] == 2 * f + i // 64 for f in range(NF)], 1))
    put("spread", np.concatenate([i == 2 * f + j // 64 for f in range(NF)], 1))
    put("eps", RMS_EPS)
    put("eps_group", GN_EPS)
    put("eps_block", NORM_EPS)
    return c


def build(nc, t, out):
    ctx = ExitStack()
    with ctx:
        def sb(name, shape, dt=F32):
            return ctx.enter_context(nc.sbuf_tensor(name, shape, dt))

        raw = sb("raw", [P, RAW, UNIT])
        whi = sb("whi", [P, RING, UNIT], F32R)
        wlo = sb("wlo", [P, RING, UNIT], F32R)
        X = sb("X", [P, NT, D])
        XT = sb("XT", [P, KC, 2 * T], F32R)
        H = sb("H", [P, 3, 2 * T], F32R)
        CON = sb("CON", [P, N_CONST])
        VEC = sb("VEC", [P, P])
        LWA = sb("LWA", [64, 2, RW])
        LWG = sb("LWG", [P, RW])
        WPL = sb("WPL", [P, NF, P])
        SMALL = sb("SMALL", [P, 512])
        AN = 24 * 1024
        arena = sb("arena", [P, AN])
        PS = [ctx.enter_context(nc.psum_tensor(f"ps{i}", [P, 512], F32)) for i in range(8)]

        def ar(off, *shape):
            n = int(np.prod(shape))
            assert off + n <= AN, (off, shape)
            v = arena[:, off:off + n]
            if len(shape) == 2:
                v = v.rearrange("p (a b) -> p a b", a=shape[0])
            return v

        def con(name, rows=P):
            a, n = CONST_COLS[name]
            return CON[0:rows, a:a + n]

        def vec(name, i=0):
            c = VEC_ROWS[name] + i
            return VEC[:, c:c + 1]

        ident = con("ident")

        DIAG = ar(0, NT, P)
        GL, GS, SG, UL, US, HS = (ar(2048 + 768 * k, 3, T) for k in range(6))
        SQJ = ar(6656, D)
        ROWS = ar(8192, P)
        FIRST = ar(8320, P)[0:KC, :]
        GFIN = ar(8192, D)
        MEMX = ar(11008, NT, D)
        SS, MS, RR = SMALL[:, 328:330], SMALL[:, 332:334], SMALL[:, 334:336]

        PR, PK, PV, SW, AA, GG, KK, K2, CC, EC, IP, BON = (ar(1024 * k, NF, T) for k in range(12))
        VTOK = ar(1024 * 1, NT, RW)
        BTOK = ar(1024 * 3, RW)
        KTOK = ar(1024 * 3 + 512, RW)
        RB = ar(1024 * 8, 4, T)
        SQ = IP
        YO = PV
        GV = EC
        MB = 12 * 1024
        mats = [{n: ar(MB + 512 * (8 * g + k), 4, P) for k, n in ((4, "XM"), (5, "XMT"), (6, "TS"), (7, "LEV"))}
                for g in range(2)]
        for g in range(2):
            for k, n in ((0, "LT"), (2, "MM")):
                mats[g][n] = ar(MB + 512 * (8 * g + k), 8 * P).rearrange("p (h m s) -> p h m s", h=2, m=4)
        MX = ar(MB + 512 * 6, NF, T)
        DP = ar(MB + 512 * 14, NF, T)
        EX = MB + 512 * 16
        LBUF = ar(EX, 2, T)
        LW = ar(EX + 512, T)
        LG = ar(EX + 768, T)
        FAC = ar(EX + 1024, NF)
        CM = ar(EX + 1032, 2 * NF)
        ST = ar(EX + 1040, NF, 64)
        PTM = ar(EX + 1296, PAD)
        WLOW = ar(EX + 1312, 2, T)
        WRAW = ar(EX + 1824, 2, T + 1)
        WDF = ar(EX + 2340, 2, T)
        PP = ar(EX + 2852, NF, PAD + T)
        PB = [ar(EX + 1312, NF, PAD + T), ar(1024 * 10, NF - 1, PAD + T)]
        OMK = SMALL[:, 360:360 + NF]

        MXR = MX[0:8, 0, :]
        GVR = GV[0:8, 0, :]

        def heads(f):
            a = CONST_COLS["heads"][0] + 8 * f
            return CON[:, a:a + 8]

        def spread(f):
            a = CONST_COLS["spread"][0] + P * f
            return CON[0:8, a:a + P]

        def turner(job, m, n=1):
            if job < 4:
                return ar(4864 + 256 * job + m * P, n * P)
            if job < 6:
                return ar(23552 + 512 * (job - 4) + m * P, n * P)
            if job < 8:
                return LWG[:, 256 * (job - 6) + m * P:256 * (job - 6) + (m + n) * P]
            if job < 10:
                return WPL[:, 2 * (job - 8) + m:2 * (job - 8) + m + n, :].rearrange("p a b -> p (a b)")
            return ODN[:, job - 10, m * P:(m + n) * P]

        def each(cols):
            return cols.rearrange("p (a b) -> p a b", b=1).broadcast_to([P, cols.shape[-1], P])

        def window(g, first=0, last=PAD + T):
            return PB[g % 2][:, g - g % 2:g - g % 2 + 1, first:last]


        QKV = ar(0, N_WIN2, T)
        KSW = ar(4608, T)
        RC, RSN = ar(4864, T), ar(5120, T)
        RT = ar(5376, 2, T)
        VT2 = ar(5888, NT, 640)
        SC = ar(7168, 12, 512)
        POSI, POSF, ANG = (ar(9216 + 256 * k, T) for k in range(3))
        RA = [ar(9984 + 256 * k, T) for k in range(4)]
        PTS = ar(13312, 9, 512)
        NMX, SUM, REC, ESK = (ar(17920 + 48 * k, 48) for k in range(4))
        ODJ = ar(0, D)
        ODS = ar(18112, 8)
        ODR = ar(18120, 8)
        ODN = ar(18432, NT, RW)
        LAMV = SMALL[:, 0:320].rearrange("p (a b) -> p a b", a=5)
        SNK = SMALL[:, 320:328]
        NSNK = SMALL[:, 364:372]
        WARM = SMALL[:, 376:377]
        LDOT = SMALL[:, 340:342]
        LEXP = SMALL[:, 342:344]
        NLAM = SMALL[:, 344:345]
        GD8 = SMALL[:, 345:346]
        CK = ar(19456, KC, T)
        CVT = ar(21504, NT, D)
        CLOW = ar(23552, 2, T)
        CTM = ar(24064, 2, T)
        CQ = ar(0, KC, T)
        CSC = ar(2048, 4, 512)
        CPT = ar(4096, 4, 512)
        CNM, CSUM, CREC = (ar(6144 + 8 * k, 8) for k in range(3))

        def sems(names):
            return [ctx.enter_context(nc.semaphore(n)) for n in names.split()]

        unit_used, half_used, hi_ready, lo_ready = \
            sems("unit_used half_used hi_ready lo_ready")
        const_in, table_in, rows_zero, rows_in, first_in, warm_set, mem_in, small_in, gain_in, pos_in = \
            sems("const_in table_in rows_zero rows_in first_in warm_set mem_in small_in gain_in pos_in")
        out_done, = sems("out_done")
        vec_tp, vec_ready, ss, rms, xn, tp, xt_hi = \
            sems("vec_tp vec_ready ss rms xn tp xt_hi")
        xt_ready, x_upd = \
            sems("xt_ready x_upd")
        g_low, g_sum, silu, u_low, u_sum, h_val, h_hi, h_ready = \
            sems("g_low g_sum silu u_low u_sum h_val h_hi h_ready")
        r_low, r_sum, r_hi, r_ready = \
            sems("r_low r_sum r_hi r_ready")
        w_zero, w_low, w_sum, w_mix, lora_act, lora_mm, sw_done, sa_done = \
            sems("w_zero w_low w_sum w_mix lora_act lora_mm sw_done sa_done")
        sg_done, sq_ready, ssq_mm, nrm_done, ec_ready, dec_done, kk_ready, bp_ready = \
            sems("sg_done sq_ready ssq_mm nrm_done ec_ready dec_done kk_ready bp_ready")
        bp_mm, bon_done, tok_mm, tok_ev, nrm_inv, nrm_mm, omk_ready, ec_base, k2_ready, scaled = \
            sems("bp_mm bon_done tok_mm tok_ev nrm_inv nrm_mm omk_ready ec_base k2_ready scaled")
        m_mm, m_ev, mm_mm, mm_ev, levmask, t_mm, t_ev, x_mm, inv_x, inv_mm, inv_ev, s_r_mm = \
            sems("m_mm m_ev mm_mm mm_ev levmask t_mm t_ev x_mm inv_x inv_mm inv_ev s_r_mm")
        s_r_ev, s_u_mm, s_u_ev, s_y_mm, s_y_ev, s_s_mm, s_s_ev = \
            sems("s_r_ev s_u_mm s_u_ev s_y_mm s_y_ev s_s_mm s_s_ev")
        mean_mm, gd_ready, var_mm, gn_inv, gn_mm, gn_scaled, gn_std, y_val, y_hi, yt_ready = \
            sems("mean_mm gd_ready var_mm gn_inv gn_mm gn_scaled gn_std y_val y_hi yt_ready")
        pooled, pool_mm, pool_hi, mid_upd = \
            sems("pooled pool_mm pool_hi mid_upd")
        rope_arg, rope_tab, lam_arg, lam_exp, q_low, q_sum, rope_mm, rope_done = \
            sems("rope_arg rope_tab lam_arg lam_exp q_low q_sum rope_mm rope_done")
        vt_mm, vt_ev, sc_mm, sc_sum, sc_max, sc_exp, p_ready, pt_mm = \
            sems("vt_mm vt_ev sc_mm sc_sum sc_max sc_exp p_ready pt_mm")
        pt_ev, pv_mm, o_hi, rec_ready, cp_ready, od_ss, od_std, od_norm, odt_mm = \
            sems("pt_ev pv_mm o_hi rec_ready cp_ready od_ss od_std od_norm odt_mm")
        c_low, c_sum, ct_mm, ct_ev = \
            sems("c_low c_sum ct_mm ct_ev")
        own_dve, = sems("own_dve")
        x_in = [ctx.enter_context(nc.semaphore(f"x_in{i}")) for i in range(NT)]
        raw_full = [ctx.enter_context(nc.semaphore(f"raw_full{i}")) for i in range(RAW)]
        block = ctx.enter_context(nc.Block())


        def bc(ap, n):
            return ap.rearrange("p (a b) -> p a b", a=1).broadcast_to([P, n, ap.shape[-1]])

        class Count:
            def __init__(self):
                self.n = 0

            def next(self):
                self.n += 1
                return 1

        RMS_NORMS = (0, 1, 2, 4)
        NTP = {"ffn1": 0, "mix": 1, "ffn2": 2, "mem": 3, "mix2": 4, "cross": 5, "mlp": 6}
        JOBS = [("swa", 1, [0, 2]), ("swa", 1, [4, 6]), ("swa", 1, [1, 3]), ("swa", 1, [5, 7]),
                ("swa", 0, [0, 2, 4, 6]), ("swa", 0, [1, 3, 5, 7]),
                ("diff", 1, [0, 2]), ("diff", 1, [1, 3]), ("diff", 1, [4, 6]), ("diff", 1, [5, 7]),
                ("diff", 0, [0, 2, 4, 6]), ("diff", 0, [1, 3, 5, 7])]
        BLOCKS = [[(j, m, kb) for m in range(2) for kb in range(2)] for j in range(4)] + \
                 [[(j, m, 0) for m in range(4)] for j in (4, 5)] + \
                 [[(j, m, kb) for m in range(2) for kb in range(2)] for j in (6, 8)] + \
                 [[(10, m, 0) for m in range(4)]]
        W_BANKS, Q_BANKS, C_BANKS = (4, 5, 2, 3), (4, 5, 0, 1), (4, 5, 6, 7)
        ORDER = list(range(6, 12)) + list(range(6))
        GROUPS = [6, 7, 8, 0, 1, 2, 3, 4, 5]
        BLOCK_AT = {b: (g, i) for g, bs in enumerate(BLOCKS) for i, b in enumerate(bs)}

        @block.sync
        def _(sp):
            def load(n, dn, src):
                if n >= RAW:
                    sp.wait_ge(lo_ready, n - RAW + 1 + dn)
                dst = raw[:, n % RAW, :]
                if len(src.shape) == 3:
                    dst = dst.rearrange("p (c n) -> p c n", c=src.shape[1])
                sp.dma_start(dst, src).then_inc(raw_full[n % RAW], 16)

            def cols(name, lo=None):
                v = t[name][0].rearrange("(c p) n -> p c n", p=P)
                return v[:, :, lo:lo + P] if lo is not None else v

            def rows(name):
                return t[name][0].rearrange("(j p) n -> p j n", p=P)

            for tt in range(NT):
                sp.dma_start(X[:, tt, :], t["x"][0, tt * P:(tt + 1) * P, :]).then_inc(x_in[tt], 16)
            sp.dma_start(CON[:, 0:N_FIRST], t["consts"][:, 0:N_FIRST]).then_inc(const_in, 16)
            sp.dma_start(FIRST, t["ffn1_norm"][0].rearrange("(a b) -> a b", b=P)).then_inc(first_in, 16)
            for n in range(RAW):
                load(n, 0, cols(("ffn1_w_gate", "ffn1_w_up")[n % 2], (n // 2) * P))
            def load_ffn(b, pre, first):
                g, u, d = pre + "_w_gate", pre + "_w_up", pre + "_w_down"
                for n, src in ((0, cols(g, 0)), (1, cols(u, 0)), (2, cols(g, P))):
                    if not first:
                        load(b + n, 0, src)
                with sp.Fori(0, 10) as i:
                    for k in range(2):
                        for m in range(3):
                            q = 3 * k + m
                            if m == 0:
                                src = cols(u)[:, :, bass.ds(i * (2 * P) + (k + 1) * P, P)]
                            elif m == 1:
                                src = rows(d)[:, bass.ds(i * 2 + k, 1), :]
                            else:
                                src = cols(g)[:, :, bass.ds(i * (2 * P) + (k + 2) * P, P)]
                            load(b + 3 + q, i * 6, src)
                load(b + 63, 0, cols(u, 21 * P))
                load(b + 64, 0, rows(d)[:, 20:21, :])
                load(b + 65, 0, rows(d)[:, 21:22, :])

            load_ffn(B_FFN1, "ffn1", True)
            for i, c in enumerate(WIN_COLS):
                load(B_WIN + i, 0, cols("w_in", c))
            for i, c in enumerate((4, 5, 6, 7, 0, 1, 2, 3)):
                load(B_WOUT + i, 0, rows("w_out")[:, c:c + 1, :])
            load_ffn(B_FFN2, "ffn2", False)
            sp.wait_ge(x_upd, 4 * 2)
            sp.dma_start(GFIN, t["final_norm"].rearrange("(a n) -> a n", a=1).broadcast_to([P,
                D])).then_inc(gain_in, 16)
            sp.dma_start(MEMX, t["mem_2"][0].rearrange("(a p) n -> p a n", p=P)).then_inc(mem_in, 16)
            sp.dma_start(POSI.bitcast(I32), t["positions_2"].broadcast_to([P, T])).then_inc(pos_in, 16)
            for k, name in enumerate(("lambda_q1_2", "lambda_k1_2", "lambda_q2_2", "lambda_k2_2")):
                sp.dma_start(LAMV[:, k, :], t[name].broadcast_to([P, 64])).then_inc(pos_in, 16)
            sp.dma_start(SNK, t["sinks_2"].broadcast_to([P, 8])).then_inc(pos_in, 16)
            for i in range(N_CKV):
                load(B_CKV + i, 0, cols("w_ckv_2", i * P))
            for i in range(N_WIN2):
                load(B_WIN2 + i, 0, cols("w_in_2", i * P))
            for c in range(KC):
                load(B_WOUT2 + c, 0, rows("w_out_2")[:, c:c + 1, :])
            for i in range(KC):
                load(B_CQ + i, 0, cols("w_cq_2", i * P))
            for c in range(KC):
                load(B_CO + c, 0, rows("w_co_2")[:, c:c + 1, :])
            load(B_MLP, 0, cols("w_up_2", 0))
            up, down = cols("w_up_2"), rows("w_down_2")
            with sp.Fori(0, 10) as i:
                for k in range(3):
                    load(B_MLP + 1 + 2 * k, i * 6, up[:, :, bass.ds(i * (3 * P) + (k + 1) * P, P)])
                    load(B_MLP + 2 + 2 * k, i * 6, down[:, bass.ds(i * 3 + k, 1), :])
            load(B_MLP + 61, 0, cols("w_up_2", 31 * P))
            load(B_MLP + 62, 0, down[:, 30:31, :])
            load(B_MLP + 63, 0, down[:, 31:32, :])
            sp.wait_ge(x_upd, 4 * 5)
            sp.dma_start(GFIN, t["g_final_2"].rearrange("(a n) -> a n", a=1).broadcast_to([P,
                D])).then_inc(gain_in, 16)
            for tt in range(NT):
                sp.wait_ge(x_upd, 4 * 8 - 2 + 2 * tt)
                sp.dma_start(out[0, tt * P:(tt + 1) * P, :], X[:, tt, :]).then_inc(out_done, 16)
            sp.wait_ge(out_done, 32)

        @block.tensor
        def _(pe):
            def mm(o, st, mv, start=True, stop=True):
                return pe.matmul(o, st, mv, start=start, stop=stop, skip_group_check=True)

            def a_unit(n, dn, bank, after=None):
                pe.wait_ge(lo_ready, n + 1 + dn)
                s = n % RING
                for c in range(KC):
                    if after and c % 2 == 0:
                        pe.wait_ge(xt_ready, 4 * NTP[after] + c // 2 + 1)
                    cs = slice(c * P, (c + 1) * P)
                    mm(bank[:, :], whi[:, s, cs], XT[:, c, :], start=(c == 0), stop=(c == KC - 1))
                    last = mm(bank[:, 0:T], wlo[:, s, cs], XT[:, c, 0:T], start=False, stop=(c == KC - 1))
                last.then_inc(unit_used, 1)

            def b_half(n, dn, act, tt, start=False, stop=False):
                pe.wait_ge(lo_ready, n + 1 + dn)
                s = n % RING
                hi = act[:, tt * P:(tt + 1) * P]
                lo = act[:, T + tt * P:T + (tt + 1) * P]
                for st, wt, a, z in ((hi, whi, start, False), (hi, wlo, False, False), (lo, whi, False, stop)):
                    for h in range(2):
                        last = mm(PS[2 * tt + h][:, :], st, wt[:, s, 512 * h:512 * h + 512], start=a, stop=z)
                if tt == NT - 1:
                    last.then_inc(unit_used, 1)
                return last

            def b_unit(n, dn, act, start=False, stop=False):
                for tt in range(NT):
                    last = b_half(n, dn, act, tt, start, stop)
                    if stop and tt == 0:
                        last.then_inc(half_used, 1)

            def norm_t(name):
                q = NTP[name]
                src = MEMX if name == "mem" else X
                for tt in range(NT):
                    pe.wait_ge(xn, 2 * q + tt + 1)
                    for b in range(4):
                        for c in (2 * b, 2 * b + 1):
                            last = mm(PS[4 + b][:, (c % 2) * T + tt * P:(c % 2) * T + (tt + 1) * P],
                                      src[:, tt, c * P:(c + 1) * P], DIAG[:, tt, :])
                        if tt == NT - 1:
                            last.then_inc(tp, 1)

            def ffn(b, f):
                J = FC * f

                def gate_up(j, n, dn=0, dj=0, after=None):
                    if J + j >= 2:
                        pe.wait_ge(h_ready, J + j - 1 + dj)
                    a_unit(b + n, dn, PS[4 + j % 2], after)
                    a_unit(b + n + 1, dn, PS[6 + j % 2])

                def down(j, n, dn=0, dj=0, **k):
                    pe.wait_ge(h_ready, J + j + 1 + dj)
                    b_unit(b + n, dn, H[:, j % 2, :], **k)

                gate_up(0, 0, after=("ffn1", "ffn2")[f])
                gate_up(1, 2)
                down(0, 4, start=True)
                with pe.Fori(0, 10) as i:
                    for k in range(2):
                        gate_up(2 + k, 5 + 3 * k, i * 6, i * 2)
                        down(1 + k, 7 + 3 * k, i * 6, i * 2)
                if f == 0:
                    pe.wait_ge(table_in, 16 * 4)
                    pe.wait_ge(rows_in, 16 * 17)
                    pe.wait_ge(h_ready, FC)
                    pe.transpose(PS[7][:, KC:N_VEC], ROWS[0:N_VEC - KC, :],
                                 ident[0:N_VEC - KC, 0:N_VEC - KC]).then_inc(vec_tp, 1)
                down(21, 65, stop=True)

            def mix():
                def lora(f):
                    fs = slice(f * P, (f + 1) * P)
                    pe.wait_ge(lora_act, 4)
                    if f >= 2:
                        pe.wait_ge(sa_done, f - 1)
                        pe.wait_ge(sg_done, f - 1)
                    wa, gate = PS[6 - 6 * (f % 2)], PS[7 - 6 * (f % 2)]
                    mm(wa[:, 0:T], LWA[:, 0, fs], LW[0:64, :])
                    mm(wa[:, T:2 * T], LWA[:, 1, fs], LW[0:64, :]).then_inc(lora_mm, 1)
                    mm(gate[:, 0:T], LWG[:, fs], LG[:, :]).then_inc(lora_mm, 1)

                def row_sums(bank, src, tiles, ready, n):
                    pe.wait_ge(ready, n)
                    for k, f in enumerate(tiles):
                        last = mm(bank[0:8, 0:T], heads(f), src[:, f, :], start=(k == 0), stop=(k == len(tiles) - 1))
                    return last

                def head_sums(src, ready, done):
                    pe.wait_ge(ready, NF)
                    for k in range(2):
                        mm(PS[6 + k][:, :], con("blk"), src[:, 2 * k:2 * k + 2, :]).then_inc(done, 1)

                pe.wait_ge(small_in, 16 * 5)
                pe.wait_ge(w_zero, 6)
                for i in range(N_WIN):
                    if i >= 4:
                        pe.wait_ge(w_sum, i - 3)
                    a_unit(B_WIN + i, 0, PS[W_BANKS[i % 4]], None if i else "mix")
                    if 4 <= i < 4 + NF:
                        lora(i - 4)
                    if i == 12:
                        pe.wait_ge(sa_done, NF - 1)
                        row_sums(PS[6], SQ, range(NF), sq_ready, NF).then_inc(ssq_mm, 1)
                    if i == 14:
                        pe.wait_ge(sg_done, NF)
                        pe.wait_ge(nrm_inv, 1)
                        for f in range(NF):
                            mm(PS[f // 2][:, (f % 2) * T:(f % 2 + 1) * T], spread(f), MXR).then_inc(nrm_mm, 1)
                        head_sums(DP, bp_ready, bp_mm)
                pe.wait_ge(w_sum, N_WIN)
                pe.wait_ge(w_mix, 14)
                for c in range(NT):
                    for f in range(NF):
                        last = pe.transpose(PS[2 + c][:, f * P:(f + 1) * P], PV[:, f, c * P:(c + 1) * P], ident)
                    last.then_inc(tok_mm, 1)
                pe.wait_ge(kk_ready, 1)
                pe.wait_ge(scaled, 2)
                for k, src in enumerate((AA, K2)):
                    for f in range(NF):
                        last = pe.transpose(PS[k][:, f * P:(f + 1) * P], src[:, f, 0:P], ident)
                    last.then_inc(tok_mm, 1)
                pe.wait_ge(bon_done, 1)
                fill = 0

                def fill_in():
                    nonlocal fill
                    n, tt = fill // 2, fill % 2
                    pe.wait_ge(yt_ready, n + 1)
                    b_half(B_WOUT + n, 0, XT[:, 4 + n, :], tt, start=(n % 2 == 0), stop=(n == 1))
                    fill += 1

                for wv in range(2):
                    if wv:
                        pe.wait_ge(s_y_ev, 1)
                        pe.wait_ge(s_s_ev, 1)
                        pe.wait_ge(s_u_ev, 2)
                    def products(g, h, bank, terms):
                        f, hp = 2 * wv + g, slice(64 * h, 64 * h + 64)
                        for k, (a, b) in enumerate(terms):
                            for c in range(NT):
                                m = 2 * k + c
                                last = mm(PS[bank][:, m * P:(m + 1) * P], a[hp, f, c * P:(c + 1) * P],
                                          b[hp, f, c * P:(c + 1) * P])
                        return last

                    for g in range(2):
                        for r, terms in enumerate((((AA, KK), (K2, KK)), ((KK, AA),))):
                            for h in range(2):
                                q = g * 4 + 2 * r + h
                                if q == 4 and wv:
                                    pe.wait_ge(mid_upd, 4)
                                elif q == 4:
                                    pe.wait_ge(tok_ev, 4)
                                products(g, h, (q + 4) % 8, terms).then_inc(m_mm, 1)
                    pe.wait_ge(m_ev, 8 * wv + 4)
                    for h in range(2):
                        products(0, h, 6 + h, ((AA, PR), (K2, PR))).then_inc(mm_mm, 1)
                    pe.wait_ge(m_ev, 8 * wv + 8)
                    for k in range(1, 7):
                        for g in range(2):
                            n = wv * 12 + (k - 1) * 2 + g
                            pe.wait_ge(inv_x, wv * 12 + (k - 1) * 2 + g + 1)
                            pe.wait_ge(levmask, n + 1)
                            M = mats[g]
                            for m in range(4):
                                last = mm(PS[3 * g][:, m * P:(m + 1) * P], M["LEV"][:, m, :], M["XM"][:, m, :])
                            last.then_inc(t_mm, 1)
                        for g in range(2):
                            n = wv * 12 + (k - 1) * 2 + g
                            pe.wait_ge(t_ev, n + 1)
                            pe.wait_ge(inv_ev, wv * 14 + (k - 1) * 2 + g + 1)
                            M = mats[g]
                            if k < 6:
                                for m in range(4):
                                    last = mm(PS[3 * g + 1][:, m * P:(m + 1) * P], M["XMT"][:, m, :],
                                              M["TS"][:, m, :])
                                last.then_inc(x_mm, 1)
                            for m in range(4):
                                last = mm(PS[3 * g + 2][:, m * P:(m + 1) * P], M["TS"][:, m, :], M["XMT"][:, m, :])
                            last.then_inc(inv_mm, 1)
                        if k == 1:
                            pe.wait_ge(mm_ev, 4 * wv + 2)
                            for h in range(2):
                                products(1, h, 6 + h, ((AA, PR), (K2, PR))).then_inc(mm_mm, 1)
                        if wv == 0 and k >= 5:
                            pe.wait_ge(mm_ev, 4)
                            for g in (2 * k - 10, 2 * k - 9):
                                pe.wait_ge(pooled, g + 1)
                                last = mm(PS[k + 1][:, (g % 2) * T:(g % 2 + 1) * T], WPL[:, g, :], window(g, PAD))
                            last.then_inc(pool_mm, 1)
                        if wv and k == 2:
                            pe.wait_ge(mm_ev, 8)
                            mm(PS[6][:, :], con("blk"), YO[:, 0:2, :]).then_inc(mean_mm, 1)
                        if wv and k == 4:
                            row_sums(PS[6], GV, (0, 1), gd_ready, 1).then_inc(var_mm, 1)
                    pe.wait_ge(inv_ev, wv * 14 + 14)
                    if wv:
                        pe.wait_ge(gn_std, 1)
                    else:
                        pe.wait_ge(yt_ready, 2)
                    pairs = [(g, hh) for g in range(2) for hh in range(2)]
                    for c in range(NT):
                        n = 2 * wv + c

                        def at(g, hh):
                            col = 64 * (2 * hh + g)
                            return 2 * wv + g, slice(64 * hh, 64 * hh + 64), slice(col, col + 64)

                        def vt(g, hh):
                            f = 2 * wv + g
                            return VTOK[:, c, f * P + 64 * hh:f * P + 64 * hh + 64]

                        if c:
                            pe.wait_ge(s_s_ev, wv + 1)
                        for hh in range(2):
                            for g in range(2):
                                f, hp, hc = at(g, hh)
                                o = PS[5 + hh][:, g * 64:g * 64 + 64]
                                if c:
                                    mm(o, KK[hp, f, P:2 * P], ST[hp, f, :], stop=False)
                                last = mm(o, mats[g]["LT"][:, hh, 2 + c, :], vt(g, hh), start=(c == 0))
                        last.then_inc(s_r_mm, 1)
                        if n == 2:
                            pe.wait_ge(gn_inv, 1)
                            for f in (0, 1):
                                last = mm(PS[4][:, f * T:(f + 1) * T], spread(f), GVR)
                            last.then_inc(gn_mm, 1)
                        fill_in()
                        pe.wait_ge(s_r_ev, n + 1)
                        if n == 0:
                            pe.wait_ge(yt_ready, 4)
                        for g, hh in pairs:
                            f, hp, hc = at(g, hh)
                            last = mm(PS[7][:, hc], mats[g]["XMT"][:, 2 * hh + c, :], RB[:, 2 * c, hc])
                        last.then_inc(s_u_mm, 1)
                        fill_in()
                        pe.wait_ge(s_u_ev, n + 1)
                        if c == 0:
                            for g, hh in pairs:
                                f, hp, hc = at(g, hh)
                                fc = slice(f * P + 64 * hh, f * P + 64 * hh + 64)
                                o = PS[7][hp, T + g * 64:T + g * 64 + 64]
                                mm(o, BTOK[:, fc], RB[:, 1, hc], stop=False)
                                last = mm(o, KTOK[:, fc], vt(g, hh), start=False)
                            last.then_inc(s_s_mm, 1)
                        if n == 2:
                            pe.wait_ge(gn_scaled, 1)
                        for g, hh in pairs:
                            f, hp, hc = at(g, hh)
                            o = PS[4][hp, g * T + c * P:g * T + (c + 1) * P]
                            if c:
                                mm(o, ST[hp, f, :], PR[hp, f, P:2 * P], stop=False)
                            mm(o, RB[:, 2 * c + 1, hc], mats[g]["MM"][:, hh, c, :], start=(c == 0), stop=False)
                            last = mm(o, vt(g, hh), mats[g]["MM"][:, hh, 2 + c, :], start=False)
                        if c:
                            last.then_inc(s_y_mm, 1)
                pe.wait_ge(s_y_ev, 2)
                mm(PS[6][:, :], con("blk"), YO[:, 2:4, :]).then_inc(mean_mm, 1)
                for step in range(4):
                    c, tt = step // 2, step % 2
                    pe.wait_ge(yt_ready, 4 + c + 1)
                    b_half(B_WOUT + 4 + c, 0, XT[:, c, :], tt)
                    if step == 0:
                        row_sums(PS[6], GV, (2, 3), gd_ready, 2).then_inc(var_mm, 1)
                    if step == 2:
                        pe.wait_ge(gn_inv, 2)
                        for f in (2, 3):
                            last = mm(PS[4][:, (f - 2) * T:(f - 1) * T], spread(f), GVR)
                        last.then_inc(gn_mm, 1)
                for c in (2, 3):
                    pe.wait_ge(yt_ready, 4 + c + 1)
                    b_unit(B_WOUT + 4 + c, 0, XT[:, c, :], stop=(c == NF - 1))

            def attention():
                norm_t("mem")

                def turn_value(i):
                    pe.wait_ge(c_sum, i + 1)
                    k = i - KC
                    if k >= 2:
                        pe.wait_ge(ct_ev, k - 1)
                    for tt in range(NT):
                        last = pe.transpose(PS[6 + i % 2][:, tt * P:(tt + 1) * P], CTM[:, i % 2, tt * P:(tt + 1) * P],
                                            ident)
                    last.then_inc(ct_mm, 1)

                for i in range(N_CKV):
                    if i == 2:
                        pe.wait_ge(x_upd, 4 * 3)
                    if i >= 4:
                        pe.wait_ge(c_sum, i - 3)
                    a_unit(B_CKV + i, 0, PS[Q_BANKS[i % 4]], None if i else "mem")
                    if i - 1 >= KC:
                        turn_value(i - 1)
                turn_value(N_CKV - 1)
                pe.wait_ge(ct_ev, KC)
                norm_t("mix2")

                n_rope = n_vt = 0
                for i in range(N_WIN2 + 1):
                    if i < N_WIN2:
                        if i >= 4:
                            pe.wait_ge(q_sum, i - 3)
                        a_unit(B_WIN2 + i, 0, PS[Q_BANKS[i % 4]], None if i else "mix2")
                    k = i - 1
                    if k < 0:
                        continue
                    pe.wait_ge(q_sum, k + 1)
                    if k == 5 or k >= 14:
                        if n_vt >= 2:
                            pe.wait_ge(vt_ev, n_vt - 1)
                        for tt in range(NT):
                            ts = slice(tt * P, (tt + 1) * P)
                            last = pe.transpose(PS[7 - 4 * (n_vt % 2)][:, ts], QKV[:, k, ts], ident)
                        last.then_inc(vt_mm, 1)
                        n_vt += 1
                    else:
                        if n_rope >= 2:
                            pe.wait_ge(rope_done, n_rope - 1)
                        mm(PS[6 - 4 * (n_rope % 2)][:, 0:T], con("swap32"), QKV[:, k, :]).then_inc(rope_mm, 1)
                        n_rope += 1
                pe.wait_ge(rope_done, n_rope)
                mm(PS[6][:, 0:T], con("swap64"), QKV[:, 4, :]).then_inc(rope_mm, 1)
                pe.wait_ge(rope_done, n_rope + 1)
                pe.wait_ge(vt_ev, 5)
                def scores(k):
                    j = ORDER[k]
                    kind, n, maps = JOBS[j]
                    if k >= 4:
                        pe.wait_ge(sc_sum, k - 3)
                    nk = (n + 1) * P
                    for m, h in enumerate(maps):
                        hp = slice(64 * (h % 2), 64 * (h % 2) + 64)
                        if kind == "swa":
                            q = QKV[hp, h // 2, n * P:(n + 1) * P]
                            kt = QKV[hp, 4, 0:nk] if h // 4 == h % 2 else KSW[hp, 0:nk]
                        else:
                            q, kt = QKV[hp, 6 + h // 2, n * P:(n + 1) * P], QKV[hp, 10 + h // 2, 0:nk]
                        last = mm(PS[k % 4][:, m * nk:(m + 1) * nk], q, kt)
                    last.then_inc(sc_mm, 1)

                def turn(k):
                    g = GROUPS[k]
                    last_job = max(j for j, m, kb in BLOCKS[g])
                    if last_job >= 6:
                        last_job += 1
                    pe.wait_ge(p_ready, ORDER.index(last_job) + 1)
                    if k >= 4:
                        pe.wait_ge(pt_ev, k - 3)
                    for i, (j, m, kb) in enumerate(BLOCKS[g]):
                        nk = (JOBS[j][1] + 1) * P
                        both = (j, j + 1) if j >= 6 else (j,)
                        for x in both:
                            last = mm(PS[4 + k % 4][:, i * P:(i + 1) * P],
                                      SC[:, x, m * nk + kb * P:m * nk + (kb + 1) * P], turner(x, m),
                                      start=(x == j), stop=(x == both[-1]))
                    last.then_inc(pt_mm, 1)

                def pt(j, m, kb):
                    g, i = BLOCK_AT[(j, m, kb)]
                    return PTS[:, g, i * P:(i + 1) * P]

                for k in range(9):
                    scores(k)
                for k in range(3):
                    turn(k)
                for k in range(9, 12):
                    scores(k)
                for k in range(3, 5):
                    turn(k)
                pe.wait_ge(sc_sum, 12)
                pe.wait_ge(pt_ev, 3)
                for n in range(NT):
                    for h in range(4):
                        o = PS[2 + n][:, h * P:(h + 1) * P]
                        vs = slice(P + h * P, P + (h + 1) * P)
                        if n == 0:
                            last = mm(o, pt(10, h, 0), VT2[:, 0, vs])
                        else:
                            mm(o, pt(6 + 2 * (h // 2), h % 2, 0), VT2[:, 0, vs], stop=False)
                            last = mm(o, pt(6 + 2 * (h // 2), h % 2, 1), VT2[:, 1, vs], start=False)
                    last.then_inc(pv_mm, 1)
                for k in range(5, 9):
                    turn(k)
                pe.wait_ge(pt_ev, 9)
                for h in range(8):
                    hp = slice(64 * (h % 2), 64 * (h % 2) + 64)
                    c, kv = h // 2, slice(64 * (h // 4), 64 * (h // 4) + 64)
                    o = PS[c // 2][hp, (c % 2) * T:(c % 2 + 1) * T]
                    j, m = 2 * (h % 2) + h // 4, (h // 2) % 2
                    mm(o[:, 0:P], VT2[:, 0, kv], pt(4 + h % 2, h // 2, 0))
                    mm(o[:, P:T], VT2[:, 0, kv], pt(j, m, 0), stop=False)
                    last = mm(o[:, P:T], VT2[:, 1, kv], pt(j, m, 1), start=False)
                    if h % 4 == 3:
                        last.then_inc(pv_mm, 1)
                for n in range(NT):
                    pe.wait_ge(od_norm, n + 1)
                for b in range(2):
                    for h in (2 * b, 2 * b + 1):
                        for n in range(NT):
                            last = pe.transpose(PS[4 + b][:, (h % 2) * T + n * P:(h % 2) * T + (n + 1) * P],
                                                ODN[:, n, h * P:(h + 1) * P], ident)
                    last.then_inc(odt_mm, 1)
                for c in range(KC):
                    pe.wait_ge(yt_ready, KC + max(4, c + 1))
                    b_unit(B_WOUT2 + c, 0, XT[:, c, :], start=(c == 0), stop=(c == KC - 1))

            def cross():
                norm_t("cross")
                for i in range(KC):
                    if i >= 4:
                        pe.wait_ge(c_sum, N_CKV + i - 3)
                    a_unit(B_CQ + i, 0, PS[C_BANKS[i % 4]], None if i else "cross")
                pe.wait_ge(x_upd, 4 * 5)
                for j in range(4):
                    n = j // 2
                    for m in range(2):
                        h = 2 * (j % 2) + m
                        pe.wait_ge(c_sum, N_CKV + 2 * h + 2)
                        for k in range(2):
                            last = mm(PS[j][:, m * T:(m + 1) * T], CQ[:, 2 * h + k, n * P:(n + 1) * P],
                                      CK[:, 2 * h + k, :], start=(k == 0), stop=(k == 1))
                    last.then_inc(sc_mm, 1)
                pe.wait_ge(c_sum, N_CKV + KC)
                for h in range(4):
                    pe.wait_ge(cp_ready, 3 + h // 2)
                    for kb in range(2):
                        for n in range(NT):
                            last = mm(PS[4 + h][:, kb * T + n * P:kb * T + (n + 1) * P],
                                      CSC[:, 2 * n + h // 2, (h % 2) * T + kb * P:(h % 2) * T + (kb + 1) * P],
                                      turner(6 + 2 * n + h // 2, h % 2))
                    last.then_inc(pt_mm, 1)
                for h in range(4):
                    pe.wait_ge(pt_ev, 9 + h + 1)
                    for d in range(2):
                        for kb in range(2):
                            vs = slice((2 * h + d) * P, (2 * h + d + 1) * P)
                            last = mm(PS[4 + h][:, d * T:(d + 1) * T], CVT[:, kb, vs],
                                      CPT[:, h, kb * T:(kb + 1) * T], start=(kb == 0), stop=(kb == 1))
                    last.then_inc(pv_mm, 1)
                pe.wait_ge(sc_exp, 12 + 4)
                for c in range(KC):
                    pe.wait_ge(yt_ready, 2 * KC + c + 1)
                    b_unit(B_CO + c, 0, XT[:, c, :], start=(c == 0), stop=(c == KC - 1))

            def mlp():
                def up(j, n, dn=0, dj=0, after=None):
                    if j >= 3:
                        pe.wait_ge(r_ready, j - 2 + dj)
                    a_unit(B_MLP + n, dn, PS[4 + j % 3], after)

                def down(j, n, dn=0, dj=0, **k):
                    pe.wait_ge(r_ready, j + 1 + dj)
                    b_unit(B_MLP + n, dn, H[:, j % 3, :], **k)

                up(0, 0, after="mlp")
                up(1, 1)
                down(0, 2, start=True)
                up(2, 3)
                down(1, 4)
                up(3, 5)
                down(2, 6)
                with pe.Fori(0, 9) as i:
                    for k in range(3):
                        up(4 + k, 7 + 2 * k, i * 6, i * 3)
                        down(3 + k, 8 + 2 * k, i * 6, i * 3)
                up(31, 61)
                down(30, 62)
                down(31, 63, stop=True)

            pe.wait_ge(const_in, 16)
            pe.wait_ge(first_in, 16)
            pe.transpose(PS[7][:, 0:KC], FIRST, ident[0:KC, 0:KC]).then_inc(vec_tp, 1)
            pe.wait_ge(vec_ready, 1)
            norm_t("ffn1")
            ffn(B_FFN1, 0)
            pe.wait_ge(vec_ready, 2)
            norm_t("mix")
            pe.wait_ge(x_upd, 4 * 1)
            mix()
            norm_t("ffn2")
            pe.wait_ge(x_upd, 4 * 2)
            ffn(B_FFN2, 1)
            attention()
            cross()
            norm_t("mlp")
            pe.wait_ge(x_upd, 4 * 6)
            mlp()

        @block.scalar
        def _(act):
            def split_hi(n, i=None):
                c = 16 * (n // RAW + 1)
                act.wait_ge(raw_full[n % RAW], c if i is None else i * (16 * RING // RAW) + c)
                if n >= RING:
                    act.wait_ge(unit_used, n - RING + 1 if i is None else i * RING + (n - RING + 1))
                act.activation(whi[:, n % RING, :], raw[:, n % RAW, :], ACT.Copy).then_inc(hi_ready, 1)

            splits = Count()

            def split_to(n):
                while splits.n < min(n, N_UNITS):
                    split_hi(splits.n)
                    splits.next()

            def norm_sums(q, src, upd):
                if q:
                    act.activation(SMALL[:, 346 + q:347 + q], con("eps"), ACT.Sqrt)
                for tt in range(NT):
                    if upd:
                        act.wait_ge(x_upd, 4 * (upd - 1) + 2 * tt + 2)
                    if q == 0:
                        act.wait_ge(x_in[tt], 16)
                    if q + tt:
                        act.wait_ge(ss, 2 * q + tt)
                    act.activation(SQJ, src[:, tt, :], ACT.Square, accum_out=SS[:, tt:tt + 1]).then_inc(ss, 1)
                    act.wait_ge(ss, 2 * q + tt + 1)
                    act.activation(MS[:, tt:tt + 1], SS[:, tt:tt + 1], ACT.Sqrt, scale=1.0 / D,
                                   bias=con("eps" if q in RMS_NORMS else "eps_block")).then_inc(rms, 1)

            def norm_hi(name, gain):
                q = NTP[name]
                for b in range(4):
                    act.wait_ge(tp, 4 * q + b + 1)
                    for c in (2 * b, 2 * b + 1):
                        ins = act.activation(XT[:, c, 0:T], PS[4 + b][:, (c % 2) * T:(c % 2 + 1) * T], ACT.Copy,
                            scale=vec(gain, c))
                        if c % 2:
                            ins.then_inc(xt_hi, 1)

            def ffn(b, f):
                J = FC * f

                def chunk(j, i=None):
                    dj, dn = (0, 0) if i is None else (i * 2, i * 6)
                    q = j % 2
                    n_gate, n_up = (0, 1) if j == 0 else (3 * j - 1, 3 * j)

                    def next_split(k):
                        n = b + 3 * j + 4 + k
                        if n < N_UNITS:
                            split_hi(n, i)
                            if i is None:
                                splits.n = n + 1

                    next_split(0)
                    act.wait_ge(unit_used, b + n_gate + 1 + dn)
                    if J + j >= 2:
                        act.wait_ge(g_sum, J + j - 1 + dj)
                    act.activation(GL[:, q, :], PS[4 + q][:, T:2 * T], ACT.Copy).then_inc(g_low, 1)
                    next_split(1)
                    act.wait_ge(unit_used, b + n_up + 1 + dn)
                    if J + j >= 2:
                        act.wait_ge(u_sum, J + j - 1 + dj)
                    act.activation(UL[:, q, :], PS[6 + q][:, T:2 * T], ACT.Copy).then_inc(u_low, 1)
                    act.wait_ge(g_sum, J + j + 1 + dj)
                    if J + j >= 2:
                        act.wait_ge(h_val, J + j - 1 + dj)
                    act.activation(SG[:, q, :], GS[:, q, :], ACT.Silu).then_inc(silu, 1)
                    act.wait_ge(h_val, J + j + 1 + dj)
                    if j >= 2:
                        act.wait_ge(unit_used, b + 3 * (j - 2) + 4 + 1 + dn)
                    act.activation(H[:, q, 0:T], HS[:, q, :], ACT.Copy).then_inc(h_hi, 1)
                    if j < FC - 1:
                        next_split(2)

                split_to(b + LEAD)
                chunk(0)
                chunk(1)
                with act.Fori(0, 9) as i:
                    for k in range(2):
                        chunk(2 + k, i)
                chunk(20)
                chunk(21)
                if f:
                    act.wait_ge(mem_in, 16)
                    norm_sums(3, MEMX, 0)

            def low(i, n, bank, dst, sem_low, sem_sum, base=0):
                split_to(n + LEAD + 1)
                act.wait_ge(unit_used, n + 1)
                if base + i >= 2:
                    act.wait_ge(sem_sum, base + i - 1)
                act.activation(dst[:, i % 2, :], bank[:, T:2 * T], ACT.Copy).then_inc(sem_low, 1)

            def deviation(wv):
                act.wait_ge(var_mm, wv + 1)
                act.activation(GVR, PS[6][0:8, 0:T], ACT.Sqrt, scale=1.0 / 64,
                               bias=con("eps_group", 8)).then_inc(gn_std, 1)

            def pool_upper(pair):
                for g in (2 * pair, 2 * pair + 1):
                    act.wait_ge(pool_mm, pair + 1)
                    act.activation(XT[:, 4 + g, 0:T], PS[6 + pair][:, (g % 2) * T:(g % 2 + 1) * T], ACT.Copy,
                                   scale=vec("pool_scale", g)).then_inc(pool_hi, 1)

            def y_upper(wv):
                for f in (2 * wv, 2 * wv + 1):
                    act.wait_ge(y_val, f + 1)
                    act.activation(XT[:, f, 0:T], YO[:, f, :], ACT.Copy).then_inc(y_hi, 1)

            def mix():
                for i in range(N_WIN):
                    low(i, B_WIN + i, PS[W_BANKS[i % 4]], WLOW, w_low, w_sum)
                    if i == 2:
                        act.wait_ge(w_mix, 2)
                        act.wait_ge(w_zero, 6)
                        act.activation(LW[0:32, :], LBUF[0:32, 0, :], ACT.Tanh).then_inc(lora_act, 1)
                        act.activation(LW[32:64, :], LBUF[32:64, 0, :], ACT.Copy).then_inc(lora_act, 1)
                        act.activation(LG[64:128, :], LBUF[64:128, 0, :], ACT.Sigmoid).then_inc(lora_act, 1)
                        act.activation(LG[0:32, :], LBUF[0:32, 1, :], ACT.Sigmoid).then_inc(lora_act, 1)
                    if 5 <= i < 5 + NF:
                        f = i - 5
                        wa, gate = PS[6 - 6 * (f % 2)], PS[7 - 6 * (f % 2)]
                        act.wait_ge(lora_mm, 2 * f + 1)
                        act.activation(SW[:, f, :], wa[:, 0:T], ACT.Sigmoid, bias=vec("w0",
                            f)).then_inc(sw_done, 1)
                        act.activation(AA[:, f, :], wa[:, T:2 * T], ACT.Sigmoid, bias=vec("a0",
                            f)).then_inc(sa_done, 1)
                        act.wait_ge(lora_mm, 2 * f + 2)
                        act.activation(GG[:, f, :], gate[:, 0:T], ACT.Copy).then_inc(sg_done, 1)
                    if i == 10:
                        act.wait_ge(w_mix, 10)
                        act.wait_ge(sa_done, NF)
                        act.wait_ge(omk_ready, 1)
                        for f in range(NF):
                            act.activation(SQ[:, f, :], PK[:, f, :], ACT.Square,
                                           scale=vec("k_k", f)).then_inc(sq_ready, 1)
                        for f in range(NF):
                            act.activation(EC[:, f, :], AA[:, f, :], ACT.Identity, scale=vec("k_a", f),
                                           bias=OMK[:, f:f + 1]).then_inc(ec_base, 1)
                        for f in range(NF):
                            act.activation(KK[:, f, :], PK[:, f, :], ACT.Copy,
                                           scale=vec("k_k", f)).then_inc(ec_base, 1)
                    if i == 12:
                        act.wait_ge(ssq_mm, 1)
                        act.activation(MXR, PS[6][0:8, 0:T], ACT.Sqrt).then_inc(nrm_done, 1)
                    if i == 13:
                        act.wait_ge(ec_ready, 2)
                        act.wait_ge(ssq_mm, 1)
                        act.activation(IP[:, :, :], CC[:, :, :], ACT.Exp, scale=-LN_DECAY).then_inc(dec_done, 1)
                        act.activation(EC[:, :, :], EC[:, :, :], ACT.Exp, scale=LN_DECAY).then_inc(dec_done, 1)
                        act.activation(CC[:, :, :], CC[:, :, :], ACT.Exp, scale=LN_DECAY).then_inc(dec_done, 1)
                        act.activation(FAC, FAC, ACT.Exp, scale=LN_DECAY).then_inc(dec_done, 1)
                act.wait_ge(kk_ready, 1)
                for b, dst in enumerate((VTOK[:, 0, :], VTOK[:, 1, :], BTOK, KTOK)):
                    act.wait_ge(tok_mm, b + 1)
                    act.activation(dst, PS[(b + 2) % 4][:, :], ACT.Copy).then_inc(tok_ev, 1)
                for wv in range(2):
                    for k in range(1, 7):
                        for g in range(2):
                            n = wv * 12 + (k - 1) * 2 + g
                            act.wait_ge(t_mm, n + 1)
                            if n >= 2:
                                act.wait_ge(inv_mm, n - 1)
                            act.activation(mats[g]["TS"][:, :, :], PS[3 * g][:, :].rearrange("p (a b) -> p a b",
                                a=4), ACT.Copy).then_inc(t_ev, 1)
                        if k == 1:
                            split_to(B_WOUT + 2 * wv + RING)
                        if wv and k == 5:
                            deviation(0)
                        if wv == 0 and k == 6:
                            pool_upper(0)
                    if wv == 0:
                        pool_upper(1)
                    for c in range(NT):
                        n = 2 * wv + c
                        act.wait_ge(s_r_mm, n + 1)
                        act.activation(RB[:, 2 * c, 0:P], PS[5][:, 0:P], ACT.Copy)
                        act.activation(RB[:, 2 * c, P:2 * P], PS[6][:, 0:P], ACT.Copy).then_inc(s_r_ev, 1)
                        act.wait_ge(s_u_mm, n + 1)
                        act.activation(RB[:, 2 * c + 1, :], PS[7][:, 0:T], ACT.Copy).then_inc(s_u_ev, 1)
                        if wv and c == 0:
                            y_upper(0)
                    act.wait_ge(s_y_mm, wv + 1)
                    act.activation(YO[:, 2 * wv:2 * wv + 2, :], PS[4][:, :].rearrange("p (a b) -> p a b", a=2),
                        ACT.Copy).then_inc(s_y_ev, 1)
                act.activation(SMALL[:, 356:357], WARM, ACT.Sqrt)
                deviation(1)
                y_upper(1)
                for c in range(KC - 1):
                    split_to(B_WOUT + c + LEAD + 1)

            def attention():
                split_to(B_CKV + LEAD)
                norm_hi("mem", "g_mem_2")
                norm_sums(4, X, 3)
                for i in range(N_CKV):
                    low(i, B_CKV + i, PS[Q_BANKS[i % 4]], CLOW, c_low, c_sum)
                    if i == 2:
                        norm_sums(5, X, 4)
                    if i - 2 >= KC:
                        value(i - 2)
                for i in (N_CKV - 2, N_CKV - 1):
                    value(i)
                norm_hi("mix2", "g_mix_2")
                n_vt = 0
                for i in range(N_WIN2 + 1):
                    if i < N_WIN2:
                        low(i, B_WIN2 + i, PS[Q_BANKS[i % 4]], CLOW, q_low, q_sum)
                    if i == 1:
                        act.wait_ge(rope_arg, 1)
                        act.activation(RC, RA[0], ACT.Sin).then_inc(rope_tab, 1)
                        act.activation(RSN, RA[1], ACT.Sin).then_inc(rope_tab, 1)
                        act.wait_ge(lam_arg, 1)
                        act.activation(LEXP, LDOT, ACT.Exp).then_inc(lam_exp, 1)
                    k = i - 1
                    if k == 5 or k >= 14:
                        act.wait_ge(vt_mm, n_vt + 1)
                        act.activation(VT2[:, :, n_vt * P:(n_vt + 1) * P], PS[7 - 4 * (n_vt % 2)][:,
                            0:T].rearrange("p (a b) -> p a b", a=NT), ACT.Copy).then_inc(vt_ev, 1)
                        n_vt += 1
                split_to(B_WOUT2 + RING)

                def exponents(k):
                    j = ORDER[k]
                    kind, n, maps = JOBS[j]
                    act.wait_ge(sc_max, k + 1)
                    nk = (n + 1) * P
                    for m in range(len(maps)):
                        e = SC[:, j, m * nk:(m + 1) * nk]
                        q = 4 * j + m
                        done = m == len(maps) - 1 and kind == "diff"
                        ins = act.activation(e, e, ACT.Exp, bias=NMX[:, q:q + 1], accum_out=SUM[:, q:q + 1])
                        if done:
                            ins.then_inc(sc_exp, 1)
                    if kind == "swa":
                        q = slice(4 * j, 4 * j + len(maps))
                        act.activation(ESK[:, q], ESK[:, q], ACT.Exp).then_inc(sc_exp, 1)

                def turned(k):
                    act.wait_ge(pt_mm, k + 1)
                    act.activation(PTS[:, GROUPS[k], :], PS[4 + k % 4][:, :], ACT.Copy).then_inc(pt_ev, 1)

                for k in range(9):
                    exponents(k)
                for k in range(3):
                    turned(k)
                for k in range(9, 12):
                    exponents(k)
                for k in range(3, 5):
                    turned(k)
                for n in range(NT):
                    act.wait_ge(pv_mm, 1 + n)
                    for h in range(4):
                        ins = act.activation(ODJ[:, (4 * n + h) * P:(4 * n + h + 1) * P], PS[2 + n][:,
                            h * P:(h + 1) * P], ACT.Square, accum_out=ODS[:, 4 * n + h:4 * n + h + 1])
                        if h == 3:
                            ins.then_inc(od_ss, 1)
                for k in range(5, 9):
                    turned(k)
                act.wait_ge(od_ss, 2)
                act.activation(ODS, ODS, ACT.Sqrt, scale=1.0 / P, bias=con("eps_block")).then_inc(od_std, 1)
                for c in range(4):
                    act.wait_ge(pv_mm, 2 + c // 2 + 1)
                    ins = act.activation(XT[:, c, 0:T], PS[c // 2][:, (c % 2) * T:(c % 2 + 1) * T], ACT.Copy)
                    if c % 2:
                        ins.then_inc(o_hi, 1)
                for h in range(4):
                    act.wait_ge(odt_mm, h // 2 + 1)
                    ins = act.activation(XT[:, 4 + h, 0:T], PS[4 + h // 2][:, (h % 2) * T:(h % 2 + 1) * T], ACT.Copy,
                        scale=GD8)
                    if h % 2:
                        ins.then_inc(o_hi, 1)
                for c in range(KC - 1):
                    split_to(B_WOUT2 + c + LEAD + 1)

            def value(i):
                k = i - KC
                act.wait_ge(ct_mm, k + 1)
                act.activation(CVT[:, :, k * P:(k + 1) * P], PS[6 + i % 2][:, 0:T].rearrange("p (a b) -> p a b",
                    a=NT), ACT.Copy).then_inc(ct_ev, 1)

            def cross():
                norm_sums(6, X, 5)
                split_to(B_CQ + LEAD)
                norm_hi("cross", "g_cross_2")
                for i in range(KC):
                    low(i, B_CQ + i, PS[C_BANKS[i % 4]], CLOW, c_low, c_sum, N_CKV)
                split_to(B_CO + RING)
                for j in range(4):
                    act.wait_ge(sc_max, 12 + j + 1)
                    for m in range(2):
                        e, q = CSC[:, j, m * T:(m + 1) * T], 2 * j + m
                        ins = act.activation(e, PS[j][:, m * T:(m + 1) * T], ACT.Exp, scale=1.0 / 16,
                                             bias=CNM[:, q:q + 1], accum_out=CSUM[:, q:q + 1])
                        if m:
                            ins.then_inc(sc_exp, 1)
                for h in range(4):
                    act.wait_ge(pt_mm, 9 + h + 1)
                    act.activation(CPT[:, h, :], PS[4 + h][:, :], ACT.Copy).then_inc(pt_ev, 1)
                for h in range(4):
                    act.wait_ge(pv_mm, 4 + h + 1)
                    for d in range(2):
                        ins = act.activation(XT[:, 2 * h + d, 0:T], PS[4 + h][:, d * T:(d + 1) * T], ACT.Copy)
                        if d:
                            ins.then_inc(o_hi, 1)
                for c in range(KC - 1):
                    split_to(B_CO + c + LEAD + 1)

            def mlp():
                def chunk(j, i=None):
                    dj, dn = (0, 0) if i is None else (i * 3, i * 6)
                    q = j % 3

                    def next_split(k):
                        n = B_MLP + 2 * j + LEAD + k
                        if n < N_UNITS:
                            split_hi(n, i)

                    next_split(0)
                    act.wait_ge(unit_used, B_MLP + max(0, 2 * j - 1) + 1 + dn)
                    if j >= 3:
                        act.wait_ge(r_sum, j - 2 + dj)
                    act.activation(UL[:, q, :], PS[4 + q][:, T:2 * T], ACT.Copy).then_inc(r_low, 1)
                    act.wait_ge(h_val, 2 * FC + j + 1 + dj)
                    if j >= 3:
                        act.wait_ge(unit_used, B_MLP + 2 * (j - 3) + 2 + 1 + dn)
                    act.activation(H[:, q, 0:T], HS[:, q, :], ACT.Copy).then_inc(r_hi, 1)
                    next_split(1)

                split_to(B_MLP + LEAD)
                for j in range(3):
                    chunk(j)
                with act.Fori(0, 9) as i:
                    for k in range(3):
                        chunk(3 + k, i)
                for j in (30, 31):
                    chunk(j)

            act.wait_ge(warm_set, 1)
            act.activation(SMALL[:, 346:347], WARM, ACT.Sqrt)
            act.wait_ge(const_in, 16)
            norm_sums(0, X, 0)
            split_to(2)
            act.wait_ge(vec_ready, 1)
            norm_hi("ffn1", "ffn1_norm")
            ffn(B_FFN1, 0)
            norm_sums(1, X, 1)
            act.wait_ge(vec_ready, 2)
            split_to(B_WIN + LEAD)
            norm_hi("mix", "mix_norm")
            mix()
            norm_sums(2, X, 2)
            split_to(B_FFN2 + LEAD)
            norm_hi("ffn2", "ffn2_norm")
            ffn(B_FFN2, 1)
            attention()
            cross()
            norm_sums(7, X, 6)
            norm_hi("mlp", "g_mlp_2")
            mlp()
            norm_sums(8, X, 7)

        @block.vector
        def _(dve):
            own = Count()

            add, sub, mul, mx, mn = ALU.add, ALU.subtract, ALU.mult, ALU.max, ALU.min

            def split_lo(n, i=None):
                dve.wait_ge(hi_ready, n + 1 if i is None else i * RING + (n + 1))
                if n >= RING:
                    dve.wait_ge(unit_used, n - RING + 1 if i is None else i * RING + (n - RING + 1))
                dve.tensor_tensor(wlo[:, n % RING, :], raw[:, n % RAW, :], whi[:, n % RING, :].bitcast(F32),
                    sub).then_inc(lo_ready, 1)

            splits = Count()

            def split_to(n):
                while splits.n < min(n, N_UNITS):
                    split_lo(splits.n)
                    splits.next()

            def norm(q, in_place=False):
                for tt in range(NT):
                    dve.wait_ge(rms, 2 * q + tt + 1)
                    dve.reciprocal(RR[:, tt:tt + 1], MS[:, tt:tt + 1]).then_inc(own_dve, own.next())
                    dve.wait_ge(own_dve, own.n)
                    if in_place:
                        for h in range(2):
                            xs, hs = X[:, tt, 512 * h:512 * h + 512], slice(512 * h, 512 * h + 512)
                            dve.scalar_tensor_tensor(xs, xs, RR[:, tt:tt + 1], GFIN[:, hs], mul,
                                mul).then_inc(x_upd, 1)
                    else:
                        dve.tensor_scalar(DIAG[:, tt, :], ident, RR[:, tt:tt + 1], None, mul).then_inc(xn, 1)

            def rest(c, ps, scale=None):
                hi = XT[:, c, 0:T].bitcast(F32)
                if scale is None:
                    return dve.tensor_tensor(XT[:, c, T:2 * T], ps, hi, sub)
                return dve.scalar_tensor_tensor(XT[:, c, T:2 * T], ps, scale, hi, mul, sub)

            def norm_lo(name, gain):
                q = NTP[name]
                for b in range(4):
                    dve.wait_ge(xt_hi, 4 * q + b + 1)
                    for c in (2 * b, 2 * b + 1):
                        ins = rest(c, PS[4 + b][:, (c % 2) * T:(c % 2 + 1) * T], vec(gain, c))
                    ins.then_inc(xt_ready, 1)

            def update_x(nth, end, factor):
                dve.wait_ge(half_used, nth)
                if nth == 2:
                    dve.wait_ge(mid_upd, 4)
                for k in range(4):
                    if k == 2:
                        dve.wait_ge(unit_used, end)
                    xs = X[:, k // 2, (k % 2) * 512:(k % 2 + 1) * 512]
                    dve.scalar_tensor_tensor(xs, PS[k][:, :], factor, xs, mul, add).then_inc(x_upd, 1)

            def ffn(b, f):
                J = FC * f

                def chunk(j, i=None):
                    dj = 0 if i is None else i * 2
                    q = j % 2

                    def next_split(k):
                        n = b + 3 * j + 4 + k
                        if n < N_UNITS:
                            split_lo(n, i)
                            if i is None:
                                splits.n = n + 1

                    next_split(0)
                    dve.wait_ge(g_low, J + j + 1 + dj)
                    dve.tensor_tensor(GS[:, q, :], PS[4 + q][:, 0:T], GL[:, q, :], add).then_inc(g_sum, 1)
                    next_split(1)
                    dve.wait_ge(u_low, J + j + 1 + dj)
                    dve.tensor_tensor(US[:, q, :], PS[6 + q][:, 0:T], UL[:, q, :], add).then_inc(u_sum, 1)
                    dve.wait_ge(u_sum, J + j + 1 + dj)
                    dve.wait_ge(silu, J + j + 1 + dj)
                    dve.tensor_tensor(HS[:, q, :], SG[:, q, :], US[:, q, :], mul).then_inc(h_val, 1)
                    dve.wait_ge(h_val, J + j + 1 + dj)
                    dve.wait_ge(h_hi, J + j + 1 + dj)
                    dve.tensor_tensor(H[:, q, T:2 * T], HS[:, q, :], H[:, q, 0:T].bitcast(F32),
                        sub).then_inc(h_ready, 1)
                    if j < FC - 1:
                        next_split(2)

                split_to(b + LEAD)
                chunk(0)
                chunk(1)
                with dve.Fori(0, 9) as i:
                    for k in range(2):
                        chunk(2 + k, i)
                chunk(20)
                chunk(21)
                if f == 0:
                    dve.wait_ge(vec_tp, 2)
                    dve.tensor_copy(VEC[:, KC:N_VEC], PS[7][:, KC:N_VEC]).then_inc(vec_ready, 1)
                if f:
                    norm(3)
                update_x(2 * f + 1, b + 66, 0.5)

            def mix():
                CC8 = CC.rearrange("p f (c s) -> p (f c) s", c=2)
                ka = VEC_ROWS["k_a"]
                dve.tensor_scalar(OMK, VEC[:, ka:ka + NF], -1.0, 1.0, mul, add).then_inc(omk_ready, 1)
                for i, col in enumerate(WIN_COLS):
                    n = B_WIN + i
                    split_to(n + LEAD + 1)
                    dve.wait_ge(w_low, i + 1)
                    ps, low = PS[W_BANKS[i % 4]][:, 0:T], WLOW[:, i % 2, :]
                    if i >= 14:
                        dve.tensor_tensor(PP[:, i - 14, PAD:], ps, low, add).then_inc(w_sum, 1)
                    else:
                        dst = LBUF[:, i, :] if i < 2 else PV[:, i - 10, :] if i >= 10 else \
                            (PK, PR)[i % 2][:, (i - 2) // 2, :]
                        mu = vec("mu_tail") if i == 1 else vec("mu_shift", col // P)
                        now, before = WRAW[:, i % 2, 1:T + 1], WRAW[:, i % 2, 0:T]
                        if i == 0:
                            dve.wait_ge(w_zero, 6)
                        dve.tensor_tensor(now, ps, low, add).then_inc(w_sum, 1)
                        dve.wait_ge(w_sum, i + 1)
                        dve.tensor_tensor(WDF[:, i % 2, :], before, now, sub).then_inc(own_dve, own.next())
                        dve.wait_ge(own_dve, own.n)
                        dve.scalar_tensor_tensor(dst, WDF[:, i % 2, :], mu, now, mul, add).then_inc(w_mix, 1)
                    if i == 9:
                        dve.wait_ge(sw_done, NF)
                        for f in range(NF):
                            for c in range(NT):
                                cs = slice(c * P, (c + 1) * P)
                                dve.tensor_tensor_scan(CC[:, f, cs], SW[:, f, cs], SW[:, f, cs], 0.0, add,
                                    mx).then_inc(own_dve, own.next())
                        dve.wait_ge(own_dve, own.n)
                        dve.tensor_copy(CM, CC8[:, :, P // 2 - 1]).then_inc(own_dve, own.next())
                        dve.wait_ge(own_dve, own.n)
                        for k in range(2 * NF):
                            dve.tensor_scalar(CC8[:, k, :], CC8[:, k, :], CM[:, k:k + 1], None,
                                sub).then_inc(own_dve, own.next())
                    if i == 11:
                        dve.wait_ge(ec_base, 2 * NF)
                        dve.wait_ge(own_dve, own.n)
                        dve.tensor_tensor(K2, EC, PK, mul).then_inc(k2_ready, 1)
                    if i == 12:
                        dve.wait_ge(nrm_done, 1)
                        dve.tensor_scalar(MXR, MXR, L2_EPS, None, mx).then_inc(own_dve, own.next())
                        dve.wait_ge(own_dve, own.n)
                        dve.reciprocal(MXR, MXR).then_inc(nrm_inv, 1)
                        dve.wait_ge(k2_ready, 1)
                        for f in range(NF):
                            dve.scalar_tensor_tensor(DP[:, f, :], PR[:, f, :], vec("r_k", f), K2[:, f, :], mul,
                                mul).then_inc(bp_ready, 1)
                    if i == 14:
                        for k in range(2):
                            dve.wait_ge(nrm_mm, 2 * k + 2)
                            dve.tensor_tensor(KK[:, 2 * k:2 * k + 2, :], PS[k][:, :].rearrange("p (a b) -> p a b",
                                a=2), KK[:, 2 * k:2 * k + 2, :], mul).then_inc(own_dve, own.next())
                        dve.wait_ge(own_dve, own.n)
                        dve.tensor_tensor(AA, AA, KK, mul).then_inc(own_dve, own.next())
                        dve.wait_ge(dec_done, 3)
                        dve.wait_ge(own_dve, own.n)
                        dve.tensor_tensor(AA, AA, IP, mul).then_inc(own_dve, own.next())
                        dve.scalar_tensor_tensor(KK, KK, -1.0, EC, mul, mul).then_inc(kk_ready, 1)
                dve.wait_ge(w_mix, 14)
                for k in range(2):
                    dve.wait_ge(bp_mm, k + 1)
                    ins = dve.tensor_tensor(BON[:, 2 * k:2 * k + 2, :], PS[6 + k][:, :].rearrange("p (a b) -> p a b",
                        a=2), PV[:, 2 * k:2 * k + 2, :], mul)
                    if k:
                        ins.then_inc(bon_done, 1)
                    else:
                        ins.then_inc(own_dve, own.next())

                def window_sum(k):
                    n, first = 1 << k, k - k % 2
                    dst = PB[k % 2][:, first:, 2 * n - 1:]
                    if k == 0:
                        src = PP
                    else:
                        src = PB[1 - k % 2][:, k - (1 - k % 2):, :]
                    dve.wait_ge(own_dve, own.n)
                    dve.tensor_tensor(dst, src[:, :, 2 * n - 1:], src[:, :, n - 1:PAD + T - n],
                                      add).then_inc(own_dve, own.next())

                def window_mean(g):
                    win = WINDOWS[g]
                    s, first = window(g, PAD), window(g, PAD, PAD + win)
                    pp = PP[:, g:g + 1, PAD:]
                    a = CONST_COLS["invc"][0] + g * PAD
                    dve.wait_ge(own_dve, own.n)
                    if g:
                        dve.wait_ge(pooled, g)
                    tm = PTM[:, 0:win].rearrange("p (a b) -> p a b", a=1)
                    dve.tensor_tensor(tm, first, CON[:, a:a + win].rearrange("p (a b) -> p a b", a=1),
                                      mul).then_inc(own_dve, own.next())
                    dve.wait_ge(own_dve, own.n)
                    dve.scalar_tensor_tensor(s, s, 1.0 / win, pp, mul, sub).then_inc(own_dve, own.next())
                    dve.wait_ge(own_dve, own.n)
                    dve.tensor_tensor(first, tm, pp[:, :, 0:win], sub).then_inc(pooled, 1)

                def centre(k):
                    fs = slice(2 * k, 2 * k + 2)
                    dve.wait_ge(mean_mm, k + 1)
                    dve.scalar_tensor_tensor(YO[:, fs, :], PS[6][:, :].rearrange("p (a b) -> p a b", a=2),
                        -1.0 / 64, YO[:, fs, :], mul, add).then_inc(own_dve, own.next())
                    dve.wait_ge(own_dve, own.n)
                    dve.tensor_tensor(GV[:, fs, :], YO[:, fs, :], YO[:, fs, :], mul).then_inc(gd_ready, 1)

                def invert(k):
                    dve.wait_ge(gn_std, k + 1)
                    dve.reciprocal(GVR, GVR).then_inc(gn_inv, 1)

                def outputs(k):
                    dve.wait_ge(gn_mm, k + 1)
                    for f in (2 * k, 2 * k + 1):
                        ins = dve.scalar_tensor_tensor(YO[:, f, :], PS[4][:, (f % 2) * T:(f % 2 + 1) * T],
                            vec("ln_w", f), YO[:, f, :], mul, mul)
                        if f % 2:
                            ins.then_inc(gn_scaled, 1)
                        else:
                            ins.then_inc(own_dve, own.next())
                    dve.wait_ge(gn_scaled, k + 1)
                    dve.wait_ge(own_dve, own.n)
                    for f in (2 * k, 2 * k + 1):
                        dve.scalar_tensor_tensor(YO[:, f, :], YO[:, f, :], vec("ln_b", f), BON[:, f, :], add,
                            add).then_inc(own_dve, own.next())
                    dve.wait_ge(own_dve, own.n)
                    for f in (2 * k, 2 * k + 1):
                        dve.tensor_tensor(YO[:, f, :], YO[:, f, :], GG[:, f, :], mul).then_inc(y_val, 1)

                def lower(k):
                    for f in (2 * k, 2 * k + 1):
                        dve.wait_ge(y_hi, f + 1)
                        rest(f, YO[:, f, :]).then_inc(yt_ready, 1)

                for wv in range(2):
                    for g in range(2):
                        M = mats[g]
                        for h in range(2):
                            dve.wait_ge(m_mm, 8 * wv + 4 * g + h + 1)
                            dve.tensor_tensor(M["LT"][:, h, :, :], PS[(4 * g + h + 4) % 8][:,
                                :].rearrange("p (a b) -> p a b", a=4), bc(con("lt"), 4), mul).then_inc(m_ev, 1)
                        for h in range(2):
                            dve.wait_ge(m_mm, 8 * wv + 4 * g + 2 + h + 1)
                            dve.tensor_tensor(M["XM"][:, 2 * h:2 * h + 2, :], PS[(4 * g + 2 + h + 4) % 8][:,
                                0:T].rearrange("p (a b) -> p a b", a=2), bc(con("lev0"), 2), mul).then_inc(m_ev, 1)
                        dve.wait_ge(m_ev, 8 * wv + 4 * g + 4)
                        for h in range(2):
                            dve.tensor_tensor(M["XMT"][:, 2 * h:2 * h + 2, :], M["LT"][:, h, 0:2, :],
                                bc(con("lev0t"), 2), mul).then_inc(own_dve, own.next())
                        dve.tensor_tensor(M["XM"][:, :, :], M["XM"][:, :, :], bc(ident, 4),
                            add).then_inc(inv_x, 1)
                        dve.wait_ge(own_dve, own.n)
                        dve.tensor_tensor(M["XMT"][:, :, :], M["XMT"][:, :, :], bc(ident, 4),
                            add).then_inc(inv_ev, 1)

                    def outward(g):
                        for h in range(2):
                            dve.wait_ge(mm_mm, 4 * wv + 2 * g + h + 1)
                            dve.tensor_tensor(mats[g]["MM"][:, h, :, :], PS[6 + h][:,
                                :].rearrange("p (a b) -> p a b", a=4), bc(con("le"), 4), mul).then_inc(mm_ev, 1)

                    outward(0)
                    for k in range(1, 7):
                        for g in range(2):
                            M = mats[g]
                            psx, psxt = (PS[3 * g + n][:, :].rearrange("p (a b) -> p a b", a=4) for n in (1, 2))
                            if k < 6:
                                dve.wait_ge(x_mm, wv * 10 + (k - 1) * 2 + g + 1)
                                dve.tensor_tensor(M["XM"], psx, M["XM"], add).then_inc(inv_x, 1)
                            dve.wait_ge(inv_mm, wv * 12 + (k - 1) * 2 + g + 1)
                            dve.tensor_tensor(M["XMT"], psxt, M["XMT"], add).then_inc(inv_ev, 1)
                        if k == 1:
                            outward(1)
                            split_to(B_WOUT + 2 * wv + RING)
                        if wv == 0:
                            if k == 1:
                                dve.wait_ge(scaled, 2)
                            if k <= 4:
                                window_sum(k - 1)
                            if 2 <= k <= 5:
                                window_mean(k - 2)
                        elif k == 3:
                            centre(0)
                        elif k == 5:
                            invert(0)
                        elif k == 6:
                            outputs(0)
                    if wv == 0:
                        for g in range(NF):
                            dve.wait_ge(pool_hi, 2 * (g // 2) + 2)
                            rest(4 + g, PS[6 + g // 2][:, (g % 2) * T:(g % 2 + 1) * T],
                                 vec("pool_scale", g)).then_inc(yt_ready, 1)
                    dve.wait_ge(s_s_mm, wv + 1)
                    dve.wait_ge(dec_done, 4)
                    for g in range(2):
                        f = 2 * wv + g
                        ins = dve.tensor_scalar(ST[:, f, :], PS[7][:, T + g * 64:T + g * 64 + 64],
                            FAC[:, f:f + 1], None, mul)
                        if g:
                            ins.then_inc(s_s_ev, 1)
                        else:
                            ins.then_inc(own_dve, own.next())
                    if wv:
                        lower(0)
                    else:
                        dve.wait_ge(unit_used, B_WOUT + 2)
                        for k in range(4):
                            xs = X[:, k // 2, (k % 2) * 512:(k % 2 + 1) * 512]
                            dve.tensor_tensor(xs, PS[k][:, :], xs, add).then_inc(mid_upd, 1)
                centre(1)
                invert(1)
                outputs(1)
                lower(1)
                for c in range(KC - 1):
                    split_to(B_WOUT + c + LEAD + 1)
                update_x(2, B_WOUT + KC, 1.0)

            def rope_args():
                C1, big = 6.28125, 12582912.0
                C2 = float(np.float32(2 * math.pi - C1))
                dve.wait_ge(pos_in, 16 * 6)
                dve.tensor_copy(POSF, POSI.bitcast(I32)).then_inc(own_dve, own.next())
                dve.wait_ge(own_dve, own.n)
                dve.tensor_scalar(ANG, POSF, con("freq"), None, mul).then_inc(own_dve, own.next())
                dve.wait_ge(own_dve, own.n)
                for k, turn in ((0, 0.25), (1, 0.0)):
                    dve.tensor_scalar(RA[k], ANG, 1.0 / (2 * math.pi), turn, mul, add).then_inc(own_dve,
                        own.next())
                    dve.wait_ge(own_dve, own.n)
                    dve.tensor_scalar(RA[k], RA[k], big, -big, add, add).then_inc(own_dve, own.next())
                    dve.wait_ge(own_dve, own.n)
                    dve.scalar_tensor_tensor(RA[2 + k], RA[k], -C1, ANG, mul, add).then_inc(own_dve, own.next())
                    dve.wait_ge(own_dve, own.n)
                    dve.scalar_tensor_tensor(RA[2 + k], RA[k], -C2, RA[2 + k], mul, add).then_inc(own_dve,
                        own.next())
                    dve.wait_ge(own_dve, own.n)
                    dve.tensor_scalar(RA[k], RA[2 + k], turn * 2 * math.pi, 3.1415925, add,
                        mn).then_inc(own_dve, own.next())
                    dve.wait_ge(own_dve, own.n)
                    dve.tensor_scalar(RA[k], RA[k], -3.1415925, None, mx).then_inc(own_dve, own.next())
                    dve.wait_ge(own_dve, own.n)
                dve.tensor_scalar(RA[1], RA[1], con("sign"), None, mul).then_inc(rope_arg, 1)
                for k in range(2):
                    dve.wait_ge(own_dve, own.n)
                    dve.tensor_tensor(LAMV[:, 4, :], LAMV[:, 2 * k, :], LAMV[:, 2 * k + 1, :],
                        mul).then_inc(own_dve, own.next())
                    dve.wait_ge(own_dve, own.n)
                    ins = dve.tensor_reduce(LDOT[:, k:k + 1], LAMV[:, 4, :], AX_X, add)
                    if k:
                        ins.then_inc(lam_arg, 1)
                    else:
                        ins.then_inc(own_dve, own.next())
                dve.tensor_scalar(GD8, vec("g_diff_2"), 1.0 - LAM_INIT, None, mul).then_inc(own_dve, own.next())

            def attention():
                split_to(B_CKV + LEAD)
                norm_lo("mem", "g_mem_2")
                dve.wait_ge(gain_in, 16)
                norm(4, in_place=True)
                for i in range(N_CKV):
                    split_to(B_CKV + i + LEAD + 1)
                    dve.wait_ge(c_low, i + 1)
                    k = i - KC
                    if k >= 2:
                        dve.wait_ge(ct_mm, k - 1)
                    dve.tensor_tensor(CK[:, i, :] if k < 0 else CTM[:, i % 2, :], PS[Q_BANKS[i % 4]][:, 0:T],
                        CLOW[:, i % 2, :], add).then_inc(c_sum, 1)
                    if i == 2:
                        norm(5)
                    if i == 6:
                        rope_args()
                norm_lo("mix2", "g_mix_2")
                dve.wait_ge(lam_arg, 1)
                n_rope = 0
                for i in range(N_WIN2 + 1):
                    if i < N_WIN2:
                        split_to(B_WIN2 + i + LEAD + 1)
                        dve.wait_ge(q_low, i + 1)
                        dve.tensor_tensor(QKV[:, i, :], PS[Q_BANKS[i % 4]][:, 0:T], CLOW[:, i % 2, :],
                            add).then_inc(q_sum, 1)
                    k = i - 1
                    if k >= 0 and k != 5 and k < 14:
                        if n_rope == 0:
                            dve.wait_ge(rope_tab, 2)
                            dve.wait_ge(lam_exp, 1)
                            dve.tensor_tensor(NLAM, LEXP[:, 1:2], LEXP[:, 0:1], sub).then_inc(own_dve,
                                own.next())
                            dve.wait_ge(own_dve, own.n)
                            dve.tensor_scalar(NLAM, NLAM, -LAM_INIT, None, add).then_inc(own_dve, own.next())
                        dve.wait_ge(rope_mm, n_rope + 1)
                        dve.wait_ge(q_sum, k + 1)
                        if n_rope:
                            dve.wait_ge(rope_done, n_rope)
                        dve.tensor_tensor(RT[:, 0, :], QKV[:, k, :], RC, mul).then_inc(own_dve, own.next())
                        dve.tensor_tensor(RT[:, 1, :], PS[6 - 4 * (n_rope % 2)][:, 0:T], RSN,
                            mul).then_inc(own_dve, own.next())
                        dve.wait_ge(own_dve, own.n)
                        dve.tensor_tensor(QKV[:, k, :], RT[:, 0, :], RT[:, 1, :], add).then_inc(rope_done, 1)
                        n_rope += 1
                dve.wait_ge(rope_mm, n_rope + 1)
                dve.tensor_copy(KSW, PS[6][:, 0:T]).then_inc(rope_done, 1)
                split_to(B_WOUT2 + RING)

                dve.tensor_scalar(NSNK, SNK, -1.0, None, mul).then_inc(own_dve, own.next())

                def maxima(k):
                    j = ORDER[k]
                    kind, n, maps = JOBS[j]
                    nk, m = (n + 1) * P, len(maps)
                    q = slice(4 * j, 4 * j + m)
                    dve.wait_ge(sc_mm, k + 1)
                    s = SC[:, j, :].rearrange("p (m k) -> p m k", m=m)
                    ps = PS[k % 4][:, :].rearrange("p (m k) -> p m k", m=m)
                    if n and kind == "swa":
                        a = CONST_COLS["prev"][0]
                        dve.scalar_tensor_tensor(s, ps, 0.125, bc(CON[:, a:a + 2 * P], m), mul,
                            add).then_inc(sc_sum, 1)
                    elif n:
                        dve.tensor_scalar(s[:, :, 0:P], ps[:, :, 0:P], 0.125, None, mul).then_inc(own_dve,
                            own.next())
                        dve.scalar_tensor_tensor(s[:, :, P:], ps[:, :, P:], 0.125, bc(con("diag"), m), mul,
                            add).then_inc(sc_sum, 1)
                    else:
                        dve.scalar_tensor_tensor(s, ps, 0.125, bc(con("diag"), m), mul, add).then_inc(sc_sum, 1)
                    dve.wait_ge(sc_sum, k + 1)
                    dve.wait_ge(own_dve, own.n)
                    if kind == "swa":
                        dve.tensor_reduce(NMX[:, q], s, AX_X, mx, negate=True).then_inc(own_dve, own.next())
                        dve.wait_ge(own_dve, own.n)
                        h = slice(maps[0], maps[-1] + 1, 2)
                        dve.tensor_tensor(NMX[:, q], NMX[:, q], NSNK[:, h], mn).then_inc(own_dve, own.next())
                        dve.wait_ge(own_dve, own.n)
                        dve.tensor_tensor(ESK[:, q], SNK[:, h], NMX[:, q], add).then_inc(sc_max, 1)
                    else:
                        dve.tensor_reduce(NMX[:, q], s, AX_X, mx, negate=True).then_inc(sc_max, 1)

                def invert_sums(k):
                    j = ORDER[k]
                    kind, n, maps = JOBS[j]
                    m = len(maps)
                    q = slice(4 * j, 4 * j + m)
                    dve.wait_ge(sc_exp, k + 1)
                    if kind == "swa":
                        dve.tensor_tensor(SUM[:, q], SUM[:, q], ESK[:, q], add).then_inc(own_dve, own.next())
                        dve.wait_ge(own_dve, own.n)
                    if kind == "diff" and j % 2:
                        dve.reciprocal(REC[:, q], SUM[:, q]).then_inc(own_dve, own.next())
                        dve.wait_ge(own_dve, own.n)
                        dve.tensor_scalar(REC[:, q], REC[:, q], NLAM, None, mul).then_inc(rec_ready, 1)
                    else:
                        dve.reciprocal(REC[:, q], SUM[:, q]).then_inc(rec_ready, 1)

                for k in range(12):
                    maxima(k)
                    if k:
                        invert_sums(k - 1)
                invert_sums(11)
                dve.wait_ge(od_std, 1)
                dve.reciprocal(ODR, ODS).then_inc(own_dve, own.next())
                dve.wait_ge(own_dve, own.n)
                for n in range(NT):
                    dve.tensor_tensor(ODN[:, n, :].rearrange("p (a b) -> p a b", a=4),
                                      PS[2 + n][:, :].rearrange("p (a b) -> p a b", a=4),
                                      each(ODR[:, 4 * n:4 * n + 4]), mul).then_inc(od_norm, 1)
                for c in range(4):
                    dve.wait_ge(o_hi, c // 2 + 1)
                    rest(c, PS[c // 2][:, (c % 2) * T:(c % 2 + 1) * T]).then_inc(yt_ready, 1)
                for h in range(4):
                    dve.wait_ge(o_hi, 2 + h // 2 + 1)
                    rest(4 + h, PS[4 + h // 2][:, (h % 2) * T:(h % 2 + 1) * T], GD8).then_inc(yt_ready, 1)
                for c in range(KC - 1):
                    split_to(B_WOUT2 + c + LEAD + 1)
                update_x(4, B_WOUT2 + KC, 1.0)

            def cross():
                norm(6)
                split_to(B_CQ + LEAD)
                norm_lo("cross", "g_cross_2")
                for i in range(KC):
                    split_to(B_CQ + i + LEAD + 1)
                    dve.wait_ge(c_low, N_CKV + i + 1)
                    dve.tensor_tensor(CQ[:, i, :], PS[C_BANKS[i % 4]][:, 0:T], CLOW[:, i % 2, :],
                        add).then_inc(c_sum, 1)
                split_to(B_CO + RING)

                def maxima(j):
                    dve.wait_ge(sc_mm, 12 + j + 1)
                    q = slice(2 * j, 2 * j + 2)
                    dve.tensor_reduce(CNM[:, q], PS[j][:, :].rearrange("p (m k) -> p m k", m=2), AX_X,
                                      mx).then_inc(own_dve, own.next())
                    dve.wait_ge(own_dve, own.n)
                    dve.tensor_scalar(CNM[:, q], CNM[:, q], -1.0 / 16, None, mul).then_inc(sc_max, 1)

                def normalise(j):
                    q = slice(2 * j, 2 * j + 2)
                    dve.wait_ge(sc_exp, 12 + j + 1)
                    dve.reciprocal(CREC[:, q], CSUM[:, q]).then_inc(own_dve, own.next())
                    dve.wait_ge(own_dve, own.n)
                    dve.tensor_tensor(turner(6 + j, 0, 2).rearrange("p (a b) -> p a b", a=2), bc(ident, 2),
                                      each(CREC[:, q]), mul).then_inc(cp_ready, 1)

                for j in range(4):
                    maxima(j)
                    if j:
                        normalise(j - 1)
                normalise(3)
                for h in range(4):
                    dve.wait_ge(o_hi, 4 + h + 1)
                    for d in range(2):
                        rest(2 * h + d, PS[4 + h][:, d * T:(d + 1) * T]).then_inc(yt_ready, 1)
                for c in range(KC - 1):
                    split_to(B_CO + c + LEAD + 1)
                update_x(5, B_CO + KC, 1.0)

            def mlp():
                def chunk(j, i=None):
                    dj = 0 if i is None else i * 3
                    q = j % 3

                    def next_split(k):
                        n = B_MLP + 2 * j + LEAD + k
                        if n < N_UNITS:
                            split_lo(n, i)

                    next_split(0)
                    dve.wait_ge(r_low, j + 1 + dj)
                    dve.tensor_tensor(US[:, q, :], PS[4 + q][:, 0:T], UL[:, q, :], add).then_inc(r_sum, 1)
                    dve.wait_ge(r_sum, j + 1 + dj)
                    dve.scalar_tensor_tensor(HS[:, q, :], US[:, q, :], 0.0, US[:, q, :], mx, mul).then_inc(h_val, 1)
                    dve.wait_ge(h_val, 2 * FC + j + 1 + dj)
                    dve.wait_ge(r_hi, j + 1 + dj)
                    dve.tensor_tensor(H[:, q, T:2 * T], HS[:, q, :], H[:, q, 0:T].bitcast(F32),
                        sub).then_inc(r_ready, 1)
                    next_split(1)

                split_to(B_MLP + LEAD)
                for j in range(3):
                    chunk(j)
                with dve.Fori(0, 9) as i:
                    for k in range(3):
                        chunk(3 + k, i)
                for j in (30, 31):
                    chunk(j)
                update_x(6, N_UNITS, 1.0)

            dve.wait_ge(vec_tp, 1)
            dve.tensor_copy(VEC[:, 0:KC], PS[7][:, 0:KC]).then_inc(vec_ready, 1)
            norm(0)
            dve.wait_ge(vec_ready, 1)
            split_to(2)
            norm_lo("ffn1", "ffn1_norm")
            ffn(B_FFN1, 0)
            norm(1)
            dve.wait_ge(vec_ready, 2)
            split_to(B_WIN + LEAD)
            norm_lo("mix", "mix_norm")
            mix()
            norm(2)
            split_to(B_FFN2 + LEAD)
            norm_lo("ffn2", "ffn2_norm")
            ffn(B_FFN2, 1)
            attention()
            cross()
            norm(7)
            norm_lo("mlp", "g_mlp_2")
            mlp()
            dve.wait_ge(gain_in, 32)
            norm(8, in_place=True)

        @block.gpsimd
        def _(pool):
            pool.memset(WARM, 1.0).then_inc(warm_set, 1)
            pool.wait_ge(warm_set, 1)
            pool.memset(ROWS, 0.0).then_inc(rows_zero, 1)
            pool.wait_ge(rows_zero, 1)
            for name in ("mix_norm", "ffn2_norm", "g_mix_2", "g_cross_2", "g_mem_2", "g_mlp_2",
                         "w0", "a0", "k_k", "k_a", "ln_w", "ln_b", "pool_scale", "g_diff_2"):
                r = VEC_ROWS[name] - KC
                n = t[name].shape[1] // P
                pool.dma_start(ROWS[r:r + n, :], t[name][0].rearrange("(a b) -> a b", b=P)).then_inc(rows_in, 16)
            r = VEC_ROWS["r_k"] - KC
            pool.dma_start(ROWS[r:r + 4, :], t["r_k"][0].rearrange("(a h) d -> a (h d)", h=2)).then_inc(rows_in,
                16)
            r = VEC_ROWS["mu_shift"] - KC
            pool.dma_start(ROWS[r:r + 13, :], t["mu_shift"][0, 0:13 * P].rearrange("(a b) -> a b",
                b=P)).then_inc(rows_in, 16)
            pool.dma_start(ROWS[r + 13:r + 14, 0:32], t["mu_shift"][:, 13 * P:POOL]).then_inc(rows_in, 16)
            for k in range(4):
                a, e = N_FIRST + k * 680, min(N_CONST, N_FIRST + (k + 1) * 680)
                pool.wait_ge(unit_used, 8 + 6 * k)
                pool.dma_start(CON[:, a:e], t["consts"][:, a:e]).then_inc(table_in, 16)
            pool.dma_start(LWA[0:32, 0, :], t["w_lora_up"][0]).then_inc(small_in, 16)
            pool.dma_start(LWA[32:64, 1, :], t["a_lora_up"][0]).then_inc(small_in, 16)
            pool.dma_start(LWG[64:128, :], t["g_lora_up"][0, 0:64, :]).then_inc(small_in, 16)
            pool.dma_start(LWG[0:32, :], t["g_lora_up"][0, 64:96, :]).then_inc(small_in, 16)
            pool.dma_start(WPL[:, :, :], t["w_pool"][0].rearrange("g c d -> c g d")).then_inc(small_in, 16)
            for n, a in enumerate((LWA[32:64, 0, :], LWA[0:32, 1, :], LWG[32:64, :], LG[32:64, :],
                                   WRAW[:, :, 0:1], PP[:, :, 0:PAD])):
                pool.memset(a, 0.0).then_inc(w_zero, 1)
                pool.wait_ge(w_zero, n + 1)
            pool.wait_ge(k2_ready, 1)
            pool.tensor_tensor(EC, CC, SW, ALU.subtract).then_inc(ec_ready, 1)
            pool.wait_ge(ec_ready, 1)
            pool.tensor_tensor(FAC, CC[:, :, P - 1], CM.rearrange("p (f c) -> p f c", c=2)[:, :, 1],
                               ALU.add).then_inc(ec_ready, 1)
            pool.wait_ge(dec_done, 3)
            pool.wait_ge(bp_ready, NF)
            pool.wait_ge(ec_ready, 2)
            pool.tensor_tensor(K2, K2, IP, ALU.mult).then_inc(scaled, 1)
            pool.wait_ge(scaled, 1)
            pool.tensor_tensor(PR, PR, CC, ALU.mult).then_inc(scaled, 1)
            pool.wait_ge(scaled, 2)
            for wv in range(2):
                for k in range(1, 7):
                    for g in range(2):
                        n = wv * 12 + (k - 1) * 2 + g
                        M = mats[g]
                        if k == 1:
                            pool.wait_ge(m_ev, 8 * wv + 4 * g + 2)
                        if n >= 2:
                            pool.wait_ge(t_mm, n - 1)
                        mask = con(f"lev{k}t").rearrange("p (a b c) -> p a b c", a=1, b=1)
                        pool.tensor_tensor(M["LEV"].rearrange("p (h c) s -> p h c s", h=2), M["LT"][:, :, 0:2, :],
                                           mask.broadcast_to([P, 2, 2, P]), ALU.mult).then_inc(levmask, 1)
                        pool.wait_ge(levmask, n + 1)
            for k, j in enumerate(ORDER):
                m = len(JOBS[j][2])
                pool.wait_ge(rec_ready, k + 1)
                pool.tensor_tensor(turner(j, 0, m).rearrange("p (a b) -> p a b", a=m), bc(ident, m),
                                   each(REC[:, 4 * j:4 * j + m]), ALU.mult).then_inc(p_ready, 1)
                pool.wait_ge(p_ready, k + 1)


NAMES_IN = ("x ffn1_norm ffn1_w_gate ffn1_w_up ffn1_w_down mix_norm w_in mu_shift w0 w_lora_up a0 a_lora_up "
            "g_lora_up k_k k_a r_k ln_w ln_b w_pool pool_scale w_out ffn2_norm ffn2_w_gate ffn2_w_up ffn2_w_down "
            "final_norm mem_2 positions_2 g_mix_2 w_in_2 sinks_2 lambda_q1_2 lambda_k1_2 lambda_q2_2 lambda_k2_2 "
            "g_diff_2 w_out_2 g_cross_2 g_mem_2 w_cq_2 w_ckv_2 w_co_2 g_mlp_2 w_up_2 w_down_2 g_final_2").split()


def kernel(**inputs):
    import numpy as _np
    import concourse.bacc as _bacc
    from concourse import mybir as _mybir
    from concourse.bass_utils import run_bass_kernel_spmd as _run

    nc = _bacc.Bacc("TRN2", target_bir_lowering=False, num_devices=1)
    arrays, handles = {}, {}
    for name in NAMES_IN:
        a = _np.ascontiguousarray(inputs[name])
        arrays[f"in_{name}"] = a
        handles[name] = nc.dram_tensor(f"in_{name}", a.shape, _mybir.dt.from_np(a.dtype), kind="ExternalInput").ap()
    c = constants()
    arrays["in_consts"] = c
    handles["consts"] = nc.dram_tensor("in_consts", c.shape, _mybir.dt.float32, kind="ExternalInput").ap()
    out = nc.dram_tensor("out", (1, T, D), _mybir.dt.float32, kind="ExternalOutput").ap()
    build(nc, handles, out)
    r = _run(nc, [arrays], core_ids=[0])
    return r.results[0]["out"]
```
